# Optimizing a Trainium2 kernel written in Bass

```python
import math
import jax
import jax.numpy as jnp
from jax import lax
import numpy as np

D_MODEL = 1024
BATCH = 1
SEQ = 256
DEPTH = 2

HEAD_DIM = 64
RMS_EPS = 1e-6
ROPE_THETA = 10000.0
Q_BLOCK = 128
N_BRANCHES = 3
BRANCH_WIDTH = 512
SSM_WIDTH = BRANCH_WIDTH
SSM_GROUP = 16
SSM_GROUPS = SSM_WIDTH // SSM_GROUP
SSM_STATE = 64
DT_MIN = 0.001
DT_MAX = 0.1
NSA_HEADS = 8
NSA_KV_HEADS = 2
NSA_GROUP = NSA_HEADS // NSA_KV_HEADS
NSA_WIDTH = NSA_HEADS * HEAD_DIM
NSA_KV_COLS = 3 * 2 * NSA_KV_HEADS * HEAD_DIM
NSA_GATE_COLS = 3 * NSA_HEADS
CMP_LEN = 32
CMP_STRIDE = 16
CMP_HIDDEN = 128
SEL_LEN = 64
SEL_TOPK = 16
WINDOW = 512
FORCE_BONUS = 1e6
SB_HEADS = 8
SB_WIDTH = SB_HEADS * HEAD_DIM
D_FF = 2816
CONV_WIDTH = 3
IN_WIDTH = SSM_WIDTH + NSA_WIDTH + NSA_KV_COLS + NSA_GATE_COLS + 3 * SB_WIDTH + N_BRANCHES * D_MODEL

kernel_name = "hybrid_s5_nsa_stickbreak_gated_merge"

def rms_norm(x, g):
    xf = x.astype(jnp.float32)
    y = xf * lax.rsqrt(jnp.mean(xf * xf, axis=-1, keepdims=True) + RMS_EPS)
    return (y * g.astype(jnp.float32)).astype(x.dtype)

def rope_tables(seq_len):
    inv_freq = 1.0 / (ROPE_THETA ** (jnp.arange(0, HEAD_DIM, 2, dtype=jnp.float32) / HEAD_DIM))
    ang = jnp.arange(seq_len, dtype=jnp.float32)[:, None] * inv_freq[None, :]
    return jnp.cos(ang), jnp.sin(ang)

def apply_rope(t, cos, sin):
    t1, t2 = jnp.split(t.astype(jnp.float32), 2, axis=-1)
    c = cos[None, :, None, :]
    s = sin[None, :, None, :]
    return jnp.concatenate([t1 * c - t2 * s, t1 * s + t2 * c], axis=-1).astype(t.dtype)

def split_columns(proj):
    sizes = (SSM_WIDTH, NSA_WIDTH, NSA_KV_COLS, NSA_GATE_COLS, 3 * SB_WIDTH, N_BRANCHES * D_MODEL)
    points = [int(p) for p in np.cumsum(sizes)[:-1]]
    return jnp.split(proj, points, axis=-1)

def masked_softmax(s, mask):
    s = jnp.where(mask, s, -jnp.inf)
    m = jnp.max(s, axis=-1, keepdims=True)
    m = jnp.where(jnp.isfinite(m), m, 0.0)
    e = jnp.exp(s - m)
    return e / jnp.maximum(jnp.sum(e, axis=-1, keepdims=True), 1e-30)

def s5_mixer(u, lam_re, lam_im, log_step, b_re, b_im, c_re, c_im, d_skip, w_glu):
    bsz, seq, _ = u.shape
    f32 = jnp.float32
    ug = u.reshape(bsz, seq, SSM_GROUPS, SSM_GROUP).astype(f32)
    step = jnp.exp(log_step.astype(f32))[:, None]
    lr = lam_re.astype(f32)
    li = lam_im.astype(f32)
    mag = jnp.exp(lr * step)
    a_re = mag * jnp.cos(li * step)
    a_im = mag * jnp.sin(li * step)
    den = lr * lr + li * li
    nr = a_re - 1.0
    f_re = (nr * lr + a_im * li) / den
    f_im = (a_im * lr - nr * li) / den
    br = b_re.astype(f32)
    bi = b_im.astype(f32)
    bb_re = f_re[..., None] * br - f_im[..., None] * bi
    bb_im = f_re[..., None] * bi + f_im[..., None] * br
    x_re = jnp.einsum('bsgi,gpi->bsgp', ug, bb_re)
    x_im = jnp.einsum('bsgi,gpi->bsgp', ug, bb_im)
    a_re_b = jnp.broadcast_to(a_re, x_re.shape)
    a_im_b = jnp.broadcast_to(a_im, x_re.shape)

    def combine(e1, e2):
        a1r, a1i, b1r, b1i = e1
        a2r, a2i, b2r, b2i = e2
        return (a2r * a1r - a2i * a1i,
                a2r * a1i + a2i * a1r,
                a2r * b1r - a2i * b1i + b2r,
                a2r * b1i + a2i * b1r + b2i)

    _, _, h_re, h_im = lax.associative_scan(combine, (a_re_b, a_im_b, x_re, x_im), axis=1)
    y = (jnp.einsum('gip,bsgp->bsgi', c_re.astype(f32), h_re)
         - jnp.einsum('gip,bsgp->bsgi', c_im.astype(f32), h_im)
         + d_skip.astype(f32) * ug)
    y = jax.nn.gelu(y.reshape(bsz, seq, SSM_WIDTH))
    y = y * jax.nn.sigmoid(y @ w_glu.astype(f32))
    return y.astype(u.dtype)

def compress_blocks(t, w1, w2, pos):
    seq = t.shape[1]
    n_cmp = (seq - CMP_LEN) // CMP_STRIDE + 1
    idx = jnp.arange(n_cmp)[:, None] * CMP_STRIDE + jnp.arange(CMP_LEN)[None, :]
    blocks = t[:, idx] + pos[None, None, :, None, :]
    hid = jax.nn.gelu(jnp.einsum('bnlhd,lde->bnhe', blocks, w1))
    return jnp.einsum('bnhe,ed->bnhd', hid, w2)

def selected_attention(qg, k, v, sel_idx):
    bsz, seq, n_kv, n_grp, hd = qg.shape
    n_sel = seq // SEL_LEN
    n_top = sel_idx.shape[-1]
    scale = HEAD_DIM ** -0.5
    kb = k.reshape(bsz, n_sel, SEL_LEN, n_kv, hd).transpose(0, 3, 1, 2, 4)
    vb = v.reshape(bsz, n_sel, SEL_LEN, n_kv, hd).transpose(0, 3, 1, 2, 4)
    gather = jax.vmap(jax.vmap(lambda blocks, ix: blocks[ix]))
    offs = jnp.arange(SEL_LEN)
    n_keys = n_top * SEL_LEN

    def block(i):
        t0 = i * Q_BLOCK
        qi = lax.dynamic_slice_in_dim(qg, t0, Q_BLOCK, axis=1)
        ix = lax.dynamic_slice_in_dim(sel_idx, t0, Q_BLOCK, axis=2)
        kg = gather(kb, ix).reshape(bsz, n_kv, Q_BLOCK, n_keys, hd)
        vg = gather(vb, ix).reshape(bsz, n_kv, Q_BLOCK, n_keys, hd)
        kpos = (ix[..., None] * SEL_LEN + offs).reshape(bsz, n_kv, 1, Q_BLOCK, n_keys)
        tq = (t0 + jnp.arange(Q_BLOCK))[:, None]
        s = jnp.einsum('bqhgd,bhqmd->bhgqm', qi, kg).astype(jnp.float32) * scale
        p = masked_softmax(s, kpos <= tq)
        return jnp.einsum('bhgqm,bhqmd->bqhgd', p, vg.astype(jnp.float32))

    out = lax.map(block, jnp.arange(seq // Q_BLOCK))
    return jnp.moveaxis(out, 0, 1).reshape(bsz, seq, n_kv, n_grp, hd)

def window_attention(qg, k, v):
    bsz, seq, n_kv, n_grp, hd = qg.shape
    scale = HEAD_DIM ** -0.5
    span = WINDOW + Q_BLOCK
    kp = jnp.pad(k, ((0, 0), (WINDOW, 0), (0, 0), (0, 0)))
    vp = jnp.pad(v, ((0, 0), (WINDOW, 0), (0, 0), (0, 0)))

    def block(i):
        t0 = i * Q_BLOCK
        qi = lax.dynamic_slice_in_dim(qg, t0, Q_BLOCK, axis=1)
        ki = lax.dynamic_slice_in_dim(kp, t0, span, axis=1)
        vi = lax.dynamic_slice_in_dim(vp, t0, span, axis=1)
        kpos = t0 - WINDOW + jnp.arange(span)
        tq = t0 + jnp.arange(Q_BLOCK)
        diff = tq[:, None] - kpos[None, :]
        mask = (diff >= 0) & (diff < WINDOW) & (kpos[None, :] >= 0)
        s = jnp.einsum('bqhgd,bkhd->bhgqk', qi, ki).astype(jnp.float32) * scale
        p = masked_softmax(s, mask)
        return jnp.einsum('bhgqk,bkhd->bqhgd', p, vi.astype(jnp.float32))

    out = lax.map(block, jnp.arange(seq // Q_BLOCK))
    return jnp.moveaxis(out, 0, 1).reshape(bsz, seq, n_kv, n_grp, hd)

def nsa_mixer(q, k_all, v_all, gates, w1_k, w2_k, pos_k, w1_v, w2_v, pos_v):
    bsz, seq = q.shape[:2]
    f32 = jnp.float32
    scale = HEAD_DIM ** -0.5
    qg = q.reshape(bsz, seq, NSA_KV_HEADS, NSA_GROUP, HEAD_DIM)
    t_pos = jnp.arange(seq)
    kc = compress_blocks(k_all[:, :, 0], w1_k, w2_k, pos_k)
    vc = compress_blocks(v_all[:, :, 0], w1_v, w2_v, pos_v)
    n_cmp = kc.shape[1]
    cmp_start = jnp.arange(n_cmp) * CMP_STRIDE
    s_cmp = jnp.einsum('bthgd,bnhd->bhgtn', qg, kc).astype(f32) * scale
    p_cmp = masked_softmax(s_cmp, (cmp_start + CMP_LEN - 1)[None, :] <= t_pos[:, None])
    o_cmp = jnp.einsum('bhgtn,bnhd->bthgd', p_cmp, vc.astype(f32))
    n_sel = seq // SEL_LEN
    sel_start = jnp.arange(n_sel) * SEL_LEN
    overlap = ((cmp_start[:, None] < sel_start[None, :] + SEL_LEN)
               & (cmp_start[:, None] + CMP_LEN > sel_start[None, :])).astype(f32)
    p_sel = jnp.einsum('bhgtn,nj->bhtj', p_cmp, overlap)
    blk = jnp.arange(n_sel)[None, :]
    t_blk = (t_pos // SEL_LEN)[:, None]
    valid = blk <= t_blk
    forced = (blk == 0) | (blk == t_blk) | (blk == t_blk - 1)
    rank = jnp.where(valid, p_sel + FORCE_BONUS * forced.astype(f32), -FORCE_BONUS)
    _, sel_idx = lax.top_k(rank, min(SEL_TOPK, n_sel))
    o_slc = selected_attention(qg, k_all[:, :, 1], v_all[:, :, 1], sel_idx)
    o_win = window_attention(qg, k_all[:, :, 2], v_all[:, :, 2])
    g = gates.astype(f32)
    o = g[..., 0:1] * o_cmp + g[..., 1:2] * o_slc + g[..., 2:3] * o_win
    return o.reshape(bsz, seq, NSA_WIDTH).astype(q.dtype)

def stick_breaking_attention(q, k, v):
    bsz, seq, n_h, hd = q.shape
    scale = HEAD_DIM ** -0.5
    kpos = jnp.arange(seq)
    vf = v.astype(jnp.float32)

    def block(i):
        t0 = i * Q_BLOCK
        qi = lax.dynamic_slice_in_dim(q, t0, Q_BLOCK, axis=1)
        z = jnp.einsum('bqhd,bkhd->bhqk', qi, k).astype(jnp.float32) * scale
        tq = t0 + jnp.arange(Q_BLOCK)
        causal = kpos[None, :] < tq[:, None]
        log_rest = jnp.where(causal, jax.nn.log_sigmoid(-z), 0.0)
        after = lax.cumsum(log_rest, axis=3, reverse=True) - log_rest
        w = jnp.where(causal, jnp.exp(jax.nn.log_sigmoid(z) + after), 0.0)
        return jnp.einsum('bhqk,bkhd->bqhd', w, vf)

    out = lax.map(block, jnp.arange(seq // Q_BLOCK))
    return jnp.moveaxis(out, 0, 1).reshape(bsz, seq, n_h, hd).astype(q.dtype)

def conv_ffn(h, w_up, conv_w, conv_b, w_down):
    u = h @ w_up
    c = lax.conv_general_dilated(
        u, conv_w[:, None, :], window_strides=(1,), padding=((CONV_WIDTH - 1, 0),),
        dimension_numbers=('NWC', 'WIO', 'NWC'), feature_group_count=u.shape[-1]) + conv_b
    gate, val = jnp.split(c, 2, axis=-1)
    return (jax.nn.silu(gate) * val) @ w_down

def setup_inputs(seed: int = 0) -> dict:
    key = jax.random.key(seed)
    ks = iter(jax.random.split(key, 32))
    f32 = jnp.float32
    L = DEPTH
    G, P, I = SSM_GROUPS, SSM_STATE, SSM_GROUP

    def nrm(shape, scale):
        return jax.random.normal(next(ks), shape, f32) * scale

    return {
        'x': nrm((BATCH, SEQ, D_MODEL), 1.0),
        'norm_mix': 1.0 + nrm((L, D_MODEL), 0.02),
        'w_in': nrm((L, D_MODEL, IN_WIDTH), D_MODEL ** -0.5),
        'ssm_lam_re': -0.5 + nrm((L, G, P), 0.01),
        'ssm_lam_im': jnp.pi * jnp.arange(P, dtype=f32) + nrm((L, G, P), 0.01),
        'ssm_log_step': jax.random.uniform(next(ks), (L, G), f32, math.log(DT_MIN), math.log(DT_MAX)),
        'ssm_b_re': nrm((L, G, P, I), (2 * I) ** -0.5),
        'ssm_b_im': nrm((L, G, P, I), (2 * I) ** -0.5),
        'ssm_c_re': nrm((L, G, I, P), (2 * P) ** -0.5),
        'ssm_c_im': nrm((L, G, I, P), (2 * P) ** -0.5),
        'ssm_d': nrm((L, G, I), 1.0),
        'ssm_w_glu': nrm((L, SSM_WIDTH, SSM_WIDTH), SSM_WIDTH ** -0.5),
        'cmp_w1_k': nrm((L, CMP_LEN, HEAD_DIM, CMP_HIDDEN), (CMP_LEN * HEAD_DIM) ** -0.5),
        'cmp_w2_k': nrm((L, CMP_HIDDEN, HEAD_DIM), CMP_HIDDEN ** -0.5),
        'cmp_pos_k': nrm((L, CMP_LEN, HEAD_DIM), 0.1),
        'cmp_w1_v': nrm((L, CMP_LEN, HEAD_DIM, CMP_HIDDEN), (CMP_LEN * HEAD_DIM) ** -0.5),
        'cmp_w2_v': nrm((L, CMP_HIDDEN, HEAD_DIM), CMP_HIDDEN ** -0.5),
        'cmp_pos_v': nrm((L, CMP_LEN, HEAD_DIM), 0.1),
        'w_branch': nrm((L, N_BRANCHES, BRANCH_WIDTH, D_MODEL), BRANCH_WIDTH ** -0.5),
        'w_out': nrm((L, D_MODEL, D_MODEL), D_MODEL ** -0.5),
        'norm_ffn': 1.0 + nrm((L, D_MODEL), 0.02),
        'ffn_w_up': nrm((L, D_MODEL, 2 * D_FF), D_MODEL ** -0.5),
        'ffn_conv_w': nrm((L, CONV_WIDTH, 2 * D_FF), CONV_WIDTH ** -0.5),
        'ffn_conv_b': nrm((L, 2 * D_FF), 0.02),
        'ffn_w_down': nrm((L, D_FF, D_MODEL), D_FF ** -0.5),
        'norm_final': 1.0 + nrm((D_MODEL,), 0.02),
    }

def reference(x, norm_mix, w_in, ssm_lam_re, ssm_lam_im, ssm_log_step, ssm_b_re, ssm_b_im,
              ssm_c_re, ssm_c_im, ssm_d, ssm_w_glu, cmp_w1_k, cmp_w2_k, cmp_pos_k,
              cmp_w1_v, cmp_w2_v, cmp_pos_v, w_branch, w_out, norm_ffn, ffn_w_up,
              ffn_conv_w, ffn_conv_b, ffn_w_down, norm_final):
    bsz, seq, _ = x.shape
    cos, sin = rope_tables(seq)
    for l in range(DEPTH):
        h = rms_norm(x, norm_mix[l])
        proj = h @ w_in[l]
        u_ssm, q_nsa, kv_nsa, g_nsa, qkv_sb, g_merge = split_columns(proj)
        o_ssm = s5_mixer(u_ssm, ssm_lam_re[l], ssm_lam_im[l], ssm_log_step[l], ssm_b_re[l],
                         ssm_b_im[l], ssm_c_re[l], ssm_c_im[l], ssm_d[l], ssm_w_glu[l])
        q_b = apply_rope(q_nsa.reshape(bsz, seq, NSA_HEADS, HEAD_DIM), cos, sin)
        kv = kv_nsa.reshape(bsz, seq, 3, 2, NSA_KV_HEADS, HEAD_DIM)
        k_b = apply_rope(kv[:, :, :, 0].reshape(bsz, seq, 3 * NSA_KV_HEADS, HEAD_DIM), cos, sin)
        k_b = k_b.reshape(bsz, seq, 3, NSA_KV_HEADS, HEAD_DIM)
        v_b = kv[:, :, :, 1]
        gates_b = jax.nn.sigmoid(g_nsa).reshape(bsz, seq, NSA_KV_HEADS, NSA_GROUP, 3)
        o_nsa = nsa_mixer(q_b, k_b, v_b, gates_b, cmp_w1_k[l], cmp_w2_k[l], cmp_pos_k[l],
                          cmp_w1_v[l], cmp_w2_v[l], cmp_pos_v[l])
        qkv = qkv_sb.reshape(bsz, seq, 3, SB_HEADS, HEAD_DIM)
        o_sb = stick_breaking_attention(qkv[:, :, 0], qkv[:, :, 1], qkv[:, :, 2]).reshape(bsz, seq, SB_WIDTH)
        branches = jnp.stack([o_ssm, o_nsa, o_sb], axis=2).astype(x.dtype)
        y = jnp.einsum('bsnc,ncd->bsnd', branches, w_branch[l])
        gate = jax.nn.sigmoid(g_merge.reshape(bsz, seq, N_BRANCHES, D_MODEL))
        x = x + (jnp.sum(gate * y, axis=2) @ w_out[l]).astype(x.dtype)
        h = rms_norm(x, norm_ffn[l])
        x = x + conv_ffn(h, ffn_w_up[l], ffn_conv_w[l], ffn_conv_b[l], ffn_w_down[l]).astype(x.dtype)
    return rms_norm(x, norm_final)


_drawn_inputs = setup_inputs


def setup_inputs(seed=0):
    import zlib

    import numpy as np

    out = dict(_drawn_inputs(seed))
    spreads = {}
    factors = {'norm_mix': 3.654,
     'ssm_lam_re': 64.0,
     'ssm_lam_im': 21.269,
     'ssm_log_step': 134.728,
     'ssm_b_re': 37.744,
     'ssm_b_im': 38.024,
     'ssm_c_re': 200.0,
     'ssm_c_im': 200.0,
     'cmp_pos_k': 8.0,
     'cmp_pos_v': 2.757,
     'norm_ffn': 2.922,
     'ffn_conv_b': 2.879,
     'norm_final': 21.88}
    for name, (base, spread) in spreads.items():
        noise = np.random.default_rng([zlib.crc32(name.encode()), seed]).standard_normal(out[name].shape)
        drawn = base * np.exp(spread * noise) if base else spread * noise
        out[name] = jnp.asarray(drawn.astype(out[name].dtype))
    for name, factor in factors.items():
        out[name] = (out[name] * factor).astype(out[name].dtype)
    return out
```

```python
from contextlib import ExitStack

import concourse.bass as bass
from concourse import mybir

F32 = mybir.dt.float32
ALU = mybir.AluOpType
ACT = mybir.ActivationFunctionType
AX = mybir.AxisListType.X

P = 128
D = 1024
T = 256
DEPTH = 2
KD = D // P
NT = T // P
EPS = 1e-6
HD = 64
SCALE = HD ** -0.5
HEADS = 8
CH = 512
JC = CH // P
GROUPS, STATES, GCH = 32, 64, 16
ST = GROUPS * STATES // P
CMP, CSTR = 32, 16
NC = (T - CMP) // CSTR + 1
L2 = CMP // 2
F = 2816
FT = F // P
STEPS = F // (2 * P)
NEG = -1e30
TWO_PI = 6.283185307179586
PI_HIGH = 6.28125
PI_MID = int((TWO_PI - PI_HIGH) * 2 ** 21) / 2 ** 21
PI_PARTS = (PI_HIGH, PI_MID, TWO_PI - PI_HIGH - PI_MID)
MAGIC = 1.5 * 2 ** 23

C_U, C_Q, C_KV = 0, 512, 1024
C_G = 1792
C_SQ, C_SK, C_SV = 1816, 2328, 2840
C_M = 3352

RING = 6
SLOT = 2048
PLAN = ([("q", 0), ("q", 1), ("in", C_KV), ("in", C_KV + 256), ("in", C_KV + 512), ("ngate", C_G),
         ("cmp", 0), ("cmp", 1), ("in", C_U), ("in", C_U + 256)]
        + [("in", c + 256 * i) for c in (C_SQ, C_SK, C_SV) for i in range(2)]
        + [("in", C_M + D * b + 256 * i) for b in (1, 2, 0) for i in range(4)]
        + [("branch", 1, 0), ("branch", 1, 1), ("branch", 2, 0), ("branch", 2, 1), ("glu",),
           ("branch", 0, 0), ("branch", 0, 1)]
        + [("out", 256 * i) for i in range(4)])
C_FFN = len(PLAN)
CHUNKS = C_FFN + 3 * STEPS
assert CHUNKS % RING == 0
I_Q, I_KV, I_CMP, I_U, I_FILL = 0, 2, 6, 8, 10
I_GLU = 32
I_OUT = 35
LOOP = 4
assert 3 + 2 * LOOP == STEPS

FILL = ([("sbq", 0), ("sbq", 1), ("sbk", 0), ("sbk", 1), ("sbv", 0), ("sbv", 1)]
        + [("gate", b, i) for b in (1, 2, 0) for i in range(4)]
        + [("y", b, i) for b in (1, 2) for i in range(4)])
U_FILL = 8
U_GLU = U_FILL + len(FILL)
U_Y = U_GLU + 2
U_OUT = U_Y + 4
U_FFN = U_OUT + 4
UNITS = U_FFN + 2 * STEPS
assert UNITS % 2 == 0

SLOTS = 2 * len(FILL)
NSA = 16
SB_Z = {18 + 2 * h: h for h in range(HEADS)}
SB_R = {s + 2: h for s, h in SB_Z.items()}
SB_O = {s + 4: h for s, h in SB_Z.items()}
S5_X = {2 * s: s for s in range(ST)}
S5_Y = {2 * s + 3: s for s in range(ST)}

K_ID, K_ROT, K_TRI, K_NEG1, K_ONE = 0, 128, 256, 384, 512
K_COS, K_SIN = 640, 896
K_MASK = 1152
K_CMASK = 1408
K_PAR = 1440
K_NPAR = 1442
K_ALL = 1444

A_MIX, A_FFN, A_D, A_FIN, A_LR, A_LI, A_PK, A_PV, A_ST, A_PKS = 0, 8, 16, 20, 32, 48, 64, 80, 96, 112
B_W0, B_W1, B_PVS = 0, 22 * 2, 96
C_W2, C_B = 0, 44


def constants():
    import numpy as np

    k = np.zeros((P, K_ALL), np.float32)
    i = np.arange(P)
    k[:, K_ID:K_ID + P] = np.eye(P)
    for m in range(P):
        d = m % HD
        if d < HD // 2:
            k[m + HD // 2, K_ROT + m] = -1.0
        else:
            k[m - HD // 2, K_ROT + m] = 1.0
    k[:, K_TRI:K_TRI + P] = -(i[:, None] >= i[None, :]).astype(np.float32)
    k[:, K_NEG1:K_NEG1 + P] = -1.0
    k[:, K_ONE:K_ONE + P] = 1.0
    freq = (np.float32(1.0) / (np.float32(10000.0) ** (np.arange(0, HD, 2, dtype=np.float32) / np.float32(HD))))
    ang = np.arange(T, dtype=np.float32)[:, None] * freq[None, :].astype(np.float32)
    cs, sn = np.cos(ang).T, np.sin(ang).T
    k[:, K_COS:K_COS + T] = np.tile(cs, (4, 1))
    k[:, K_SIN:K_SIN + T] = np.tile(sn, (4, 1))
    k[:, K_MASK + P:K_MASK + 2 * P] = np.where(i[None, :] <= i[:, None], 0.0, NEG)
    for t in range(NT):
        ends = np.arange(NC) * CSTR + CMP - 1
        k[:, K_CMASK + 16 * t:K_CMASK + 16 * t + NC] = np.where(ends[None, :] <= i[:, None] + P * t, 0.0, NEG)
    for w in range(2):
        k[:, K_PAR + w] = ((i // GCH) % 2 == w)
        k[:, K_NPAR + w] = -k[:, K_PAR + w]
    return k


class Tally:

    def __init__(self, sem, name, per_layer, start=0):
        self.sem, self.name, self.per_layer, self.start, self.made = sem, name, per_layer, start, 0

    def up(self, n=1):
        self.made += n
        return n

    def last(self, l):
        return self.at(l, self.made)

    def at(self, l, k):
        return l * self.per_layer + (self.start + k)


def build(nc, x, norm_mix, w_in, ssm_lam_re, ssm_lam_im, ssm_log_step, ssm_b_re, ssm_b_im,
          ssm_c_re, ssm_c_im, ssm_d, ssm_w_glu, cmp_w1_k, cmp_w2_k, cmp_pos_k,
          cmp_w1_v, cmp_w2_v, cmp_pos_v, w_branch, w_out, norm_ffn, ffn_w_up,
          ffn_conv_w, ffn_conv_b, ffn_w_down, norm_final, consts, out):
    with ExitStack() as ctx:
        def sb(name, shape):
            return ctx.enter_context(nc.sbuf_tensor(name, shape, F32))

        def bank(name):
            return ctx.enter_context(nc.psum_tensor(name, [P, 512], F32))

        tallies = []

        def sem(name, per_layer=0, start=0):
            t = Tally(ctx.enter_context(nc.semaphore(name)), name, per_layer, start)
            tallies.append(t)
            return t

        ring = sb("ring", [P, RING, SLOT])
        kon = sb("kon", [P, K_ALL])
        xT = sb("xT", [P, KD, T])
        hT = sb("hT", [P, KD, T])
        mT = sb("mT", [P, KD, T])
        ms = sb("ms", [P, T])
        rstd = sb("rstd", [P, T])
        stA = sb("stA", [P, P])
        stB = sb("stB", [P, P])
        stC = sb("stC", [P, P])
        par = sb("par", [P, 3, P])
        lstep = sb("lstep", [P, 2])
        bnat = sb("bnat", [P, 2, ST, GCH])
        cnat = sb("cnat", [P, 2, JC, STATES])
        w2 = sb("w2", [P, 2, HD])
        uT = sb("uT", [P, JC, T])
        qr = sb("qr", [P, 4, T])
        kr = sb("kr", [P, 4, T])
        vn = sb("vn", [P, NT, 2, P])
        ng = sb("ng", [P, NT, 3 * HEADS])
        hid = sb("hid", [P, 2, 32])
        kc = sb("kc", [P, 16])
        vc = sb("vc", [P, HD])
        cE = sb("cE", [P, NSA, 32])
        cm = sb("cm", [P, 3, NSA])
        pcT = sb("pcT", [P, 4, P])
        mx = sb("mx", [P, 2, 2])
        nm = sb("nm", [P, 2, 2])
        sm = sb("sm", [P, 2, 2])
        rc = sb("rc", [P, 2, 2])
        rg = sb("rg", [P, 2, 2])
        sbq = sb("sbq", [P, JC, T])
        sbk = sb("sbk", [P, 4, T])
        sbv = sb("sbv", [P, NT, CH])
        sbw = sb("sbw", [P, 2, 384])
        sbp = sb("sbp", [P, 2, 384])
        gate = sb("gate", [P, 3 * KD, T])
        oN = sb("oN", [P, JC, T])
        oB = sb("oB", [P, JC, T])
        oS = sbq
        tab = sb("tab", [P, 2, ST, P])
        s5p = sb("s5p", [P, 20, ST])
        BL = sb("BL", [P, 2, JC, P])
        CL = sb("CL", [P, 2, JC, P])
        s5a = sb("s5a", [P, 2, 2 * T])
        s5x = sb("s5x", [P, 2, T])
        s5i = sb("s5i", [P, 4])
        s5h = sb("s5h", [P, 2, 2, T])
        yT = sb("yT", [P, JC, T])
        work = sb("work", [P, 3, 2, 2 * T])
        sc = work[:, 0]
        pr = work[:, 1]
        pT = work[:, 2]
        cv = work[:, 0]
        aT = work[:, 1]
        yt = work[:, 2]
        cS = work[:, 2, 0, 0:NSA * NC].rearrange("p (n c) -> p n c", c=NC)
        cP = cE[:, :, 0:NC]
        rt = work[:, 0, 0, :]
        blk = s5a[:, :, :].rearrange("p a b -> p (a b)")[:, 0:4 * NC * L2].rearrange(
            "p (r g n a) -> p r g n a", r=2, g=2, n=NC)
        bb = s5h[:, 0, :, :].rearrange("p c (t i) -> p c t i", i=GCH)
        bbt = s5h[:, 1, :, :].rearrange("p c (t i) -> p c t i", i=GCH)
        bx = gate[:, 0:4, :].rearrange("p a b -> p (a b)").rearrange("p (c t i) -> p c t i", c=2, t=ST)
        cx = gate[:, 4:8, :].rearrange("p a b -> p (a b)").rearrange("p (c j q) -> p c j q", c=2, j=JC)
        tmp_d = gate[:, 8:12, :].rearrange("p a b -> p (a b)").rearrange("p (t n) -> p t n", t=ST)
        tmp_p = gate[:, 12:16, :].rearrange("p a b -> p (a b)").rearrange("p (t n) -> p t n", t=ST)

        sq = gate[:, 2 * KD:3 * KD, :]

        pj = [bank(f"pj{i}") for i in range(2)]
        bX = [bank(f"bX{i}") for i in range(2)]
        bY = bank("bY")
        bA = bank("bA")
        bB = bank("bB")
        bO = bank("bO")
        down = [bX[0], bX[1], bA, bB]

        consts_in = sem("consts_in")
        x_in = sem("x_in")
        setup = sem("setup")
        passed = sem("passed")
        out_sent = sem("out_sent")
        landed = [sem(f"landed{i}", 16 * CHUNKS // RING) for i in range(RING)]
        q_in = sem("q_in", 16 * 6)
        cmp_in = sem("cmp_in", 32)
        upper_in = sem("upper_in", 32)
        rows_in = sem("rows_in", 16 * 17)
        mats_in = sem("mats_in", 16 * 6)
        params_free = sem("params_free", 1, 1)
        unit_done = sem("unit_done", UNITS, 3)
        unit_out = [sem(f"unit_out{i}", UNITS // 2, 1) for i in range(2)]
        x_turned = sem("x_turned")
        x_ready = sem("x_ready", 8, 4)
        sq_ready = sem("sq_ready", 8)
        ss_done = sem("ss_done", 2)
        ms_ready = sem("ms_ready", 2)
        rstd_ready = sem("rstd_ready", 2)
        h_ready = sem("h_ready", 2 * KD)
        step_row = sem("step_row", 1)
        par_turned = sem("par_turned", 3)
        par_ready = sem("par_ready", 3)
        step_exp = sem("step_exp", 1)
        ang_ready = sem("ang_ready", 2)
        mag_ready = sem("mag_ready", 1)
        sin_ready = sem("sin_ready", 1)
        tab_d = sem("tab_d", 8)
        tab_p = sem("tab_p", 7)
        bx_ready = sem("bx_ready", 2)
        cx_ready = sem("cx_ready", 2)
        bc_turned = sem("bc_turned", 4)
        bc_ready = sem("bc_ready", 4)
        dve_step = sem("dve_step", 136)
        rot_done = sem("rot_done", 4)
        rot_cos = sem("rot_cos", 4)
        rot_ready = sem("rot_ready", 4)
        blk_ready = sem("blk_ready", 2)
        hid_done = sem("hid_done", 2)
        hid_ready = sem("hid_ready", 2)
        kc_done = sem("kc_done", 2)
        kc_ready = sem("kc_ready", 2)
        cs_done = sem("cs_done", 1)
        cs_ready = sem("cs_ready", 1)
        ce_ready = sem("ce_ready", 1)
        cp_ready = sem("cp_ready", 1)
        pc_done = sem("pc_done", 1)
        pc_ready = sem("pc_ready", 1)
        s_done = sem("s_done", NSA)
        s_max = sem("s_max", NSA)
        s_exp = sem("s_exp", NSA)
        s_rec = sem("s_rec", NSA)
        s_prob = sem("s_prob", NSA)
        t_done = sem("t_done", NSA)
        t_ready = sem("t_ready", NSA)
        v_done = sem("v_done", NSA)
        on_ready = sem("on_ready", 4)
        z_done = sem("z_done", HEADS)
        z_abs = sem("z_abs", HEADS)
        z_exp = sem("z_exp", HEADS)
        z_ln = sem("z_ln", HEADS)
        z_sp = sem("z_sp", HEADS)
        z_spm = sem("z_spm", HEADS)
        r_done = sem("r_done", HEADS)
        w_exp = sem("w_exp", HEADS)
        w_ready = sem("w_ready", HEADS)
        o_done = sem("o_done", HEADS)
        ob_ready = sem("ob_ready", 4)
        x5_done = sem("x5_done", ST)
        x5_used = sem("x5_used", ST)
        x5_turned = sem("x5_turned", ST)
        g5_ready = sem("g5_ready", ST)
        pool_step = sem("pool_step", 7 + ST)
        h5_ready = sem("h5_ready", ST)
        y_done = sem("y_done", ST)
        y_used = sem("y_used", JC)
        y_ready = sem("y_ready", 1)
        os_ready = sem("os_ready", 2)
        m_ready = sem("m_ready", 8)
        cv_last = sem("cv_last", 2 * STEPS)
        cv_mid = sem("cv_mid", 2 * STEPS)
        sg_ready = sem("sg_ready", STEPS)
        a_ready = sem("a_ready", STEPS)
        a_used = sem("a_used", STEPS, 3)
        down_done = sem("down_done", 1)
        fin_turned = sem("fin_turned")
        fin_ready = sem("fin_ready")

        ident = kon[:, K_ID:K_ID + P]
        ones = kon[:, K_ONE:K_ONE + P]

        def chunk_at(l, i):
            return landed[i % RING].at(l, 16 * (i // RING + 1))

        def unit(n):
            return pj[n % 2][:, :].rearrange("p (m t) -> p m t", m=2)

        def slot_of(i):
            return ring[:, i % RING, :]

        def nsa_unit(n):
            i, s, t = n // 4, n // 2 % 2, n % 2
            return i, s, t, P * (t + 1)

        def cols(ap, w):
            return ap[:, 0:2 * w].rearrange("p (b w) -> p b w", b=2)

        xd = x.rearrange("b (t p) d -> p (b t) d", p=P)
        od = out.rearrange("b (t p) d -> p (b t) d", p=P)

        block = ctx.enter_context(nc.Block())

        @block.sync
        def _(sp):
            sp.dma_start(kon[:, :], consts).then_inc(consts_in.sem, 16)
            sp.dma_start(hT[:, :, :].rearrange("p (t a) b -> p t (a b)", t=NT), xd).then_inc(x_in.sem, 16)
            sp.wait_ge(setup.sem, 3)

            def row(w, l):
                return w[bass.ds(l, 1)]

            def par_in(dst, src):
                sp.dma_start(dst, src).then_inc(rows_in.sem, rows_in.up(16))

            def mat_in(dst, src):
                sp.dma_start(dst, src).then_inc(mats_in.sem, mats_in.up(16))

            def last_reader(i):
                if i < I_KV:
                    return unit_done, i + 1
                if i < I_CMP:
                    return unit_done, 6
                if i < I_U:
                    return hid_done, i - I_CMP + 1
                if i < I_FILL:
                    return unit_done, i - I_U + 7
                if i < I_GLU:
                    kind = PLAN[i]
                    last = {14: 5, 15: 5, 28: 19, 29: 21, 30: 23, 31: 25}.get(i, i - I_FILL)
                    return unit_done, U_FILL + last + 1
                if i < I_OUT:
                    return unit_done, U_GLU + 2 * (i - I_GLU + 1)
                if i < C_FFN:
                    return unit_done, U_OUT + i - I_OUT + 1
                i -= C_FFN
                if i < 4:
                    return unit_done, U_FFN + i + 1
                step, part = (i - 5) // 3 + 2, (i - 5) % 3
                if i == 4 or part == 2:
                    return a_used, 1 if i == 4 else step
                if i == CHUNKS - C_FFN - 1:
                    return a_used, STEPS
                return unit_done, U_FFN + 2 * step + part + 1

            def load(l, i):
                kind, *at = PLAN[i]
                dst = slot_of(i)
                t, k = last_reader((i - RING) % CHUNKS)
                sp.wait_ge(t.sem, t.at(l, k if i >= RING else k - t.per_layer))
                sp.sem_inc(passed.sem, 1)
                if kind in ("in", "ngate", "out"):
                    n = 3 * HEADS if kind == "ngate" else 256
                    w = w_out if kind == "out" else w_in
                    src = row(w, l)[:, :, at[0]:at[0] + n].rearrange("l (k p) n -> p (l k) n", p=P)
                    dst = dst[:, 0:KD * n].rearrange("p (k n) -> p k n", k=KD)
                elif kind == "q":
                    for s in range(2):
                        c = C_Q + CH // 2 * s + P * at[0]
                        src = row(w_in, l)[:, :, c:c + P].rearrange("l (k p) (i d) -> p (l k) i d", p=P, i=2)
                        to = dst.rearrange("p (k i s d) -> p k i s d", k=KD, i=2, s=2)[:, :, :, s, :]
                        for i in range(2):
                            ins = sp.dma_start(to[:, :, i, :], src[:, :, i, :])
                            if s and i:
                                ins.then_inc(landed[at[0]].sem, landed[at[0]].up(16))
                            else:
                                ins.then_inc(q_in.sem, q_in.up(16))
                    return
                elif kind == "cmp":
                    src = row((cmp_w1_k, cmp_w1_v)[at[0]], l).rearrange("l (a b) d e -> (b d) (l a) e", b=2)
                    dst = dst.rearrange("p (a e) -> p a e", e=P)
                    sp.dma_start(dst[:, 0:L2 // 2], src[:, 0:L2 // 2]).then_inc(cmp_in.sem, cmp_in.up(16))
                    dst, src = dst[:, L2 // 2:L2], src[:, L2 // 2:L2]
                elif kind == "glu":
                    src = row(ssm_w_glu, l).rearrange("l (k p) n -> p (l k) n", p=P)
                    dst = dst.rearrange("p (k n) -> p k n", k=JC)
                else:
                    b, half = at
                    dst = dst.rearrange("p (k n) -> p k n", k=JC)
                    w = row(w_branch, l)[:, b, :, CH * half:CH * half + CH]
                    if b == 1:
                        src = w.rearrange("l (s k p) n -> s p (l k) n", p=HD, s=2)
                        sp.dma_start(dst[0:HD], src[0]).then_inc(upper_in.sem, upper_in.up(16))
                        dst, src = dst[HD:P], src[1]
                    else:
                        src = w.rearrange("l (k p) n -> p (l k) n", p=P)
                sp.dma_start(dst, src).then_inc(landed[i % RING].sem, landed[i % RING].up(16))

            def load_ffn(l, i, part, c, turn=0, times=1, turn_step=0):
                if times == 1:
                    t, k = last_reader((i - RING) % CHUNKS)
                    sp.wait_ge(t.sem, t.at(l, k))
                elif part == "down":
                    sp.wait_ge(a_used.sem, a_used.at(l, turn_step - 2 + turn * 2))
                else:
                    sp.wait_ge(unit_done.sem, unit_done.at(l, U_FFN + 2 * (turn_step - 2) + (part == "value") + 1 + turn * 4))
                sp.sem_inc(passed.sem, 1)
                if part == "down":
                    src = row(ffn_w_down, l)[:, bass.ds(c * 256, 256), :].rearrange("l (k p) n -> p (l k) n", p=P)
                    dst = slot_of(i).rearrange("p (k n) -> p k n", k=2)
                else:
                    first = F if part == "value" else 0
                    src = row(ffn_w_up, l)[:, :, bass.ds(c * 256 + first, 256)].rearrange(
                        "l (k p) n -> p (l k) n", p=P)
                    dst = slot_of(i).rearrange("p (k n) -> p k n", k=KD)
                sp.dma_start(dst, src).then_inc(landed[i % RING].sem, 16)
                landed[i % RING].made += 16 * times

            with sp.Fori(0, DEPTH) as l:
                sp.wait_ge(params_free.sem, params_free.at(l, 0))
                sp.sem_inc(passed.sem, 1)
                par_in(stA[A_MIX:A_MIX + 8, :], row(norm_mix, l).rearrange("l (k p) -> (l k) p", p=P))
                par_in(stA[A_FFN:A_FFN + 8, :], row(norm_ffn, l).rearrange("l (k p) -> (l k) p", p=P))
                par_in(stA[A_D:A_D + 4, :], row(ssm_d, l).rearrange("l (k g) i -> (l k) (g i)", k=4))
                par_in(stA[A_FIN:A_FIN + 8, :], norm_final.rearrange("(k p) -> k p", p=P))
                par_in(stA[A_LR:A_LR + ST, :], row(ssm_lam_re, l).rearrange("l (t w) p -> (l t) (w p)", w=2))
                par_in(stA[A_LI:A_LI + ST, :], row(ssm_lam_im, l).rearrange("l (t w) p -> (l t) (w p)", w=2))
                par_in(lstep[A_ST:A_ST + ST, :], row(ssm_log_step, l).rearrange("l (t w) -> (l t) w", w=2))
                for pos, own, st, swap in ((cmp_pos_k, A_PK, stA, A_PKS), (cmp_pos_v, A_PV, stB, B_PVS)):
                    src = row(pos, l).rearrange("l (a b) d -> (l a) b d", b=2)
                    par_in(stA[own:own + L2, :].rearrange("a (b d) -> a b d", b=2), src)
                    dst = st[swap:swap + L2, :].rearrange("a (b d) -> a b d", b=2)
                    for b in range(2):
                        par_in(dst[:, b:b + 1, :], src[:, 1 - b:2 - b, :])
                cw = row(ffn_conv_w, l)
                par_in(stB[B_W0:B_W0 + 2 * FT, :], cw[:, 0, :].rearrange("l (k p) -> (l k) p", p=P))
                par_in(stB[B_W1:B_W1 + 2 * FT, :], cw[:, 1, :].rearrange("l (k p) -> (l k) p", p=P))
                par_in(stC[C_W2:C_W2 + 2 * FT, :], cw[:, 2, :].rearrange("l (k p) -> (l k) p", p=P))
                par_in(stC[C_B:C_B + 2 * FT, :], row(ffn_conv_b, l).rearrange("l (k p) -> (l k) p", p=P))
                load(l, 0)
                load(l, 1)
                for r, w in enumerate((ssm_b_re, ssm_b_im)):
                    mat_in(bnat[:, r], row(w, l).rearrange("l (t w) p i -> (w p) (l t) i", w=2))
                for r, w in enumerate((ssm_c_re, ssm_c_im)):
                    mat_in(cnat[:, r], row(w, l).rearrange("l (j q) i p -> (q i) (l j) p", j=JC))
                for r, w in enumerate((cmp_w2_k, cmp_w2_v)):
                    mat_in(w2[:, r], row(w, l).rearrange("l e d -> (l e) d"))
                for i in range(2, C_FFN):
                    load(l, i)
                i = C_FFN
                load_ffn(l, i, "gate", 0)
                load_ffn(l, i + 1, "value", 0)
                load_ffn(l, i + 2, "gate", 1)
                load_ffn(l, i + 3, "value", 1)
                load_ffn(l, i + 4, "down", 0)
                i += 5
                with sp.Fori(0, LOOP) as j:
                    for e in range(2):
                        for n, part in enumerate(("gate", "value", "down")):
                            c = j * 2 + (1 + e if part == "down" else 2 + e)
                            load_ffn(l, i + 3 * e + n, part, c, j, LOOP, 2 + e)
                i += RING * LOOP
                load_ffn(l, i, "gate", STEPS - 1)
                load_ffn(l, i + 1, "value", STEPS - 1)
                load_ffn(l, i + 2, "down", STEPS - 2)
                load_ffn(l, i + 3, "down", STEPS - 1)
            sp.wait_ge(fin_ready.sem, 4)
            sp.dma_start(od, mT[:, :, :].rearrange("p (t a) b -> p t (a b)", t=NT)).then_inc(out_sent.sem, 16)
            sp.wait_ge(out_sent.sem, 16)

        @block.tensor
        def _(pe):
            def mm(o, a, b, start, stop):
                return nc.tensor.matmul(o, a, b, start=start, stop=stop, skip_group_check=True)

            def tiles(n, lhs, rhs, kt, halves=(0, 1)):
                for m in halves:
                    for k in range(kt):
                        ins = mm(pj[n % 2][:, T * m:T * m + T], lhs(m, k), rhs(k), k == 0, k == kt - 1)
                if 1 in halves:
                    ins.then_inc(unit_done.sem, unit_done.up())

            def h_k(k):
                return hT[:, k, :]

            def sum_squares(l, first):
                for k in range(KD):
                    if k % 2 == 0:
                        pe.wait_ge(sq_ready.sem, sq_ready.at(l, first + k // 2 + 1))
                    ins = mm(bO[:, 0:T], ones, sq[:, k, :], k == 0, k == KD - 1)
                return ins

            pe.wait_ge(consts_in.sem, 16)
            pe.wait_ge(x_in.sem, 16)
            xs = hT[:, :, :].rearrange("p (t a) b -> p t (a b)", t=NT)
            for b, o in enumerate(down):
                for k in range(2):
                    for t in range(NT):
                        kk = 2 * b + k
                        ins = nc.tensor.transpose(o[:, T * k + P * t:T * k + P * t + P],
                                                  xs[:, t, P * kk:P * kk + P], ident)
                ins.then_inc(x_turned.sem, 1)

            with pe.Fori(0, DEPTH) as l:
                sum_squares(l, 0).then_inc(ss_done.sem, ss_done.up())
                pe.wait_ge(step_row.sem, step_row.at(l, 1))
                for n, st in enumerate((stA, stB, stC)):
                    nc.tensor.transpose(bX[0][:, P * n:P * n + P], st[:, :], ident)\
                        .then_inc(par_turned.sem, par_turned.up())

                for n in range(2):
                    pe.wait_ge(landed[(I_Q + n) % RING].sem, chunk_at(l, I_Q + n))
                    pe.wait_ge(q_in.sem, q_in.at(l, 96))
                    pe.wait_ge(unit_out[n % 2].sem, unit_out[n % 2].at(l, n // 2))
                    if n == 0:
                        pe.wait_ge(h_ready.sem, h_ready.at(l, KD))
                    qw = slot_of(I_Q + n).rearrange("p (k n) -> p k n", k=KD)
                    tiles(n, lambda m, k: qw[:, k, P * m:P * m + P], h_k, KD)
                kvw = [slot_of(I_KV + b).rearrange("p (k n) -> p k n", k=KD) for b in range(3)]
                for b in range(3):
                    pe.wait_ge(landed[(I_KV + b) % RING].sem, chunk_at(l, I_KV + b))
                pe.wait_ge(unit_out[0].sem, unit_out[0].at(l, 1))
                tiles(2, lambda m, k: kvw[m][:, k, 0:P], h_k, KD)
                pe.wait_ge(unit_out[1].sem, unit_out[1].at(l, 1))
                tiles(3, lambda m, k: kvw[2][:, k, 0:P] if m == 0 else kvw[0][:, k, P:2 * P], h_k, KD)
                pe.wait_ge(landed[(I_KV + 3) % RING].sem, chunk_at(l, I_KV + 3))
                gw = slot_of(I_KV + 3)[:, 0:KD * 3 * HEADS].rearrange("p (k n) -> p k n", k=KD)
                for t in range(NT):
                    n = 4 + t
                    pe.wait_ge(unit_out[n % 2].sem, unit_out[n % 2].at(l, n // 2))
                    for w, at, width in ((kvw[1][:, :, P:2 * P], 0, P), (kvw[2][:, :, P:2 * P], P, P),
                                         (gw, 2 * P, 3 * HEADS)):
                        for k in range(KD):
                            ins = mm(pj[n % 2][:, at:at + width], hT[:, k, P * t:P * t + P], w[:, k, :],
                                     k == 0, k == KD - 1)
                    ins.then_inc(unit_done.sem, unit_done.up())
                for n, (o, src, u) in enumerate(((bO, kr[:, 0:2, :], 2), (bX[1], kr[:, 2:3, :], 3),
                                                 (bA, qr[:, 0:2, :], 0), (bB, qr[:, 2:4, :], 1))):
                    pe.wait_ge(unit_out[u % 2].sem, unit_out[u % 2].at(l, u // 2 + 1))
                    src = src.rearrange("p a b -> p (a b)")
                    mm(o[:, 0:src.shape[1]], kon[:, K_ROT:K_ROT + P], src, True, True)\
                        .then_inc(rot_done.sem, rot_done.up())
                uw = [slot_of(I_U + n).rearrange("p (k n) -> p k n", k=KD) for n in range(2)]
                pe.wait_ge(landed[I_U % RING].sem, chunk_at(l, I_U))
                pe.wait_ge(unit_out[0].sem, unit_out[0].at(l, 3))
                tiles(6, lambda m, k: uw[0][:, k, P * m:P * m + P], h_k, KD)
                pe.wait_ge(landed[(I_U + 1) % RING].sem, chunk_at(l, I_U + 1))
                pe.wait_ge(unit_out[1].sem, unit_out[1].at(l, 3))
                tiles(7, lambda m, k: uw[1][:, k, P * m:P * m + P], h_k, KD)
                pe.wait_ge(rot_ready.sem, rot_ready.at(l, 4))
                for r in range(2):
                    pe.wait_ge(landed[(I_CMP + r) % RING].sem, chunk_at(l, I_CMP + r))
                    pe.wait_ge(cmp_in.sem, cmp_in.at(l, 32))
                    w = slot_of(I_CMP + r).rearrange("p (a e) -> p a e", e=P)
                    pe.wait_ge(blk_ready.sem, blk_ready.at(l, r + 1))
                    for a in range(L2):
                        ins = mm((bA, bB)[r][:, 0:2 * NC], w[:, a, :], blk[:, r, :, :, a], a == 0, a == L2 - 1)
                    ins.then_inc(hid_done.sem, hid_done.up())
                for r in range(2):
                    pe.wait_ge(hid_ready.sem, hid_ready.at(l, r + 1))
                    for s in range(2):
                        hs = hid[:, r, NC * s:NC * s + NC]
                        if r == 0:
                            ins = mm(bO[HD * s:HD * s + HD, 0:NC], w2[:, 0, :], hs, True, True)
                        else:
                            for t in range(NT):
                                row = 32 * (2 * s + t)
                                ins = nc.tensor.matmul(bB[row:row + NC, 64:64 + HD], hs, w2[:, 1, :], start=True,
                                                       stop=True, skip_group_check=True, tile_position=(0, row))
                    ins.then_inc(kc_done.sem, kc_done.up())
                pe.wait_ge(kc_ready.sem, kc_ready.at(l, 1))
                for n in range(NSA):
                    i, s, t, _ = nsa_unit(n)
                    c = 16 * (NT * i + t)
                    ins = mm((bA, bO)[s][:, c:c + NC], qr[HD * s:HD * s + HD, i, P * t:P * t + P],
                             kc[HD * s:HD * s + HD, 0:NC], True, True)
                ins.then_inc(cs_done.sem, cs_done.up())
                for r in range(2):
                    pe.wait_ge(bx_ready.sem, bx_ready.at(l, r + 1))
                    for j in range(JC):
                        ins = nc.tensor.transpose(bX[r][:, P * j:P * j + P],
                                                  bx[:, r, 4 * j:4 * j + 4, :].rearrange("p a b -> p (a b)"), ident)
                    ins.then_inc(bc_turned.sem, bc_turned.up())
                for r in range(2):
                    pe.wait_ge(cx_ready.sem, cx_ready.at(l, r + 1))
                    if r == 1:
                        pe.wait_ge(bc_ready.sem, bc_ready.at(l, 1))
                    for j in range(JC):
                        ins = nc.tensor.transpose((bY, bX[0])[r][:, P * j:P * j + P], cx[:, r, j, :], ident)
                    ins.then_inc(bc_turned.sem, bc_turned.up())
                params_free.made += 1
                pe.sem_inc(params_free.sem, 1)

                def filler(f, half):
                    kind, *at = FILL[f]
                    n = U_FILL + f
                    if half == 0:
                        pe.wait_ge(unit_out[n % 2].sem, unit_out[n % 2].at(l, n // 2))
                    if kind == "sbv":
                        t = at[0]
                        i = I_FILL + 4
                        pe.wait_ge(landed[(i + half) % RING].sem, chunk_at(l, i + half))
                        w = slot_of(i + half).rearrange("p (k n) -> p k n", k=KD)
                        for k in range(KD):
                            ins = mm(pj[n % 2][:, T * half:T * half + T], hT[:, k, P * t:P * t + P], w[:, k, :],
                                     k == 0, k == KD - 1)
                        if half:
                            ins.then_inc(unit_done.sem, unit_done.up())
                    elif kind == "y":
                        b, q = at
                        i = I_FILL + 18 + 2 * (b - 1) + q // 2
                        src, ready = ((oN, on_ready), (oB, ob_ready))[b - 1]
                        if half == 0:
                            if q == 0:
                                pe.wait_ge(ready.sem, ready.at(l, 4))
                            pe.wait_ge(landed[i % RING].sem, chunk_at(l, i))
                            if b == 1:
                                pe.wait_ge(upper_in.sem, upper_in.at(l, 16 * (q // 2 + 1)))
                        w = slot_of(i).rearrange("p (k n) -> p k n", k=JC)
                        c = 2 * P * (q % 2)
                        tiles(n, lambda m, k: w[:, k, c + P * m:c + P * m + P], lambda k: src[:, k, :], JC, (half,))
                    else:
                        i = I_FILL + f
                        pe.wait_ge(landed[i % RING].sem, chunk_at(l, i))
                        w = slot_of(i).rearrange("p (k n) -> p k n", k=KD)
                        tiles(n, lambda m, k: w[:, k, P * m:P * m + P], h_k, KD, (half,))

                def nsa_scores(n):
                    i, s, t, w = nsa_unit(n)
                    if n == 0:
                        pe.wait_ge(cs_ready.sem, cs_ready.at(l, 1))
                    else:
                        pe.wait_ge(s_max.sem, s_max.at(l, n))
                    mm(bA[:, 0:2 * w], qr[HD * s:HD * s + HD, i, P * t:P * t + P],
                       kr[HD * s:HD * s + HD, 1:3, 0:w], True, True).then_inc(s_done.sem, s_done.up())

                def nsa_turn(n):
                    i, s, t, w = nsa_unit(n)
                    pe.wait_ge(s_prob.sem, s_prob.at(l, n + 1))
                    if n == 0:
                        pe.wait_ge(cp_ready.sem, cp_ready.at(l, 1))
                        pe.wait_ge(kc_ready.sem, kc_ready.at(l, 2))
                        for i in range(4):
                            ins = nc.tensor.transpose(bO[:, P * i:P * i + P],
                                                      cE[:, 4 * i:4 * i + 4, :].rearrange("p a b -> p (a b)"), ident)
                        ins.then_inc(pc_done.sem, pc_done.up())
                    else:
                        pe.wait_ge(t_ready.sem, t_ready.at(l, n))
                    for b in range(2):
                        for k in range(t + 1):
                            c = P * (b * (t + 1) + k)
                            ins = nc.tensor.transpose(bB[:, c:c + P], pr[:, n % 2, c:c + P], ident)
                    ins.then_inc(t_done.sem, t_done.up())

                def nsa_values(n):
                    i, s, t, w = nsa_unit(n)
                    pe.wait_ge(t_ready.sem, t_ready.at(l, n + 1))
                    if n % 4 == 0 and n:
                        pe.wait_ge(on_ready.sem, on_ready.at(l, n // 4))
                    if n == 0:
                        pe.wait_ge(pc_ready.sem, pc_ready.at(l, 1))
                    else:
                        pe.wait_ge(v_done.sem, v_done.at(l, n))
                    o = bO[HD * s:HD * s + HD, P * t:P * t + P]
                    row = 32 * (2 * s + t)
                    nc.tensor.matmul(o, vc[row:row + NC, :], pcT[row:row + NC, i, :], start=True, stop=False,
                                     skip_group_check=True, tile_position=(row, HD * s))
                    for b in range(2):
                        for k in range(t + 1):
                            c = P * (b * (t + 1) + k)
                            ins = mm(o, vn[:, k, b, HD * s:HD * s + HD], pT[:, n % 2, c:c + P],
                                     False, b == 1 and k == t)
                    ins.then_inc(v_done.sem, v_done.up())

                def sb_scores(h):
                    i, s = h // 2, HD * (h % 2)
                    if h == 0:
                        for f in (4, 5):
                            n = U_FILL + f
                            pe.wait_ge(unit_out[n % 2].sem, unit_out[n % 2].at(l, n // 2 + 1))
                        pe.wait_ge(s_max.sem, s_max.at(l, NSA))
                        pe.wait_ge(t_ready.sem, t_ready.at(l, NSA))
                    elif h > 1:
                        pe.wait_ge(w_exp.sem, w_exp.at(l, h - 1))
                    z = (bA, bB)[h % 2]
                    mm(z[:, 0:T], sbk[s:s + HD, i, 0:P], sbq[s:s + HD, i, :], True, False)
                    mm(z[:, T:T + P], sbk[s:s + HD, i, P:T], sbq[s:s + HD, i, P:T], False, False)\
                        .then_inc(z_done.sem, z_done.up())

                def sb_rest(h):
                    pe.wait_ge(z_spm.sem, z_spm.at(l, h + 1))
                    z, p = (bA, bB)[h % 2], sbp[:, h % 2, :]
                    tri, neg1 = kon[:, K_TRI:K_TRI + P], kon[:, K_NEG1:K_NEG1 + P]
                    mm(z[:, 0:T], tri, p[:, 0:T], False, False)
                    mm(z[:, P:T], neg1, p[:, T:T + P], False, False)
                    mm(z[:, T:T + P], tri, p[:, T:T + P], False, True).then_inc(r_done.sem, r_done.up())

                def sb_values(h):
                    pe.wait_ge(w_ready.sem, w_ready.at(l, h + 1))
                    if h == 0:
                        pe.wait_ge(on_ready.sem, on_ready.at(l, 4))
                    elif h % 2 == 0:
                        pe.wait_ge(ob_ready.sem, ob_ready.at(l, h // 2))
                    o = bO[HD * (h % 2):HD * (h % 2) + HD, 0:T]
                    w = sbw[:, h % 2, :]
                    mm(o, sbv[:, 0, HD * h:HD * h + HD], w[:, 0:T], True, False)
                    mm(o[:, P:T], sbv[:, 1, HD * h:HD * h + HD], w[:, T:T + P], False, True)\
                        .then_inc(o_done.sem, o_done.up())

                def s5_inputs(s):
                    b, j, r = bX[s % 2], s // 4, 32 * (s % 4)
                    if s == 0:
                        pe.wait_ge(unit_out[0].sem, unit_out[0].at(l, 4))
                        pe.wait_ge(unit_out[1].sem, unit_out[1].at(l, 4))
                        pe.wait_ge(bc_ready.sem, bc_ready.at(l, 4))
                    elif s > 1:
                        pe.wait_ge(x5_used.sem, x5_used.at(l, s - 1))
                    for c in range(2):
                        ins = nc.tensor.matmul(b[:, T * c:T * c + T], BL[r:r + 32, c, j, :], uT[r:r + 32, j, :],
                                               start=True, stop=True, skip_group_check=True, tile_position=(r, 0))
                    ins.then_inc(x5_done.sem, x5_done.up())

                def s5_outputs(s):
                    j, r = s // 4, 32 * (s % 4)
                    pe.wait_ge(h5_ready.sem, h5_ready.at(l, s + 1))
                    if s % 4 == 0 and j:
                        pe.wait_ge(y_used.sem, y_used.at(l, j))
                    for c in range(2):
                        ins = nc.tensor.matmul(bY[r:r + 32, 0:T], CL[:, c, j, r:r + 32],
                                               s5h[:, s % 2, c, :], start=c == 0, stop=c == 1,
                                               skip_group_check=True, tile_position=(0, r))
                    ins.then_inc(y_done.sem, y_done.up())

                for q in range(SLOTS):
                    filler(q // 2, q % 2)
                    if q in S5_X:
                        s5_inputs(S5_X[q])
                    if q < NSA:
                        nsa_scores(q)
                    if 1 <= q <= NSA:
                        nsa_turn(q - 1)
                    if 2 <= q <= NSA + 1:
                        nsa_values(q - 2)
                    if q in SB_Z:
                        sb_scores(SB_Z[q])
                    if q in SB_R:
                        sb_rest(SB_R[q])
                    if q in SB_O:
                        sb_values(SB_O[q])
                    if q in S5_Y:
                        s5_outputs(S5_Y[q])

                pe.wait_ge(landed[I_GLU % RING].sem, chunk_at(l, I_GLU))
                w = slot_of(I_GLU).rearrange("p (k n) -> p k n", k=JC)
                pe.wait_ge(y_ready.sem, y_ready.at(l, 1))
                for n in range(2):
                    u = U_GLU + n
                    pe.wait_ge(unit_out[u % 2].sem, unit_out[u % 2].at(l, u // 2))
                    tiles(U_GLU + n, lambda m, k: w[:, k, P * (2 * n + m):P * (2 * n + m) + P],
                          lambda k: yT[:, k, :], JC)
                pe.wait_ge(os_ready.sem, os_ready.at(l, 2))
                for q in range(4):
                    i = I_GLU + 1 + q // 2
                    pe.wait_ge(landed[i % RING].sem, chunk_at(l, i))
                    u = U_Y + q
                    pe.wait_ge(unit_out[u % 2].sem, unit_out[u % 2].at(l, u // 2))
                    w = slot_of(i).rearrange("p (k n) -> p k n", k=JC)
                    c = 2 * P * (q % 2)
                    tiles(U_Y + q, lambda m, k: w[:, k, c + P * m:c + P * m + P], lambda k: oS[:, k, :], JC)
                pe.wait_ge(m_ready.sem, m_ready.at(l, 8))
                for q in range(4):
                    pe.wait_ge(landed[(I_OUT + q) % RING].sem, chunk_at(l, I_OUT + q))
                    u = U_OUT + q
                    pe.wait_ge(unit_out[u % 2].sem, unit_out[u % 2].at(l, u // 2))
                    w = slot_of(I_OUT + q).rearrange("p (k n) -> p k n", k=KD)
                    tiles(U_OUT + q, lambda m, k: w[:, k, P * m:P * m + P], lambda k: mT[:, k, :], KD)

                sum_squares(l, 4).then_inc(ss_done.sem, ss_done.up())
                pe.wait_ge(h_ready.sem, h_ready.at(l, 2 * KD))

                def up(i, n, turn=0, times=1):
                    pe.wait_ge(landed[i % RING].sem, chunk_at(l, i) + turn * 16)
                    pe.wait_ge(unit_out[n % 2].sem, unit_out[n % 2].at(l, n // 2) + turn * 2)
                    w = slot_of(i).rearrange("p (k n) -> p k n", k=KD)
                    for m in range(2):
                        for k in range(KD):
                            ins = mm(pj[n % 2][:, T * m:T * m + T], w[:, k, P * m:P * m + P], hT[:, k, :],
                                     k == 0, k == KD - 1)
                    ins.then_inc(unit_done.sem, 1)
                    unit_done.made += times

                def dn(i, c, first=False, turn=0, times=1):
                    pe.wait_ge(landed[i % RING].sem, chunk_at(l, i) + turn * 16)
                    pe.wait_ge(a_ready.sem, a_ready.at(l, c + 1) + turn * 2)
                    w = slot_of(i).rearrange("p (k n) -> p k n", k=2)
                    for k in range(2):
                        for m in range(KD):
                            ins = mm(down[m // 2][:, T * (m % 2):T * (m % 2) + T], w[:, k, P * m:P * m + P],
                                     aT[:, c % 2, T * k:T * k + T], first and k == 0 and m % 2 == 0, False)
                    ins.then_inc(a_used.sem, 1)
                    a_used.made += times

                i = C_FFN
                for e in range(4):
                    up(i + e, U_FFN + e)
                dn(i + 4, 0, True)
                i += 5
                with pe.Fori(0, LOOP) as j:
                    for e in range(2):
                        up(i + 3 * e, U_FFN + 4 + 2 * e, j, LOOP)
                        up(i + 3 * e + 1, U_FFN + 5 + 2 * e, j, LOOP)
                        dn(i + 3 * e + 2, 1 + e, False, j, LOOP)
                i += RING * LOOP
                up(i, U_FFN + 2 * STEPS - 2)
                up(i + 1, U_FFN + 2 * STEPS - 1)
                dn(i + 2, STEPS - 2)
                dn(i + 3, STEPS - 1)
                pe.wait_ge(a_used.sem, a_used.at(l, STEPS))
                down_done.made += 1
                pe.sem_inc(down_done.sem, 1)

            sum_squares(DEPTH, 0).then_inc(ss_done.sem, 1)
            pe.wait_ge(h_ready.sem, h_ready.at(DEPTH, KD))
            for b, o in enumerate(down):
                for e in range(4):
                    t, k = b // 2, 4 * (b % 2) + e
                    ins = nc.tensor.transpose(o[:, P * e:P * e + P], hT[:, k, P * t:P * t + P], ident)
                ins.then_inc(fin_turned.sem, 1)

        @block.scalar
        def _(a):
            A = nc.scalar.activation

            def squares(l, first, x_first):
                for b in range(4):
                    a.wait_ge(x_ready.sem, x_ready.at(l, x_first + b + 1))
                    A(sq[:, 2 * b:2 * b + 2, :], xT[:, 2 * b:2 * b + 2, :], ACT.Square)\
                        .then_inc(sq_ready.sem, sq_ready.up())

            def root(l, n):
                a.wait_ge(ms_ready.sem, ms_ready.at(l, n))
                A(rstd[:, :], ms[:, :], ACT.Sqrt).then_inc(rstd_ready.sem, rstd_ready.up())

            def copy_out(l, n, dst, func=ACT.Copy, scale=1.0):
                a.wait_ge(unit_done.sem, unit_done.at(l, n + 1))
                A(dst, unit(n), func, scale=scale).then_inc(unit_out[n % 2].sem, unit_out[n % 2].up())

            with a.Fori(0, DEPTH) as l:
                squares(l, 0, -4)
                a.wait_ge(par_turned.sem, par_turned.at(l, 3))
                for n in range(3):
                    A(par[:, n, :], bX[0][:, P * n:P * n + P], ACT.Copy).then_inc(par_ready.sem, par_ready.up())
                root(l, 1)
                a.wait_ge(par_ready.sem, par_ready.at(l, 3))
                A(s5p[:, 0, :], par[:, 0, A_ST:A_ST + ST], ACT.Exp).then_inc(step_exp.sem, step_exp.up())
                a.wait_ge(ang_ready.sem, ang_ready.at(l, 1))
                A(s5p[:, 3, :], s5p[:, 1, :], ACT.Exp).then_inc(mag_ready.sem, mag_ready.up())
                a.wait_ge(ang_ready.sem, ang_ready.at(l, 2))
                A(s5p[:, 4, :], s5p[:, 8, :], ACT.Sin)
                A(s5p[:, 5, :], s5p[:, 8, :], ACT.Sin, scale=0.5).then_inc(sin_ready.sem, sin_ready.up())
                copy_out(l, 0, qr[:, 0:2, :])
                copy_out(l, 1, qr[:, 2:4, :])
                copy_out(l, 2, kr[:, 0:2, :])
                copy_out(l, 3, kr[:, 2:4, :])
                for t in range(NT):
                    n = 4 + t
                    a.wait_ge(unit_done.sem, unit_done.at(l, n + 1))
                    A(vn[:, t, :, :], pj[n % 2][:, 0:2 * P].rearrange("p (b c) -> p b c", b=2), ACT.Copy)
                    A(ng[:, t, :], pj[n % 2][:, 2 * P:2 * P + 3 * HEADS], ACT.Tanh, scale=0.5)\
                        .then_inc(unit_out[n % 2].sem, unit_out[n % 2].up())
                copy_out(l, 6, uT[:, 0:2, :])
                copy_out(l, 7, uT[:, 2:4, :])
                for r in range(2):
                    a.wait_ge(hid_done.sem, hid_done.at(l, r + 1))
                    A(hid[:, r, 0:2 * NC], (bA, bB)[r][:, 0:2 * NC], ACT.Gelu_apprx_tanh)\
                        .then_inc(hid_ready.sem, hid_ready.up())
                a.wait_ge(kc_done.sem, kc_done.at(l, 1))
                A(kc[:, 0:NC], bO[:, 0:NC], ACT.Copy).then_inc(kc_ready.sem, kc_ready.up())
                a.wait_ge(kc_done.sem, kc_done.at(l, 2))
                for r in range(0, P, 32):
                    ins = A(vc[r:r + NC, :], bB[r:r + NC, 64:64 + HD], ACT.Copy)
                ins.then_inc(kc_ready.sem, kc_ready.up())
                for n in range(4):
                    a.wait_ge(bc_turned.sem, bc_turned.at(l, n + 1))
                    src = (bX[0], bX[1], bY, bX[0])[n]
                    dst = (BL[:, 0], BL[:, 1], CL[:, 0], CL[:, 1])[n]
                    A(dst, src[:, :].rearrange("p (j c) -> p j c", j=JC), ACT.Copy)\
                        .then_inc(bc_ready.sem, bc_ready.up())
                a.wait_ge(cs_ready.sem, cs_ready.at(l, 1))
                A(cP, cS, ACT.Exp, scale=SCALE).then_inc(ce_ready.sem, ce_ready.up())

                for q in range(SLOTS):
                    f = q // 2
                    if q < NSA:
                        n = q
                        w = nsa_unit(n)[3]
                        a.wait_ge(s_max.sem, s_max.at(l, n + 1))
                        if n >= 2:
                            a.wait_ge(t_done.sem, t_done.at(l, n - 1))
                        for b in range(2):
                            ins = A(pr[:, n % 2, w * b:w * b + w], sc[:, n % 2, w * b:w * b + w], ACT.Exp,
                                    bias=nm[:, n % 2, b:b + 1], scale=SCALE, accum_out=sm[:, n % 2, b:b + 1])
                        ins.then_inc(s_exp.sem, s_exp.up())
                    if 1 <= q <= NSA:
                        n = q - 1
                        w = nsa_unit(n)[3]
                        a.wait_ge(t_done.sem, t_done.at(l, n + 1))
                        if n >= 2:
                            a.wait_ge(v_done.sem, v_done.at(l, n - 1))
                        A(pT[:, n % 2, 0:2 * w], bB[:, 0:2 * w], ACT.Copy).then_inc(t_ready.sem, t_ready.up())
                        if n == 0:
                            a.wait_ge(pc_done.sem, pc_done.at(l, 1))
                            A(pcT[:, :, :], bO[:, :].rearrange("p (i t) -> p i t", i=4), ACT.Copy)\
                                .then_inc(pc_ready.sem, pc_ready.up())
                    if q in SB_R:
                        h = SB_R[q]
                        a.wait_ge(r_done.sem, r_done.at(l, h + 1))
                        A(sbw[:, h % 2, :], (bA, bB)[h % 2][:, 0:384], ACT.Exp).then_inc(w_exp.sem, w_exp.up())
                    if q in SB_Z:
                        h = SB_Z[q]
                        a.wait_ge(z_done.sem, z_done.at(l, h + 1))
                        if h >= 2:
                            a.wait_ge(o_done.sem, o_done.at(l, h - 1))
                        A(sbw[:, h % 2, :], (bA, bB)[h % 2][:, 0:384], ACT.Abs).then_inc(z_abs.sem, z_abs.up())
                        a.wait_ge(z_abs.sem, z_abs.at(l, h + 1))
                        A(sbw[:, h % 2, :], sbw[:, h % 2, :], ACT.Exp, scale=-1.0).then_inc(z_exp.sem, z_exp.up())
                        a.wait_ge(z_exp.sem, z_exp.at(l, h + 1))
                        A(sbw[:, h % 2, :], sbw[:, h % 2, :], ACT.Ln, bias=1.0).then_inc(z_ln.sem, z_ln.up())
                    if q % 2:
                        kind, *at = FILL[f]
                        if kind == "sbq":
                            copy_out(l, U_FILL + f, sbq[:, 2 * at[0]:2 * at[0] + 2, :], scale=SCALE)
                        elif kind == "gate":
                            b, i = at
                            copy_out(l, U_FILL + f, gate[:, KD * b + 2 * i:KD * b + 2 * i + 2, :], ACT.Tanh, 0.5)
                a.wait_ge(y_used.sem, y_used.at(l, JC))
                A(yT[:, :, :], yT[:, :, :], ACT.Gelu_apprx_tanh).then_inc(y_ready.sem, y_ready.up())
                for n in range(2):
                    copy_out(l, U_GLU + n, oS[:, 2 * n:2 * n + 2, :], ACT.Tanh, 0.5)
                squares(l, 4, 0)
                root(l, 2)

                def conv(n, e, tile, turn=0, times=1):
                    a.wait_ge(unit_done.sem, unit_done.at(l, n + 1) + turn * 4)
                    for m in range(2):
                        ins = A(cv[:, e, T * m:T * m + T], pj[n % 2][:, T * m:T * m + T], ACT.Identity,
                                bias=par[:, 2, bass.ds(tile + (C_B + m), 1)],
                                scale=par[:, 2, bass.ds(tile + (C_W2 + m), 1)])
                    ins.then_inc(cv_last.sem, 1)
                    cv_last.made += times

                def ffn_step(c, cc, turn=0, times=1):
                    if cc:
                        a.wait_ge(a_ready.sem, a_ready.at(l, cc) + turn * 2)
                    conv(U_FFN + 2 * cc, 0, c * 2, turn, times)
                    conv(U_FFN + 2 * cc + 1, 1, c * 2 + FT, turn, times)
                    n = U_FFN + 2 * cc
                    a.wait_ge(unit_out[n % 2].sem, unit_out[n % 2].at(l, n // 2 + 1) + turn * 2)
                    A(cv[:, 0, :], cv[:, 0, :], ACT.Silu).then_inc(sg_ready.sem, 1)
                    sg_ready.made += times

                ffn_step(0, 0)
                ffn_step(1, 1)
                with a.Fori(0, LOOP) as j:
                    ffn_step(j * 2 + 2, 2, j, LOOP)
                    ffn_step(j * 2 + 3, 3, j, LOOP)
                ffn_step(STEPS - 1, STEPS - 1)
            squares(DEPTH, 0, -4)
            sq_ready.made -= 4
            root(DEPTH, 1)
            rstd_ready.made -= 1

        @block.vector
        def _(v):
            TT, TS, STT = nc.vector.tensor_tensor, nc.vector.tensor_scalar, nc.vector.scalar_tensor_tensor

            nc.vector.memset(cE[:, :, :], 0.0)
            for st in (stA, stB, stC):
                nc.vector.memset(st[:, :], 0.0).then_inc(setup.sem, 1)
            v.sem_inc(unit_done.sem, 3)
            v.sem_inc(params_free.sem, 1)
            v.sem_inc(unit_out[0].sem, 1)
            v.sem_inc(unit_out[1].sem, 1)
            v.sem_inc(a_used.sem, 3)
            for b, o in enumerate(down):
                v.wait_ge(x_turned.sem, b + 1)
                nc.vector.tensor_copy(xT[:, 2 * b:2 * b + 2, :], o[:, :].rearrange("p (k t) -> p k t", k=2))\
                    .then_inc(x_ready.sem, 1)

            def norm(l, n, gain):
                v.wait_ge(ss_done.sem, ss_done.at(l, n))
                TS(ms[:, :], bO[:, 0:T], 1.0 / D, EPS, ALU.mult, ALU.add).then_inc(dve_step.sem, dve_step.up())
                v.wait_ge(dve_step.sem, dve_step.at(l, dve_step.made))
                nc.vector.reciprocal(ms[:, :], ms[:, :]).then_inc(ms_ready.sem, ms_ready.up())
                v.wait_ge(rstd_ready.sem, rstd_ready.at(l, n))
                for k in range(KD):
                    STT(hT[:, k, :], xT[:, k, :], par[:, 0, gain + k:gain + k + 1], rstd[:, :],
                        ALU.mult, ALU.mult).then_inc(h_ready.sem, h_ready.up())

            def gate_unit(b, i):
                return U_FILL + FILL.index(("gate", b, i))

            def merge(l, n, b, q):
                u = gate_unit(b, q)
                v.wait_ge(unit_out[u % 2].sem, unit_out[u % 2].at(l, u // 2 + 1))
                v.wait_ge(unit_done.sem, unit_done.at(l, n + 1))
                if b == 1:
                    dst = mT[:, 2 * q:2 * q + 2, :]
                else:
                    k = q if b == 2 else 4 + q
                    if k >= 2:
                        v.wait_ge(m_ready.sem, m_ready.at(l, k - 1))
                    dst = yt[:, k % 2, :].rearrange("p (m t) -> p m t", m=2)
                STT(dst, gate[:, KD * b + 2 * q:KD * b + 2 * q + 2, :], 1.0, unit(n),
                    ALU.add, ALU.mult).then_inc(unit_out[n % 2].sem, unit_out[n % 2].up())

            with v.Fori(0, DEPTH) as l:
                v.wait_ge(rows_in.sem, rows_in.at(l, 16 * 17))
                nc.vector.tensor_copy(
     stA[A_ST:A_ST + ST, :].rearrange("t (w p) -> t w p", w=2),
     lstep[A_ST:A_ST + ST, :].rearrange("t (w o) -> t w o", o=1).broadcast_to([ST, 2, HD]))\
         .then_inc(step_row.sem, step_row.up())
                v.wait_ge(par_ready.sem, par_ready.at(l, 1))
                norm(l, 1, A_MIX)

                def p(n):
                    return s5p[:, n, :]

                lr, li = par[:, 0, A_LR:A_LR + ST], par[:, 0, A_LI:A_LI + ST]
                step, lrs, th, mag, sn, sh, kk, t1, r, cs, ar, ai, den, rden, nr, fr, fi, t2 = map(p, range(18))
                v.wait_ge(step_exp.sem, step_exp.at(l, 1))
                TT(lrs, lr, step, ALU.mult)
                TT(th, li, step, ALU.mult).then_inc(ang_ready.sem, ang_ready.up())
                v.wait_ge(ang_ready.sem, ang_ready.at(l, 1))
                TS(kk, th, 1.0 / TWO_PI, MAGIC, ALU.mult, ALU.add).then_inc(dve_step.sem, dve_step.up())
                v.wait_ge(dve_step.sem, dve_step.last(l))
                TS(kk, kk, -MAGIC, None, ALU.add).then_inc(dve_step.sem, dve_step.up())
                v.wait_ge(dve_step.sem, dve_step.last(l))
                src = th
                for part in PI_PARTS:
                    STT(r, kk, -part, src, ALU.mult, ALU.add).then_inc(dve_step.sem, dve_step.up())
                    v.wait_ge(dve_step.sem, dve_step.last(l))
                    src = r
                TS(r, r, 3.1415925, -3.1415925, ALU.min, ALU.max).then_inc(ang_ready.sem, ang_ready.up())
                v.wait_ge(sin_ready.sem, sin_ready.at(l, 1))
                v.wait_ge(mag_ready.sem, mag_ready.at(l, 1))
                TT(cs, sh, sh, ALU.mult).then_inc(dve_step.sem, dve_step.up())
                v.wait_ge(dve_step.sem, dve_step.last(l))
                TS(cs, cs, -2.0, 1.0, ALU.mult, ALU.add).then_inc(dve_step.sem, dve_step.up())
                v.wait_ge(dve_step.sem, dve_step.last(l))
                TT(ar, mag, cs, ALU.mult)
                TT(ai, mag, sn, ALU.mult)
                TT(den, lr, lr, ALU.mult)
                TT(t1, li, li, ALU.mult).then_inc(dve_step.sem, dve_step.up())
                v.wait_ge(dve_step.sem, dve_step.last(l))
                TS(nr, ar, -1.0, None, ALU.add)
                TT(den, den, t1, ALU.add).then_inc(dve_step.sem, dve_step.up())
                v.wait_ge(dve_step.sem, dve_step.last(l))
                TT(t1, nr, lr, ALU.mult)
                TT(t2, ai, li, ALU.mult)
                nc.vector.reciprocal(rden, den).then_inc(dve_step.sem, dve_step.up())
                v.wait_ge(dve_step.sem, dve_step.last(l))
                TT(fr, t1, t2, ALU.add).then_inc(dve_step.sem, dve_step.up())
                v.wait_ge(dve_step.sem, dve_step.last(l))
                TT(fr, fr, rden, ALU.mult).then_inc(dve_step.sem, dve_step.up())
                v.wait_ge(dve_step.sem, dve_step.last(l))
                TT(t1, ai, lr, ALU.mult)
                TT(t2, nr, li, ALU.mult).then_inc(dve_step.sem, dve_step.up())
                v.wait_ge(dve_step.sem, dve_step.last(l))
                TT(fi, t1, t2, ALU.subtract).then_inc(dve_step.sem, dve_step.up())
                v.wait_ge(dve_step.sem, dve_step.last(l))
                TT(fi, fi, rden, ALU.mult).then_inc(dve_step.sem, dve_step.up())
                v.wait_ge(dve_step.sem, dve_step.last(l))
                TC, TN = tab[:, 0], tab[:, 1]
                nc.vector.tensor_copy(TC[:, :, 0], cs)
                nc.vector.tensor_copy(TN[:, :, 0], sn).then_inc(tab_d.sem, tab_d.up())
                v.wait_ge(tab_d.sem, tab_d.at(l, 1))

                v.wait_ge(mats_in.sem, mats_in.at(l, 16 * 6))

                def w3(ap):
                    return ap.rearrange("p (t o) -> p t o", o=1).broadcast_to([P, ST, GCH])

                def w3r(ap):
                    return w3(ap)

                TT(bb[:, 0], bnat[:, 0], w3(fr), ALU.mult)
                TT(bbt[:, 0], bnat[:, 1], w3(fi), ALU.mult)
                TT(bb[:, 1], bnat[:, 1], w3(fr), ALU.mult)
                TT(bbt[:, 1], bnat[:, 0], w3(fi), ALU.mult).then_inc(dve_step.sem, dve_step.up())
                v.wait_ge(dve_step.sem, dve_step.last(l))
                nc.vector.memset(bx, 0.0)
                TT(bb[:, 0], bb[:, 0], bbt[:, 0], ALU.subtract)
                TT(bb[:, 1], bb[:, 1], bbt[:, 1], ALU.add).then_inc(dve_step.sem, dve_step.up())
                v.wait_ge(dve_step.sem, dve_step.last(l))
                for c in range(2):
                    nc.vector.tensor_copy(bx[0:STATES, c, :, 0:GCH], bb[0:STATES, c])
                    nc.vector.tensor_copy(bx[STATES:P, c, :, GCH:2 * GCH], bb[STATES:P, c])\
                        .then_inc(bx_ready.sem, bx_ready.up())
                for c, mask in enumerate((K_PAR, K_NPAR)):
                    m = kon[:, mask:mask + 2]
                    for w in range(2):
                        ins = TS(cx[:, c, :, STATES * w:STATES * w + STATES], cnat[:, c], m[:, w:w + 1], None, ALU.mult)
                    ins.then_inc(cx_ready.sem, cx_ready.up())

                for e in range(7):
                    n = 1 << e
                    if e:
                        v.wait_ge(tab_p.sem, tab_p.at(l, e))
                    cn = TC[:, :, n - 1:n].broadcast_to([P, ST, n])
                    nn = TN[:, :, n - 1:n].broadcast_to([P, ST, n])
                    TT(TC[:, :, n:2 * n], TC[:, :, 0:n], cn, ALU.mult)
                    TT(tmp_d[:, :, 0:n], TN[:, :, 0:n], nn, ALU.mult).then_inc(dve_step.sem, dve_step.up())
                    v.wait_ge(dve_step.sem, dve_step.last(l))
                    TT(TC[:, :, n:2 * n], TC[:, :, n:2 * n], tmp_d[:, :, 0:n], ALU.subtract)\
                        .then_inc(tab_d.sem, tab_d.up())
                    v.wait_ge(tab_d.sem, tab_d.at(l, e + 2))

                sin_b = kon[:, K_SIN:K_SIN + T].rearrange("p (o t) -> p o t", o=1)
                for n, (o, dst) in enumerate(((bO, kr[:, 0:2, :]), (bX[1], kr[:, 2:3, :]),
                                              (bA, qr[:, 0:2, :]), (bB, qr[:, 2:4, :]))):
                    v.wait_ge(rot_done.sem, rot_done.at(l, n + 1))
                    if n:
                        v.wait_ge(rot_ready.sem, rot_ready.at(l, n))
                    m = dst.shape[1]
                    r2 = rt[:, 0:T * m].rearrange("p (m t) -> p m t", m=m)
                    TT(r2, o[:, 0:T * m].rearrange("p (m t) -> p m t", m=m), sin_b.broadcast_to([P, m, T]), ALU.mult)\
                        .then_inc(dve_step.sem, dve_step.up())
                    v.wait_ge(dve_step.sem, dve_step.last(l))
                    v.wait_ge(rot_cos.sem, rot_cos.at(l, n + 1))
                    TT(dst, dst, r2, ALU.add).then_inc(rot_ready.sem, rot_ready.up())
                v.wait_ge(rot_ready.sem, rot_ready.at(l, 4))
                v.wait_ge(unit_out[1].sem, unit_out[1].at(l, 2))

                for c, (src, own, sw) in enumerate(((kr[:, 0, :], par[:, 0, A_PK:A_PK + L2], par[:, 0, A_PKS:A_PKS + L2]),
                                                    (kr[:, 3, :], par[:, 0, A_PV:A_PV + L2], par[:, 1, B_PVS:B_PVS + L2]))):
                    rows = src.rearrange("p (m w) -> p m w", w=CSTR)
                    for g in range(2):
                        for w in range(2):
                            pos = (own if g == w else sw)[HD * g:HD * g + HD, :]
                            for b in range(2):
                                h8 = L2 // 2
                                ins = TT(blk[HD * w:HD * w + HD, c, g, :, h8 * b:h8 * b + h8],
                                         rows[HD * g:HD * g + HD, b:b + NC, w::2],
                                         pos[:, h8 * b:h8 * b + h8].rearrange("p (o a) -> p o a", o=1)
                                         .broadcast_to([HD, NC, h8]), ALU.add)
                    ins.then_inc(blk_ready.sem, blk_ready.up())
                v.wait_ge(unit_out[0].sem, unit_out[0].at(l, 3))
                v.wait_ge(unit_out[1].sem, unit_out[1].at(l, 3))
                TS(ng[:, :, :], ng[:, :, :], 0.5, 0.5, ALU.mult, ALU.add).then_inc(dve_step.sem, dve_step.up())
                v.wait_ge(dve_step.sem, dve_step.last(l))

                v.wait_ge(cs_done.sem, cs_done.at(l, 1))

                def per_key(n):
                    return cm[:, n, :].rearrange("p (n o) -> p n o", o=1).broadcast_to([P, NSA, NC])

                cmask = kon[:, K_CMASK:K_CMASK + 16 * NT].rearrange("p (o t c) -> p o t c", o=1, t=NT)
                for s in range(2):
                    raw = (bA, bO)[s][:, 0:8 * NSA].rearrange("p (i t c) -> p i t c", i=4, c=16)
                    ins = TT(cS.rearrange("p (i s t) c -> p i s t c", i=4, s=2)[:, :, s, :, :], raw[:, :, :, 0:NC],
                             cmask[:, :, :, 0:NC].broadcast_to([P, 4, NT, NC]), ALU.add)
                ins.then_inc(dve_step.sem, dve_step.up())
                v.wait_ge(dve_step.sem, dve_step.last(l))
                nc.vector.tensor_reduce(cm[:, 0, :], cS, AX, ALU.max).then_inc(dve_step.sem, dve_step.up())
                v.wait_ge(dve_step.sem, dve_step.last(l))
                TS(cm[:, 0, :], cm[:, 0, :], 0.1 * NEG, None, ALU.max).then_inc(dve_step.sem, dve_step.up())
                v.wait_ge(dve_step.sem, dve_step.last(l))
                TT(cS, cS, per_key(0), ALU.subtract).then_inc(cs_ready.sem, cs_ready.up())
                v.wait_ge(ce_ready.sem, ce_ready.at(l, 1))
                nc.vector.tensor_reduce(cm[:, 1, :], cP, AX, ALU.add).then_inc(dve_step.sem, dve_step.up())
                v.wait_ge(dve_step.sem, dve_step.last(l))
                TS(cm[:, 1, :], cm[:, 1, :], 1e-30, None, ALU.max).then_inc(dve_step.sem, dve_step.up())
                v.wait_ge(dve_step.sem, dve_step.last(l))
                nc.vector.reciprocal(cm[:, 1, :], cm[:, 1, :]).then_inc(dve_step.sem, dve_step.up())
                v.wait_ge(dve_step.sem, dve_step.last(l))
                g0 = ng[:, :, :].rearrange("p t (s i b) -> p i s t b", s=2, b=3)
                TT(cm[:, 2, :].rearrange("p (i s t) -> p i s t", i=4, s=2),
                   cm[:, 1, :].rearrange("p (i s t) -> p i s t", i=4, s=2), g0[:, :, :, :, 0], ALU.mult)\
                       .then_inc(dve_step.sem, dve_step.up())
                v.wait_ge(dve_step.sem, dve_step.last(l))
                TT(cP, cP, per_key(2), ALU.mult).then_inc(cp_ready.sem, cp_ready.up())

                def nsa_max(n):
                    t, w = nsa_unit(n)[2:]
                    v.wait_ge(s_done.sem, s_done.at(l, n + 1))
                    if n >= 2:
                        v.wait_ge(s_exp.sem, s_exp.at(l, n - 1))
                    v.sem_inc(passed.sem, 1)
                    for b in range(2):
                        ins = nc.vector.tensor_tensor_reduce(
                            sc[:, n % 2, w * b:w * b + w], bA[:, w * b:w * b + w],
                            kon[:, K_MASK + T - w:K_MASK + T], 1.0, 3.0 * NEG, ALU.add, ALU.max,
                            mx[:, n % 2, b:b + 1])
                    ins.then_inc(dve_step.sem, dve_step.up())
                    v.wait_ge(dve_step.sem, dve_step.last(l))
                    TS(nm[:, n % 2, :], mx[:, n % 2, :], -SCALE, None, ALU.mult).then_inc(s_max.sem, s_max.up())

                def nsa_sum(n):
                    i, s, t, w = nsa_unit(n)
                    v.wait_ge(s_exp.sem, s_exp.at(l, n + 1))
                    if n >= 2:
                        v.wait_ge(s_prob.sem, s_prob.at(l, n - 1))
                    TS(rc[:, n % 2, :], sm[:, n % 2, :], 1e-30, None, ALU.max).then_inc(dve_step.sem, dve_step.up())
                    v.wait_ge(dve_step.sem, dve_step.last(l))
                    nc.vector.reciprocal(rc[:, n % 2, :], rc[:, n % 2, :]).then_inc(dve_step.sem, dve_step.up())
                    v.wait_ge(dve_step.sem, dve_step.last(l))
                    c = 3 * (4 * s + i) + 1
                    TT(rg[:, n % 2, :], rc[:, n % 2, :], ng[:, t, c:c + 2], ALU.mult).then_inc(s_rec.sem, s_rec.up())

                def halves(ap, m=4):
                    return ap.rearrange("p (m t) -> p m t", m=m)

                def s5_turn(s):
                    v.wait_ge(x5_done.sem, x5_done.at(l, s + 1))
                    if s:
                        v.wait_ge(h5_ready.sem, h5_ready.at(l, s))
                    for c in range(2):
                        ins = TT(halves(s5a[:, c, :]), halves(bX[s % 2][:, :]),
                                 tab[:, c, s:s + 1, :].broadcast_to([P, 4, P]), ALU.mult)
                    ins.then_inc(x5_used.sem, x5_used.up())

                def s5_scan(s):
                    v.wait_ge(x5_turned.sem, x5_turned.at(l, s + 1))
                    decay = mag[:, s:s + 1].broadcast_to([P, P])
                    cn, nn = tab[:, 0, s, P - 1:P], tab[:, 1, s, P - 1:P]
                    for b in range(2):
                        for c in range(2):
                            g = s5x[:, c, P * b:P * b + P]
                            ins = nc.vector.tensor_tensor_scan(g, decay, g, s5i[:, 2 + c:3 + c] if b else 0.0,
                                                               ALU.mult, ALU.add)
                        if b:
                            break
                        ins.then_inc(dve_step.sem, dve_step.up())
                        v.wait_ge(dve_step.sem, dve_step.last(l))
                        gr, gi = s5x[:, 0, P - 1:P], s5x[:, 1, P - 1:P]
                        TT(s5i[:, 0:1], gi, nn, ALU.mult)
                        TT(s5i[:, 1:2], gi, cn, ALU.mult).then_inc(dve_step.sem, dve_step.up())
                        v.wait_ge(dve_step.sem, dve_step.last(l))
                        STT(s5i[:, 2:3], gr, cn, s5i[:, 0:1], ALU.mult, ALU.subtract)
                        STT(s5i[:, 3:4], gr, nn, s5i[:, 1:2], ALU.mult, ALU.add).then_inc(dve_step.sem, dve_step.up())
                        v.wait_ge(dve_step.sem, dve_step.last(l))
                    ins.then_inc(g5_ready.sem, g5_ready.up())

                for q in range(SLOTS):
                    f = q // 2
                    if q < NSA:
                        nsa_max(q)
                    if q in S5_X:
                        s5_turn(S5_X[q])
                    if q - 1 in S5_X:
                        s5_scan(S5_X[q - 1])
                    if q < NSA:
                        nsa_sum(q)
                    if 2 <= q <= NSA + 1 and (q - 2) % 4 == 3:
                        n = q - 2
                        v.wait_ge(v_done.sem, v_done.at(l, n + 1))
                        nc.vector.tensor_copy(oN[:, n // 4, :], bO[:, 0:T]).then_inc(on_ready.sem, on_ready.up())
                    if q - 1 in SB_Z:
                        h = SB_Z[q - 1]
                        v.wait_ge(z_ln.sem, z_ln.at(l, h + 1))
                        if h >= 2:
                            v.wait_ge(r_done.sem, r_done.at(l, h - 1))
                        STT(sbp[:, h % 2, :], (bA, bB)[h % 2][:, 0:384], 0.0, sbw[:, h % 2, :],
                            ALU.max, ALU.add).then_inc(z_sp.sem, z_sp.up())
                    if q in SB_O and SB_O[q] % 2:
                        h = SB_O[q]
                        v.wait_ge(o_done.sem, o_done.at(l, h + 1))
                        nc.vector.tensor_copy(oB[:, h // 2, :], bO[:, 0:T]).then_inc(ob_ready.sem, ob_ready.up())
                    if q in S5_Y and S5_Y[q] % 4 == 3:
                        j = S5_Y[q] // 4
                        v.wait_ge(y_done.sem, y_done.at(l, 4 * j + 4))
                        STT(yT[:, j, :], uT[:, j, :], par[:, 0, A_D + j:A_D + j + 1],
                            bY[:, 0:T], ALU.mult, ALU.add).then_inc(y_used.sem, y_used.up())
                    if q % 2:
                        kind, *at = FILL[f]
                        n = U_FILL + f
                        if kind in ("sbk", "sbv"):
                            v.wait_ge(unit_done.sem, unit_done.at(l, n + 1))
                            dst = (sbk[:, 2 * at[0]:2 * at[0] + 2, :] if kind == "sbk"
                                   else sbv[:, at[0], :].rearrange("p (m t) -> p m t", m=2))
                            nc.vector.tensor_copy(dst, unit(n)).then_inc(unit_out[n % 2].sem, unit_out[n % 2].up())
                        elif kind == "y":
                            merge(l, n, *at)

                for n in range(2):
                    u = U_GLU + n
                    v.wait_ge(unit_out[u % 2].sem, unit_out[u % 2].at(l, u // 2 + 1))
                    o = oS[:, 2 * n:2 * n + 2, :]
                    TS(o, o, 0.5, 0.5, ALU.mult, ALU.add).then_inc(dve_step.sem, dve_step.up())
                    v.wait_ge(dve_step.sem, dve_step.last(l))
                    TT(o, o, yT[:, 2 * n:2 * n + 2, :], ALU.mult).then_inc(os_ready.sem, os_ready.up())
                for q in range(4):
                    merge(l, U_Y + q, 0, q)
                for q in range(4):
                    n = U_OUT + q
                    v.wait_ge(unit_done.sem, unit_done.at(l, n + 1))
                    xq = xT[:, 2 * q:2 * q + 2, :]
                    STT(xq, unit(n), 0.5, xq, ALU.mult, ALU.add).then_inc(unit_out[n % 2].sem, unit_out[n % 2].up())
                    x_ready.made += 1
                    v.wait_ge(unit_out[n % 2].sem, unit_out[n % 2].at(l, n // 2 + 1))
                    v.sem_inc(x_ready.sem, 1)
                norm(l, 2, A_FFN)

                def taps(n, e, tile, turn=0, times=1):
                    u = unit_out[n % 2]
                    v.wait_ge(cv_last.sem, cv_last.at(l, n - U_FFN + 1) + turn * 4)
                    for back, col in ((1, B_W1), (2, B_W0)):
                        for m in range(2):
                            dst = cv[:, e, T * m + back:T * m + T]
                            ins = STT(dst, pj[n % 2][:, T * m:T * m + T - back],
                                      par[:, 1, bass.ds(tile + (col + m), 1)], dst, ALU.mult, ALU.add)
                        if back == 1:
                            ins.then_inc(cv_mid.sem, 1)
                            v.wait_ge(cv_mid.sem, cv_mid.at(l, n - U_FFN + 1) + turn * 4)
                        else:
                            ins.then_inc(u.sem, 1)
                    cv_mid.made += times
                    u.made += times

                def ffn_step(c, cc, turn=0, times=1):
                    taps(U_FFN + 2 * cc, 0, c * 2, turn, times)
                    taps(U_FFN + 2 * cc + 1, 1, c * 2 + FT, turn, times)

                ffn_step(0, 0)
                ffn_step(1, 1)
                with v.Fori(0, LOOP) as j:
                    ffn_step(j * 2 + 2, 2, j, LOOP)
                    ffn_step(j * 2 + 3, 3, j, LOOP)
                ffn_step(STEPS - 1, STEPS - 1)
                v.wait_ge(down_done.sem, down_done.at(l, 1))
                for b, o in enumerate(down):
                    xq = xT[:, 2 * b:2 * b + 2, :]
                    TT(xq, xq, o[:, :].rearrange("p (k t) -> p k t", k=2), ALU.add)\
                        .then_inc(x_ready.sem, x_ready.up())

            saved = dve_step.made, ms_ready.made, h_ready.made
            dve_step.made = 0
            norm(DEPTH, 1, A_FIN)
            dve_step.made, ms_ready.made, h_ready.made = saved
            for b, o in enumerate(down):
                t, k = b // 2, 4 * (b % 2)
                v.wait_ge(fin_turned.sem, b + 1)
                nc.vector.tensor_copy(mT[:, 4 * t + k // 2:4 * t + k // 2 + 2, :],
                                      o[:, :].rearrange("p (k t) -> p k t", k=2)).then_inc(fin_ready.sem, 1)

        @block.gpsimd
        def _(g):
            TT = nc.gpsimd.tensor_tensor
            with g.Fori(0, DEPTH) as l:
                TC, TN = tab[:, 0], tab[:, 1]
                for e in range(7):
                    n = 1 << e
                    g.wait_ge(tab_d.sem, tab_d.at(l, e + 1))
                    if e:
                        g.wait_ge(tab_p.sem, tab_p.at(l, e))
                    cn = TC[:, :, n - 1:n].broadcast_to([P, ST, n])
                    nn = TN[:, :, n - 1:n].broadcast_to([P, ST, n])
                    TT(TN[:, :, n:2 * n], TN[:, :, 0:n], cn, ALU.mult)
                    TT(tmp_p[:, :, 0:n], TC[:, :, 0:n], nn, ALU.mult).then_inc(pool_step.sem, pool_step.up())
                    g.wait_ge(pool_step.sem, pool_step.at(l, pool_step.made))
                    TT(TN[:, :, n:2 * n], TN[:, :, n:2 * n], tmp_p[:, :, 0:n], ALU.add)\
                        .then_inc(tab_p.sem, tab_p.up())
                cos_b = kon[:, K_COS:K_COS + T].rearrange("p (o t) -> p o t", o=1)
                for n, dst in enumerate((kr[:, 0:2, :], kr[:, 2:3, :], qr[:, 0:2, :], qr[:, 2:4, :])):
                    g.wait_ge(rot_done.sem, rot_done.at(l, n + 1))
                    TT(dst, dst, cos_b.broadcast_to([P, dst.shape[1], T]), ALU.mult)\
                        .then_inc(rot_cos.sem, rot_cos.up())

                def add_merged(k, n):
                    g.wait_ge(unit_out[n % 2].sem, unit_out[n % 2].at(l, n // 2 + 1))
                    if k >= 4:
                        g.wait_ge(m_ready.sem, m_ready.at(l, k - 3))
                    m = mT[:, 2 * (k % 4):2 * (k % 4) + 2, :]
                    TT(m, m, yt[:, k % 2, :].rearrange("p (m t) -> p m t", m=2), ALU.add)\
                        .then_inc(m_ready.sem, m_ready.up())

                def s5_turn(s):
                    g.wait_ge(x5_used.sem, x5_used.at(l, s + 1))
                    c, n = s5a[:, 0, :], s5a[:, 1, :]
                    TT(s5x[:, 0, :], c[:, 0:T], n[:, T:2 * T], ALU.add)
                    TT(s5x[:, 1, :], c[:, T:2 * T], n[:, 0:T], ALU.subtract).then_inc(x5_turned.sem, x5_turned.up())

                def s5_back(s):
                    g.wait_ge(g5_ready.sem, g5_ready.at(l, s + 1))
                    gs = s5x[:, :, :].rearrange("p c (b t) -> p (c b) t", b=2)
                    for c in range(2):
                        ins = TT(s5a[:, c, :].rearrange("p (m t) -> p m t", m=4), gs,
                                 tab[:, c, s:s + 1, :].broadcast_to([P, 4, P]), ALU.mult)
                    ins.then_inc(pool_step.sem, pool_step.up())
                    g.wait_ge(pool_step.sem, pool_step.at(l, pool_step.made))
                    if s >= 2:
                        g.wait_ge(y_done.sem, y_done.at(l, s - 1))
                    c, n = s5a[:, 0, :], s5a[:, 1, :]
                    TT(s5h[:, s % 2, 0, :], c[:, 0:T], n[:, T:2 * T], ALU.subtract)
                    TT(s5h[:, s % 2, 1, :], c[:, T:2 * T], n[:, 0:T], ALU.add).then_inc(h5_ready.sem, h5_ready.up())

                def diagonal(ap):
                    d = ap.rearrange("p (b t) -> p b t", b=3)[:, 0:3:2, :]
                    g.sem_inc(passed.sem, 1)
                    return nc.gpsimd.affine_select(out=d, in_=d, pattern=[[0, 2], [1, P]], compare_op=ALU.is_gt,
                                                   fill=0.0, base=0, channel_multiplier=-1)

                for q in range(SLOTS):
                    f = q // 2
                    if q in S5_X:
                        s5_turn(S5_X[q])
                    if q < NSA:
                        n = q
                        w = nsa_unit(n)[3]
                        g.wait_ge(s_rec.sem, s_rec.at(l, n + 1))
                        pv = cols(pr[:, n % 2, :], w)
                        TT(pv, pv, rg[:, n % 2, :].rearrange("p (b o) -> p b o", o=1)
                           .broadcast_to([P, 2, w]), ALU.mult).then_inc(s_prob.sem, s_prob.up())
                    if q - 1 in S5_X:
                        s5_back(S5_X[q - 1])
                    if q - 1 in SB_Z:
                        h = SB_Z[q - 1]
                        g.wait_ge(z_sp.sem, z_sp.at(l, h + 1))
                        diagonal(sbp[:, h % 2, :]).then_inc(z_spm.sem, z_spm.up())
                    if q in SB_R:
                        h = SB_R[q]
                        g.wait_ge(w_exp.sem, w_exp.at(l, h + 1))
                        diagonal(sbw[:, h % 2, :]).then_inc(w_ready.sem, w_ready.up())
                    if q % 2 and FILL[f][0] == "y" and FILL[f][1] == 2:
                        add_merged(FILL[f][2], U_FILL + f)
                for q in range(4):
                    add_merged(4 + q, U_Y + q)

                def product(cc, turn=0, times=1):
                    n = U_FFN + 2 * cc + 1
                    g.wait_ge(sg_ready.sem, sg_ready.at(l, cc + 1) + turn * 2)
                    g.wait_ge(unit_out[n % 2].sem, unit_out[n % 2].at(l, n // 2 + 1) + turn * 2)
                    g.wait_ge(a_used.sem, a_used.at(l, cc - 1) + turn * 2)
                    TT(aT[:, cc % 2, :], cv[:, 0, :], cv[:, 1, :], ALU.mult).then_inc(a_ready.sem, 1)
                    a_ready.made += times

                product(0)
                product(1)
                with g.Fori(0, LOOP) as j:
                    product(2, j, LOOP)
                    product(3, j, LOOP)
                product(STEPS - 1)

        off = [(t.name, t.made, t.per_layer) for t in tallies if t.made != t.per_layer]
        assert not off, off


def kernel(**inputs):
    import numpy as np
    import concourse.bacc as bacc
    from concourse.bass_utils import run_bass_kernel_spmd

    names = ["x", "norm_mix", "w_in", "ssm_lam_re", "ssm_lam_im", "ssm_log_step", "ssm_b_re", "ssm_b_im",
             "ssm_c_re", "ssm_c_im", "ssm_d", "ssm_w_glu", "cmp_w1_k", "cmp_w2_k", "cmp_pos_k",
             "cmp_w1_v", "cmp_w2_v", "cmp_pos_v", "w_branch", "w_out", "norm_ffn", "ffn_w_up",
             "ffn_conv_w", "ffn_conv_b", "ffn_w_down", "norm_final"]
    nc = bacc.Bacc("TRN2", target_bir_lowering=False, num_devices=1)
    arrays, args = {}, []
    for name in names + ["consts"]:
        a = constants() if name == "consts" else np.ascontiguousarray(inputs[name])
        arrays[f"in_{name}"] = a
        args.append(nc.dram_tensor(f"in_{name}", a.shape, mybir.dt.from_np(a.dtype), kind="ExternalInput").ap())
    args.append(nc.dram_tensor("out", (1, T, D), F32, kind="ExternalOutput").ap())
    build(nc, *args)
    r = run_bass_kernel_spmd(nc, [arrays], core_ids=[0])
    return r.results[0]["out"]
```

```python
from contextlib import ExitStack

import concourse.bass as bass
from concourse import mybir

F32 = mybir.dt.float32
F32R = mybir.dt.float32r
ALU = mybir.AluOpType
ACT = mybir.ActivationFunctionType
AX = mybir.AxisListType.X

P = 128
D = 1024
T = 256
DEPTH = 2
KD = D // P
NT = T // P
EPS = 1e-6
HD = 64
SCALE = HD ** -0.5
HEADS = 8
CH = 512
JC = CH // P
GROUPS, STATES, GCH = 32, 64, 16
ST = GROUPS * STATES // P
CMP, CSTR = 32, 16
NC = (T - CMP) // CSTR + 1
L2 = CMP // 2
F = 2816
FT = F // P
STEPS = F // (2 * P)
NEG = -1e30
TWO_PI = 6.283185307179586
PI_HIGH = 6.28125
PI_MID = int((TWO_PI - PI_HIGH) * 2 ** 21) / 2 ** 21
PI_PARTS = (PI_HIGH, PI_MID, TWO_PI - PI_HIGH - PI_MID)
MAGIC = 1.5 * 2 ** 23

C_U, C_Q, C_KV = 0, 512, 1024
C_G = 1792
C_SQ, C_SK, C_SV = 1816, 2328, 2840
C_M = 3352

RING = 3
SLOT = 2048
PLAN = ([("q", 0), ("q", 1), ("pair", C_KV, C_KV + 256), ("pair", C_KV + 512, C_KV + 128),
         ("pair", C_KV + 384, C_KV + 640), ("ngate", C_G), ("in", C_U), ("in", C_U + 256), ("cmp", 0), ("cmp", 1)]
        + [("in", c + 256 * i) for c in (C_SQ, C_SK, C_SV) for i in range(2)]
        + [("in", C_M + D * b + 256 * i) for b in (1, 2, 0) for i in range(4)]
        + [("branch", 1, 0), ("branch", 1, 1), ("branch", 2, 0), ("branch", 2, 1), ("glu",),
           ("branch", 0, 0), ("branch", 0, 1)]
        + [("out", 256 * i) for i in range(4)])
C_FFN = len(PLAN)
CHUNKS = C_FFN + 3 * STEPS
assert CHUNKS % RING == 0
I_V, I_GATES, I_CMP, I_FILL = 4, 5, 8, 10
I_SBV = I_FILL + 4
I_Y = I_FILL + 18
I_GLU = 32
I_OUT = 35
LOOP = 4
assert 3 + 2 * LOOP == STEPS

PIECE = SLOT // 2
SPLIT = 3
BY_ROW = {I_V, I_SBV, I_SBV + 1} | {C_FFN + 4 + 3 * c for c in range(STEPS - 1)} | {CHUNKS - 1}
PIECES = [(i, e) for i in range(CHUNKS) if not (I_CMP <= i < I_FILL or I_Y <= i < C_FFN)
          for e in range(1 if i == I_GATES else 2)]
PIECE_OF = {at: s for s, at in reversed(list(enumerate(PIECES)))}
S_GATES, S_FILL, S_FFN = PIECE_OF[(I_GATES, 0)], PIECE_OF[(I_FILL, 0)], PIECE_OF[(C_FFN, 0)]
assert len(PIECES) % SPLIT == 0 and S_FFN == S_FILL + 36
TURN = 12

FILL = ([("sbq", 0), ("sbq", 1), ("sbk", 0), ("sbk", 1), ("sbv", 0), ("sbv", 1)]
        + [("gate", b, i) for b in (1, 2, 0) for i in range(4)]
        + [("y", b, i) for b in (1, 2) for i in range(4)])
U_FILL = 8
U_GLU = U_FILL + len(FILL)
U_Y = U_GLU + 2
U_OUT = U_Y + 4
U_FFN = U_OUT + 4
UNITS = U_FFN + 2 * STEPS
WHOLE = 18
assert UNITS % 2 == 0


def ffn_piece(c, n=0):
    return S_FFN + 2 * n + (4 + 6 * (c - 1) if c else 0)


SLOTS = 2 * len(FILL)
NSA = 16
CMP_HID, CMP_OUT, CMP_S = {0: 0, 1: 1}, 2, 3
NSA_S = {5 + n: n for n in range(NSA)}
NSA_T = {7 + n: n for n in range(NSA)}
NSA_V = {8 + n: n for n in range(NSA)}
SB_Z = {24 + 2 * h: h for h in range(HEADS)}
SB_R = {s + 2: h for s, h in SB_Z.items()}
SB_O = {s + 3: h for s, h in SB_Z.items()}
S5_X = {4 + 2 * s: s for s in range(ST)}
S5_Y = {7 + 2 * s: s for s in range(ST)}

K_ID, K_ROT, K_TRI, K_NEG1 = 0, 128, 256, 384
K_COS, K_SIN = 512, 768
K_MASK = 1024
K_CMASK = 1280
K_PAR = 1312
K_NPAR = 1314
K_EPS = 1316
K_ALL = 1317

A_MIX, A_FFN, A_D, A_FIN, A_LR, A_LI, A_PK, A_PV, A_ST, A_PKS = 0, 8, 16, 20, 32, 48, 64, 80, 96, 112
B_W0, B_W1, B_PVS = 0, 22 * 2, 96
C_W2, C_B = 0, 44


def constants():
    import numpy as np

    k = np.zeros((P, K_ALL), np.float32)
    i = np.arange(P)
    k[:, K_ID:K_ID + P] = np.eye(P)
    for m in range(P):
        d = m % HD
        if d < HD // 2:
            k[m + HD // 2, K_ROT + m] = -1.0
        else:
            k[m - HD // 2, K_ROT + m] = 1.0
    k[:, K_TRI:K_TRI + P] = -(i[:, None] >= i[None, :]).astype(np.float32)
    k[:, K_NEG1:K_NEG1 + P] = -1.0
    freq = (np.float32(1.0) / (np.float32(10000.0) ** (np.arange(0, HD, 2, dtype=np.float32) / np.float32(HD))))
    ang = np.arange(T, dtype=np.float32)[:, None] * freq[None, :].astype(np.float32)
    cs, sn = np.cos(ang).T, np.sin(ang).T
    k[:, K_COS:K_COS + T] = np.tile(cs, (4, 1))
    k[:, K_SIN:K_SIN + T] = np.tile(sn, (4, 1))
    k[:, K_MASK + P:K_MASK + 2 * P] = np.where(i[None, :] <= i[:, None], 0.0, NEG)
    for t in range(NT):
        ends = np.arange(NC) * CSTR + CMP - 1
        k[:, K_CMASK + 16 * t:K_CMASK + 16 * t + NC] = np.where(ends[None, :] <= i[:, None] + P * t, 0.0, NEG)
    for w in range(2):
        k[:, K_PAR + w] = ((i // GCH) % 2 == w)
        k[:, K_NPAR + w] = -k[:, K_PAR + w]
    k[:, K_EPS] = EPS
    return k


def kind_of(i):
    return PLAN[i][0] if i < C_FFN else "ffn"


class Tally:

    def __init__(self, sem, name, per_layer, start=0):
        self.sem, self.name, self.per_layer, self.start, self.made = sem, name, per_layer, start, 0

    def up(self, n=1):
        self.made += n
        return n

    def last(self, l):
        return self.at(l, self.made)

    def at(self, l, k):
        return l * self.per_layer + (self.start + k)


def build(nc, x, norm_mix, w_in, ssm_lam_re, ssm_lam_im, ssm_log_step, ssm_b_re, ssm_b_im,
          ssm_c_re, ssm_c_im, ssm_d, ssm_w_glu, cmp_w1_k, cmp_w2_k, cmp_pos_k,
          cmp_w1_v, cmp_w2_v, cmp_pos_v, w_branch, w_out, norm_ffn, ffn_w_up,
          ffn_conv_w, ffn_conv_b, ffn_w_down, norm_final, consts, out):
    with ExitStack() as ctx:
        def sb(name, shape, dtype=F32):
            return ctx.enter_context(nc.sbuf_tensor(name, shape, dtype))

        def bank(name):
            return ctx.enter_context(nc.psum_tensor(name, [P, 512], F32))

        tallies = []

        def sem(name, per_layer=0, start=0):
            t = Tally(ctx.enter_context(nc.semaphore(name)), name, per_layer, start)
            tallies.append(t)
            return t

        ring = sb("ring", [P, RING, SLOT])
        kon = sb("kon", [P, K_ALL])
        xT = sb("xT", [P, KD, T])
        hh = sb("hh", [P, KD, T], F32R)
        hl = sb("hl", [P, KD, T], F32R)
        wh = sb("wh", [P, SPLIT, PIECE], F32R)
        wl = sb("wl", [P, SPLIT, PIECE], F32R)
        ah = sb("ah", [P, 2 * T], F32R)
        al = sb("al", [P, 2 * T], F32R)
        mT = sb("mT", [P, KD, T])
        rstd = sb("rstd", [P, T])
        eps2 = sb("eps2", [P, 1])
        stA = sb("stA", [P, P])
        stB = sb("stB", [P, P])
        stC = sb("stC", [P, P])
        par = sb("par", [P, 3, P])
        lstep = sb("lstep", [P, 2])
        bnat = sb("bnat", [P, 2, ST, GCH])
        cnat = sb("cnat", [P, 2, JC, STATES])
        w2 = sb("w2", [P, 2, HD])
        uT = sb("uT", [P, JC, T])
        qr = sb("qr", [P, 4, T])
        kr = sb("kr", [P, 4, T])
        vn = sb("vn", [P, NT, 2, P])
        ng = sb("ng", [P, NT, 3 * HEADS])
        hid = sb("hid", [P, 2, 32])
        kc = sb("kc", [P, 16])
        vc = sb("vc", [P, HD])
        cE = sb("cE", [P, NSA, 32])
        cm = sb("cm", [P, 3, NSA])
        pcT = sb("pcT", [P, 4, P])
        mx = sb("mx", [P, 2, 2])
        nm = sb("nm", [P, 2, 2])
        sm = sb("sm", [P, 2, 2])
        rc = sb("rc", [P, 2, 2])
        rg = sb("rg", [P, 2, 2])
        sbq = sb("sbq", [P, JC, T])
        sbk = sb("sbk", [P, 4, T])
        sbv = sb("sbv", [P, NT, CH])
        sbw = sb("sbw", [P, 3, 384])
        sbp = sb("sbp", [P, 2, 384])
        gate = sb("gate", [P, 3 * KD, T])
        oN, oB, oS, yT = qr, sbk, sbq, uT
        tab = sb("tab", [P, 2, ST, P])
        s5p = sb("s5p", [P, 20, ST])
        BL = sb("BL", [P, 2, JC, P])
        CL = sb("CL", [P, 2, JC, P])
        s5a = sb("s5a", [P, 2, 2 * T])
        s5x = sb("s5x", [P, 2, T])
        s5i = sb("s5i", [P, 4])
        s5h = sb("s5h", [P, 2, 2, T])
        work = sb("work", [P, 3, 2, 2 * T])
        sc = work[:, 0]
        pr = work[:, 1]
        pT = work[:, 2]
        cv = work[:, 0]
        aT = work[:, 1]
        yt = work[:, 2]
        cS = work[:, 2, 0, 0:NSA * NC].rearrange("p (n c) -> p n c", c=NC)
        cP = cE[:, :, 0:NC]
        rt = work[:, 0, 0, :]
        blk = s5a[:, :, :].rearrange("p a b -> p (a b)")[:, 0:4 * NC * L2].rearrange(
            "p (r g n a) -> p r g n a", r=2, g=2, n=NC)
        bb = s5h[:, 0, :, :].rearrange("p c (t i) -> p c t i", i=GCH)
        bbt = s5h[:, 1, :, :].rearrange("p c (t i) -> p c t i", i=GCH)
        bx = gate[:, 0:4, :].rearrange("p a b -> p (a b)").rearrange("p (c t i) -> p c t i", c=2, t=ST)
        cx = gate[:, 4:8, :].rearrange("p a b -> p (a b)").rearrange("p (c j q) -> p c j q", c=2, j=JC)
        tmp_d = gate[:, 8:12, :].rearrange("p a b -> p (a b)").rearrange("p (t n) -> p t n", t=ST)
        tmp_p = gate[:, 12:16, :].rearrange("p a b -> p (a b)").rearrange("p (t n) -> p t n", t=ST)

        sq = gate[:, 2 * KD:3 * KD, :]
        hT = sq
        xs = sq.rearrange("p (t a) b -> p t (a b)", t=NT)

        pj = [bank(f"pj{i}") for i in range(2)]
        bX = [bank(f"bX{i}") for i in range(2)]
        bY = bank("bY")
        bA = bank("bA")
        bB = bank("bB")
        bO = bank("bO")
        down = [bX[0], bX[1], bA, bB]

        consts_in = sem("consts_in")
        x_in = sem("x_in")
        setup = sem("setup")
        passed = sem("passed")
        out_sent = sem("out_sent")
        landed = [sem(f"landed{i}", 16 * CHUNKS // RING) for i in range(RING)]
        q_in = [sem(f"q_in{i}", 16 * 3) for i in range(2)]
        pair_in = sem("pair_in", 16 * 3)
        w_hi = sem("w_hi", len(PIECES))
        w_lo = sem("w_lo", len(PIECES), 6)
        w_used = sem("w_used", len(PIECES), SPLIT)
        cmp_in = sem("cmp_in", 32)
        upper_in = sem("upper_in", 32)
        rows_in = sem("rows_in", 16 * 17)
        mats_in = sem("mats_in", 16 * 6)
        params_free = sem("params_free", 1, 1)
        unit_done = sem("unit_done", WHOLE)
        unit_out = [sem(f"unit_out{i}", UNITS // 2, 1) for i in range(2)]
        x_turned = sem("x_turned")
        x_ready = sem("x_ready", 8, 4)
        sq_ready = sem("sq_ready", 8)
        ss_done = sem("ss_done", 2)
        rms_ready = sem("rms_ready", 2)
        h_new = sem("h_new", 2 * KD)
        h_hi = sem("h_hi", 2 * KD)
        h_ready = sem("h_ready", 2 * KD)
        step_row = sem("step_row", 1)
        par_turned = sem("par_turned", 3)
        par_ready = sem("par_ready", 3)
        step_exp = sem("step_exp", 1)
        ang_ready = sem("ang_ready", 2)
        mag_ready = sem("mag_ready", 1)
        sin_ready = sem("sin_ready", 1)
        tab_d = sem("tab_d", 8)
        tab_p = sem("tab_p", 7)
        bx_ready = sem("bx_ready", 2)
        cx_ready = sem("cx_ready", 2)
        bx_clear = sem("bx_clear", 1)
        bc_turned = sem("bc_turned", 4)
        bc_ready = sem("bc_ready", 4)
        dve_step = sem("dve_step", 136)
        rot_done = sem("rot_done", 4)
        rot_cos = sem("rot_cos", 4)
        rot_ready = sem("rot_ready", 4)
        blk_ready = sem("blk_ready", 2)
        hid_done = sem("hid_done", 2)
        hid_ready = sem("hid_ready", 2)
        kc_done = sem("kc_done", 2)
        kc_ready = sem("kc_ready", 2)
        cs_done = sem("cs_done", 1)
        cs_ready = sem("cs_ready", 1)
        ce_ready = sem("ce_ready", 1)
        cp_ready = sem("cp_ready", 1)
        pc_done = sem("pc_done", 1)
        pc_ready = sem("pc_ready", 1)
        s_done = sem("s_done", NSA)
        s_max = sem("s_max", NSA)
        s_exp = sem("s_exp", NSA)
        s_rec = sem("s_rec", NSA)
        s_prob = sem("s_prob", NSA)
        t_done = sem("t_done", NSA)
        t_ready = sem("t_ready", NSA)
        v_done = sem("v_done", NSA)
        on_ready = sem("on_ready", 4)
        z_done = sem("z_done", HEADS)
        z_abs = sem("z_abs", HEADS)
        z_exp = sem("z_exp", HEADS)
        z_ln = sem("z_ln", HEADS)
        z_sp = sem("z_sp", HEADS)
        z_spm = sem("z_spm", HEADS)
        r_done = sem("r_done", HEADS)
        w_exp = sem("w_exp", HEADS)
        w_ready = sem("w_ready", HEADS)
        o_done = sem("o_done", HEADS)
        ob_ready = sem("ob_ready", 4)
        x5_done = sem("x5_done", ST)
        x5_used = sem("x5_used", ST)
        x5_turned = sem("x5_turned", ST)
        g5_ready = sem("g5_ready", ST)
        pool_step = sem("pool_step", 7 + ST)
        h5_ready = sem("h5_ready", ST)
        y_done = sem("y_done", ST)
        y_used = sem("y_used", JC)
        y_ready = sem("y_ready", 1)
        os_ready = sem("os_ready", 2)
        m_ready = sem("m_ready", 8)
        cv_last = sem("cv_last", 2 * STEPS)
        cv_mid = sem("cv_mid", 2 * STEPS)
        sg_ready = sem("sg_ready", STEPS)
        a_ready = sem("a_ready", STEPS)
        a_hi = sem("a_hi", STEPS)
        a_split = sem("a_split", STEPS, 2)
        down_done = sem("down_done", 4)
        fin_turned = sem("fin_turned")
        fin_ready = sem("fin_ready")

        ident = kon[:, K_ID:K_ID + P]

        def chunk_at(l, i):
            return landed[i % RING].at(l, 16 * (i // RING + 1))

        def summed(n):
            if n < U_FILL:
                return w_used, (2, 4, 6, 8, 10, 11, 13, 15)[n]
            if n < U_FILL + 18:
                return w_used, S_FILL + 2 * (n - U_FILL + 1)
            if n < U_FFN:
                return unit_done, n - U_FILL - 17
            return w_used, ffn_piece((n - U_FFN) // 2, (n - U_FFN) % 2) + 2

        def piece_from(s, dst):
            i, e = PIECES[s]
            dst = dst[:, s % SPLIT, :]
            if i == I_GATES:
                n = KD * 3 * HEADS
                return slot_of(i)[:, 0:n], dst[:, 0:n]
            if i in BY_ROW:
                return slot_of(i)[:, PIECE * e:PIECE * e + PIECE], dst
            return (slot_of(i).rearrange("p (k n) -> p k n", k=KD)[:, :, P * e:P * e + P],
                    dst.rearrange("p (k n) -> p k n", k=KD))

        def unit(n):
            return pj[n % 2][:, :].rearrange("p (m t) -> p m t", m=2)

        def slot_of(i):
            return ring[:, i % RING, :]

        def nsa_unit(n):
            i, s, t = n // 4, n // 2 % 2, n % 2
            return i, s, t, P * (t + 1)

        def cols(ap, w):
            return ap[:, 0:2 * w].rearrange("p (b w) -> p b w", b=2)

        xd = x.rearrange("b (t p) d -> p (b t) d", p=P)
        od = out.rearrange("b (t p) d -> p (b t) d", p=P)

        block = ctx.enter_context(nc.Block())

        @block.sync
        def _(sp):
            sp.dma_start(kon[:, :], consts).then_inc(consts_in.sem, 16)
            sp.dma_start(xs, xd).then_inc(x_in.sem, 16)
            sp.wait_ge(setup.sem, 3)

            def row(w, l):
                return w[bass.ds(l, 1)]

            def par_in(dst, src):
                sp.dma_start(dst, src).then_inc(rows_in.sem, rows_in.up(16))

            def mat_in(dst, src):
                sp.dma_start(dst, src).then_inc(mats_in.sem, mats_in.up(16))

            def last_reader(i):
                if (i, 0) in PIECE_OF:
                    return w_lo, PIECE_OF[(i, 0 if i == I_GATES else 1)] + 1
                if i < I_FILL:
                    return hid_done, i - I_CMP + 1
                if i < I_OUT:
                    return unit_done, 2 * (i - I_Y + 1)
                return unit_done, 2 * (I_OUT - I_Y) + i - I_OUT + 1

            def load(l, i):
                kind, *at = PLAN[i]
                dst = slot_of(i)
                t, k = last_reader((i - RING) % CHUNKS)
                sp.wait_ge(t.sem, t.at(l, k if i >= RING else k - t.per_layer))
                sp.sem_inc(passed.sem, 1)
                if kind in ("in", "ngate", "out"):
                    n = 3 * HEADS if kind == "ngate" else 256
                    w = w_out if kind == "out" else w_in
                    src = row(w, l)[:, :, at[0]:at[0] + n].rearrange("l (k p) n -> p (l k) n", p=P)
                    dst = dst[:, 0:KD * n].rearrange("p (k n) -> p k n", k=KD)
                elif kind == "q":
                    for s in range(2):
                        c = C_Q + CH // 2 * s + P * at[0]
                        src = row(w_in, l)[:, :, c:c + P].rearrange("l (k p) (i d) -> p (l k) i d", p=P, i=2)
                        to = dst.rearrange("p (k i s d) -> p k i s d", k=KD, i=2, s=2)[:, :, :, s, :]
                        for i in range(2):
                            ins = sp.dma_start(to[:, :, i, :], src[:, :, i, :])
                            if s and i:
                                ins.then_inc(landed[at[0]].sem, landed[at[0]].up(16))
                            else:
                                ins.then_inc(q_in[at[0]].sem, q_in[at[0]].up(16))
                    return
                elif kind == "pair":
                    dst = dst.rearrange("p (k n) -> p k n", k=KD)
                    src = [row(w_in, l)[:, :, c:c + P].rearrange("l (k p) n -> p (l k) n", p=P) for c in at]
                    sp.dma_start(dst[:, :, 0:P], src[0]).then_inc(pair_in.sem, pair_in.up(16))
                    dst, src = dst[:, :, P:2 * P], src[1]
                elif kind == "cmp":
                    src = row((cmp_w1_k, cmp_w1_v)[at[0]], l).rearrange("l (a b) d e -> (b d) (l a) e", b=2)
                    dst = dst.rearrange("p (a e) -> p a e", e=P)
                    sp.dma_start(dst[:, 0:L2 // 2], src[:, 0:L2 // 2]).then_inc(cmp_in.sem, cmp_in.up(16))
                    dst, src = dst[:, L2 // 2:L2], src[:, L2 // 2:L2]
                elif kind == "glu":
                    src = row(ssm_w_glu, l).rearrange("l (k p) n -> p (l k) n", p=P)
                    dst = dst.rearrange("p (k n) -> p k n", k=JC)
                else:
                    b, half = at
                    dst = dst.rearrange("p (k n) -> p k n", k=JC)
                    w = row(w_branch, l)[:, b, :, CH * half:CH * half + CH]
                    if b == 1:
                        src = w.rearrange("l (s k p) n -> s p (l k) n", p=HD, s=2)
                        sp.dma_start(dst[0:HD], src[0]).then_inc(upper_in.sem, upper_in.up(16))
                        dst, src = dst[HD:P], src[1]
                    else:
                        src = w.rearrange("l (k p) n -> p (l k) n", p=P)
                sp.dma_start(dst, src).then_inc(landed[i % RING].sem, landed[i % RING].up(16))

            def load_ffn(l, i, part, c, turn=0, times=1):
                t, k = last_reader(i - RING)
                more = turn * TURN if times > 1 else 0
                sp.wait_ge(t.sem, t.at(l, k) + more)
                sp.sem_inc(passed.sem, 1)
                if part == "down":
                    src = row(ffn_w_down, l)[:, bass.ds(c * 256, 256), :].rearrange("l (k p) n -> p (l k) n", p=P)
                    dst = slot_of(i).rearrange("p (k n) -> p k n", k=2)
                else:
                    first = F if part == "value" else 0
                    src = row(ffn_w_up, l)[:, :, bass.ds(c * 256 + first, 256)].rearrange(
                        "l (k p) n -> p (l k) n", p=P)
                    dst = slot_of(i).rearrange("p (k n) -> p k n", k=KD)
                sp.dma_start(dst, src).then_inc(landed[i % RING].sem, 16)
                landed[i % RING].made += 16 * times

            with sp.Fori(0, DEPTH) as l:
                load(l, 0)
                load(l, 1)
                sp.wait_ge(params_free.sem, params_free.at(l, 0))
                sp.sem_inc(passed.sem, 1)
                par_in(stA[A_MIX:A_MIX + 8, :], row(norm_mix, l).rearrange("l (k p) -> (l k) p", p=P))
                par_in(stA[A_FFN:A_FFN + 8, :], row(norm_ffn, l).rearrange("l (k p) -> (l k) p", p=P))
                par_in(stA[A_D:A_D + 4, :], row(ssm_d, l).rearrange("l (k g) i -> (l k) (g i)", k=4))
                par_in(stA[A_FIN:A_FIN + 8, :], norm_final.rearrange("(k p) -> k p", p=P))
                par_in(stA[A_LR:A_LR + ST, :], row(ssm_lam_re, l).rearrange("l (t w) p -> (l t) (w p)", w=2))
                par_in(stA[A_LI:A_LI + ST, :], row(ssm_lam_im, l).rearrange("l (t w) p -> (l t) (w p)", w=2))
                par_in(lstep[A_ST:A_ST + ST, :], row(ssm_log_step, l).rearrange("l (t w) -> (l t) w", w=2))
                for pos, own, st, swap in ((cmp_pos_k, A_PK, stA, A_PKS), (cmp_pos_v, A_PV, stB, B_PVS)):
                    src = row(pos, l).rearrange("l (a b) d -> (l a) b d", b=2)
                    par_in(stA[own:own + L2, :].rearrange("a (b d) -> a b d", b=2), src)
                    dst = st[swap:swap + L2, :].rearrange("a (b d) -> a b d", b=2)
                    for b in range(2):
                        par_in(dst[:, b:b + 1, :], src[:, 1 - b:2 - b, :])
                cw = row(ffn_conv_w, l)
                par_in(stB[B_W0:B_W0 + 2 * FT, :], cw[:, 0, :].rearrange("l (k p) -> (l k) p", p=P))
                par_in(stB[B_W1:B_W1 + 2 * FT, :], cw[:, 1, :].rearrange("l (k p) -> (l k) p", p=P))
                par_in(stC[C_W2:C_W2 + 2 * FT, :], cw[:, 2, :].rearrange("l (k p) -> (l k) p", p=P))
                par_in(stC[C_B:C_B + 2 * FT, :], row(ffn_conv_b, l).rearrange("l (k p) -> (l k) p", p=P))
                for r, w in enumerate((ssm_b_re, ssm_b_im)):
                    mat_in(bnat[:, r], row(w, l).rearrange("l (t w) p i -> (w p) (l t) i", w=2))
                for r, w in enumerate((ssm_c_re, ssm_c_im)):
                    mat_in(cnat[:, r], row(w, l).rearrange("l (j q) i p -> (q i) (l j) p", j=JC))
                for r, w in enumerate((cmp_w2_k, cmp_w2_v)):
                    mat_in(w2[:, r], row(w, l).rearrange("l e d -> (l e) d"))
                for i in range(2, C_FFN):
                    load(l, i)
                i = C_FFN
                load_ffn(l, i, "gate", 0)
                load_ffn(l, i + 1, "value", 0)
                load_ffn(l, i + 2, "gate", 1)
                load_ffn(l, i + 3, "value", 1)
                load_ffn(l, i + 4, "down", 0)
                i += 5
                with sp.Fori(0, LOOP) as j:
                    for e in range(2):
                        for n, part in enumerate(("gate", "value", "down")):
                            c = j * 2 + (1 + e if part == "down" else 2 + e)
                            load_ffn(l, i + 3 * e + n, part, c, j, LOOP)
                i += 6 * LOOP
                load_ffn(l, i, "gate", STEPS - 1)
                load_ffn(l, i + 1, "value", STEPS - 1)
                load_ffn(l, i + 2, "down", STEPS - 2)
                load_ffn(l, i + 3, "down", STEPS - 1)
            sp.wait_ge(fin_ready.sem, 4)
            sp.dma_start(od, mT[:, :, :].rearrange("p (t a) b -> p t (a b)", t=NT)).then_inc(out_sent.sem, 16)
            sp.wait_ge(out_sent.sem, 16)

        @block.tensor
        def _(pe):
            def mm(o, a, b, start, stop):
                return nc.tensor.matmul(o, a, b, start=start, stop=stop, skip_group_check=True)

            def tiles(n, lhs, rhs, kt, halves=(0, 1)):
                for m in halves:
                    for k in range(kt):
                        ins = mm(pj[n % 2][:, T * m:T * m + T], lhs(m, k), rhs(k), k == 0, k == kt - 1)
                if 1 in halves:
                    ins.then_inc(unit_done.sem, unit_done.up())

            def piece(l, s, o, turn=0):
                pe.wait_ge(w_lo.sem, w_lo.at(l, s + 1) + turn)
                hi, lo = (w[:, s % SPLIT, :].rearrange("p (k n) -> p k n", k=KD) for w in (wh, wl))
                for k in range(KD):
                    if s in (0, S_FFN):
                        pe.wait_ge(h_ready.sem, h_ready.at(l, (KD if s else 0) + k + 1))
                    mm(o, hi[:, k, :], hh[:, k, :], k == 0, False)
                    mm(o, hi[:, k, :], hl[:, k, :], False, False)
                    ins = mm(o, lo[:, k, :], hh[:, k, :], False, k == KD - 1)
                return ins

            def turned_piece(l, s, o, n):
                pe.wait_ge(w_lo.sem, w_lo.at(l, s + 1))
                rows = KD if s == S_GATES else KD // 2
                first = 0 if s == S_GATES else rows * PIECES[s][1]
                hi, lo = (w[:, s % SPLIT, 0:rows * n].rearrange("p (k n) -> p k n", k=rows) for w in (wh, wl))
                for k in range(rows):
                    for t in range(NT):
                        c = slice(P * t, P * t + P)
                        kk = first + k
                        mm(o(t), hh[:, kk, c], hi[:, k, :], kk == 0 and t == 0, False)
                        mm(o(t), hh[:, kk, c], lo[:, k, :], False, False)
                        ins = mm(o(t), hl[:, kk, c], hi[:, k, :], False, kk == KD - 1)
                return ins

            def sum_squares(l, first):
                for k in range(KD):
                    if k == KD - 2 and first == 0 and l is not DEPTH:
                        pe.wait_ge(step_row.sem, step_row.at(l, 1))
                        for n, st in enumerate((stA, stB, stC)):
                            nc.tensor.transpose(bX[0][:, P * n:P * n + P], st[:, :], ident)\
                                .then_inc(par_turned.sem, par_turned.up())
                    if k % 2 == 0:
                        pe.wait_ge(sq_ready.sem, sq_ready.at(l, first + k // 2 + 1))
                    ins = mm(bO[:, 0:T], kon[:, K_NEG1:K_NEG1 + P], sq[:, k, :], k == 0, k == KD - 1)
                return ins

            pe.wait_ge(consts_in.sem, 16)
            pe.wait_ge(x_in.sem, 16)
            for b, o in enumerate(down):
                for k in range(2):
                    for t in range(NT):
                        kk = 2 * b + k
                        ins = nc.tensor.transpose(o[:, T * k + P * t:T * k + P * t + P],
                                                  xs[:, t, P * kk:P * kk + P], ident)
                ins.then_inc(x_turned.sem, 1)

            with pe.Fori(0, DEPTH) as l:
                sum_squares(l, 0).then_inc(ss_done.sem, ss_done.up())
                for s in range(8):
                    n = s // 2
                    if s % 2 == 0:
                        pe.wait_ge(unit_out[n % 2].sem, unit_out[n % 2].at(l, n // 2))
                    c = T * (s % 2)
                    piece(l, s, pj[n % 2][:, c:c + T]).then_inc(w_used.sem, w_used.up())
                pe.wait_ge(unit_out[0].sem, unit_out[0].at(l, 2))
                for s in (8, 9):
                    turned_piece(l, s, lambda t: pj[0][:, T * t:T * t + T], T).then_inc(w_used.sem, w_used.up())
                pe.wait_ge(unit_out[1].sem, unit_out[1].at(l, 2))
                turned_piece(l, S_GATES, lambda t: pj[1][:, 3 * HEADS * t:3 * HEADS * (t + 1)], 3 * HEADS)\
                    .then_inc(w_used.sem, w_used.up())
                for n, (o, src, u) in enumerate(((bO, kr[:, 0:2, :], 2), (bX[1], kr[:, 2:3, :], 3),
                                                 (bA, qr[:, 0:2, :], 0), (bB, qr[:, 2:4, :], 1))):
                    pe.wait_ge(unit_out[u % 2].sem, unit_out[u % 2].at(l, u // 2 + 1))
                    src = src.rearrange("p a b -> p (a b)")
                    mm(o[:, 0:src.shape[1]], kon[:, K_ROT:K_ROT + P], src, True, True)\
                        .then_inc(rot_done.sem, rot_done.up())
                for s in range(11, 15):
                    n = 6 + (s - 11) // 2
                    if s % 2:
                        pe.wait_ge(unit_out[n % 2].sem, unit_out[n % 2].at(l, n // 2))
                    c = T * ((s - 11) % 2)
                    piece(l, s, pj[n % 2][:, c:c + T]).then_inc(w_used.sem, w_used.up())
                def filler(f, half):
                    kind, *at = FILL[f]
                    n = U_FILL + f
                    if half == 0:
                        pe.wait_ge(unit_out[n % 2].sem, unit_out[n % 2].at(l, n // 2))
                    if kind == "sbv":
                        turned_piece(l, S_FILL + 2 * f + half, lambda t: pj[n % 2][:, T * t:T * t + T], T)\
                            .then_inc(w_used.sem, w_used.up())
                    elif kind == "y":
                        b, q = at
                        i = I_Y + 2 * (b - 1) + q // 2
                        src, ready = ((oN, on_ready), (oB, ob_ready))[b - 1]
                        if half == 0:
                            if q == 0:
                                pe.wait_ge(ready.sem, ready.at(l, 4))
                            pe.wait_ge(landed[i % RING].sem, chunk_at(l, i))
                            if b == 1:
                                pe.wait_ge(upper_in.sem, upper_in.at(l, 16 * (q // 2 + 1)))
                        w = slot_of(i).rearrange("p (k n) -> p k n", k=JC)
                        c = 2 * P * (q % 2)
                        tiles(n, lambda m, k: w[:, k, c + P * m:c + P * m + P], lambda k: src[:, k, :], JC, (half,))
                    else:
                        piece(l, S_FILL + 2 * f + half, pj[n % 2][:, T * half:T * half + T])\
                            .then_inc(w_used.sem, w_used.up())

                def cmp_hidden(r):
                    if r == 0:
                        pe.wait_ge(rot_ready.sem, rot_ready.at(l, 4))
                    pe.wait_ge(landed[(I_CMP + r) % RING].sem, chunk_at(l, I_CMP + r))
                    pe.wait_ge(cmp_in.sem, cmp_in.at(l, 32))
                    w = slot_of(I_CMP + r).rearrange("p (a e) -> p a e", e=P)
                    pe.wait_ge(blk_ready.sem, blk_ready.at(l, r + 1))
                    for a in range(L2):
                        ins = mm((bA, bB)[r][:, 0:2 * NC], w[:, a, :], blk[:, r, :, :, a], a == 0, a == L2 - 1)
                    ins.then_inc(hid_done.sem, hid_done.up())

                def cmp_out():
                    for r in range(2):
                        pe.wait_ge(hid_ready.sem, hid_ready.at(l, r + 1))
                        for s in range(2):
                            hs = hid[:, r, NC * s:NC * s + NC]
                            if r == 0:
                                ins = mm(bO[HD * s:HD * s + HD, 0:NC], w2[:, 0, :], hs, True, True)
                            else:
                                for t in range(NT):
                                    row = 32 * (2 * s + t)
                                    ins = nc.tensor.matmul(bB[row:row + NC, 64:64 + HD], hs, w2[:, 1, :], start=True,
                                                           stop=True, skip_group_check=True, tile_position=(0, row))
                        ins.then_inc(kc_done.sem, kc_done.up())

                def cmp_scores():
                    pe.wait_ge(kc_ready.sem, kc_ready.at(l, 1))
                    for n in range(NSA):
                        i, s, t, _ = nsa_unit(n)
                        c = 16 * (NT * i + t)
                        ins = mm((bA, bO)[s][:, c:c + NC], qr[HD * s:HD * s + HD, i, P * t:P * t + P],
                                 kc[HD * s:HD * s + HD, 0:NC], True, True)
                    ins.then_inc(cs_done.sem, cs_done.up())

                def s5_operands():
                    for r in range(2):
                        pe.wait_ge(bx_ready.sem, bx_ready.at(l, r + 1))
                        for j in range(JC):
                            ins = nc.tensor.transpose(bX[r][:, P * j:P * j + P],
                                                      bx[:, r, 4 * j:4 * j + 4, :].rearrange("p a b -> p (a b)"), ident)
                        ins.then_inc(bc_turned.sem, bc_turned.up())
                    for r in range(2):
                        pe.wait_ge(cx_ready.sem, cx_ready.at(l, r + 1))
                        if r == 1:
                            pe.wait_ge(bc_ready.sem, bc_ready.at(l, 1))
                        for j in range(JC):
                            ins = nc.tensor.transpose((bY, bX[0])[r][:, P * j:P * j + P], cx[:, r, j, :], ident)
                        ins.then_inc(bc_turned.sem, bc_turned.up())
                    params_free.made += 1
                    pe.sem_inc(params_free.sem, 1)

                def nsa_scores(n):
                    i, s, t, w = nsa_unit(n)
                    if n == 0:
                        pe.wait_ge(cs_ready.sem, cs_ready.at(l, 1))
                    else:
                        pe.wait_ge(s_max.sem, s_max.at(l, n))
                    mm(bA[:, 0:2 * w], qr[HD * s:HD * s + HD, i, P * t:P * t + P],
                       kr[HD * s:HD * s + HD, 1:3, 0:w], True, True).then_inc(s_done.sem, s_done.up())

                def nsa_turn(n):
                    i, s, t, w = nsa_unit(n)
                    pe.wait_ge(s_prob.sem, s_prob.at(l, n + 1))
                    if n == 0:
                        pe.wait_ge(cp_ready.sem, cp_ready.at(l, 1))
                        pe.wait_ge(kc_ready.sem, kc_ready.at(l, 2))
                        for i in range(4):
                            ins = nc.tensor.transpose(bO[:, P * i:P * i + P],
                                                      cE[:, 4 * i:4 * i + 4, :].rearrange("p a b -> p (a b)"), ident)
                        ins.then_inc(pc_done.sem, pc_done.up())
                    else:
                        pe.wait_ge(t_ready.sem, t_ready.at(l, n))
                    for b in range(2):
                        for k in range(t + 1):
                            c = P * (b * (t + 1) + k)
                            ins = nc.tensor.transpose(bB[:, c:c + P], pr[:, n % 2, c:c + P], ident)
                    ins.then_inc(t_done.sem, t_done.up())

                def nsa_values(n):
                    i, s, t, w = nsa_unit(n)
                    pe.wait_ge(t_ready.sem, t_ready.at(l, n + 1))
                    if n % 4 == 0 and n:
                        pe.wait_ge(on_ready.sem, on_ready.at(l, n // 4))
                    if n == 0:
                        pe.wait_ge(pc_ready.sem, pc_ready.at(l, 1))
                    else:
                        pe.wait_ge(v_done.sem, v_done.at(l, n))
                    o = bO[HD * s:HD * s + HD, P * t:P * t + P]
                    row = 32 * (2 * s + t)
                    nc.tensor.matmul(o, vc[row:row + NC, :], pcT[row:row + NC, i, :], start=True, stop=False,
                                     skip_group_check=True, tile_position=(row, HD * s))
                    for b in range(2):
                        for k in range(t + 1):
                            c = P * (b * (t + 1) + k)
                            ins = mm(o, vn[:, k, b, HD * s:HD * s + HD], pT[:, n % 2, c:c + P],
                                     False, b == 1 and k == t)
                    ins.then_inc(v_done.sem, v_done.up())

                def sb_scores(h):
                    i, s = h // 2, HD * (h % 2)
                    if h == 0:
                        for f in (4, 5):
                            n = U_FILL + f
                            pe.wait_ge(unit_out[n % 2].sem, unit_out[n % 2].at(l, n // 2 + 1))
                        pe.wait_ge(s_max.sem, s_max.at(l, NSA))
                        pe.wait_ge(t_ready.sem, t_ready.at(l, NSA))
                    elif h > 1:
                        pe.wait_ge(w_exp.sem, w_exp.at(l, h - 1))
                    z = (bA, bB)[h % 2]
                    mm(z[:, 0:T], sbk[s:s + HD, i, 0:P], sbq[s:s + HD, i, :], True, False)
                    mm(z[:, T:T + P], sbk[s:s + HD, i, P:T], sbq[s:s + HD, i, P:T], False, False)\
                        .then_inc(z_done.sem, z_done.up())

                def sb_rest(h):
                    pe.wait_ge(z_spm.sem, z_spm.at(l, h + 1))
                    z, p = (bA, bB)[h % 2], sbp[:, h % 2, :]
                    tri, neg1 = kon[:, K_TRI:K_TRI + P], kon[:, K_NEG1:K_NEG1 + P]
                    mm(z[:, 0:T], tri, p[:, 0:T], False, False)
                    mm(z[:, P:T], neg1, p[:, T:T + P], False, False)
                    mm(z[:, T:T + P], tri, p[:, T:T + P], False, True).then_inc(r_done.sem, r_done.up())

                def sb_values(h):
                    pe.wait_ge(w_ready.sem, w_ready.at(l, h + 1))
                    if h == 0:
                        pe.wait_ge(on_ready.sem, on_ready.at(l, 4))
                    elif h % 2 == 0:
                        pe.wait_ge(ob_ready.sem, ob_ready.at(l, h // 2))
                    o = bO[HD * (h % 2):HD * (h % 2) + HD, 0:T]
                    w = sbw[:, h % 3, :]
                    mm(o, sbv[:, 0, HD * h:HD * h + HD], w[:, 0:T], True, False)
                    mm(o[:, P:T], sbv[:, 1, HD * h:HD * h + HD], w[:, T:T + P], False, True)\
                        .then_inc(o_done.sem, o_done.up())

                def s5_inputs(s):
                    b, j, r = bX[s % 2], s // 4, 32 * (s % 4)
                    if s == 0:
                        pe.wait_ge(unit_out[0].sem, unit_out[0].at(l, 4))
                        pe.wait_ge(unit_out[1].sem, unit_out[1].at(l, 4))
                        pe.wait_ge(bc_ready.sem, bc_ready.at(l, 4))
                    elif s > 1:
                        pe.wait_ge(x5_used.sem, x5_used.at(l, s - 1))
                    for c in range(2):
                        ins = nc.tensor.matmul(b[:, T * c:T * c + T], BL[r:r + 32, c, j, :], uT[r:r + 32, j, :],
                                               start=True, stop=True, skip_group_check=True, tile_position=(r, 0))
                    ins.then_inc(x5_done.sem, x5_done.up())

                def s5_outputs(s):
                    j, r = s // 4, 32 * (s % 4)
                    pe.wait_ge(h5_ready.sem, h5_ready.at(l, s + 1))
                    if s % 4 == 0 and j:
                        pe.wait_ge(y_used.sem, y_used.at(l, j))
                    for c in range(2):
                        ins = nc.tensor.matmul(bY[r:r + 32, 0:T], CL[:, c, j, r:r + 32],
                                               s5h[:, s % 2, c, :], start=c == 0, stop=c == 1,
                                               skip_group_check=True, tile_position=(0, r))
                    ins.then_inc(y_done.sem, y_done.up())

                for q in range(SLOTS):
                    filler(q // 2, q % 2)
                    if q in CMP_HID:
                        cmp_hidden(CMP_HID[q])
                    if q == CMP_OUT:
                        cmp_out()
                    if q == CMP_S:
                        cmp_scores()
                        s5_operands()
                    if q in S5_X:
                        s5_inputs(S5_X[q])
                    if q in NSA_S:
                        nsa_scores(NSA_S[q])
                    if q in NSA_T:
                        nsa_turn(NSA_T[q])
                    if q in NSA_V:
                        nsa_values(NSA_V[q])
                    if q in SB_Z:
                        sb_scores(SB_Z[q])
                    if q in SB_R:
                        sb_rest(SB_R[q])
                    if q in SB_O:
                        sb_values(SB_O[q])
                    if q in S5_Y:
                        s5_outputs(S5_Y[q])

                pe.wait_ge(landed[I_GLU % RING].sem, chunk_at(l, I_GLU))
                w = slot_of(I_GLU).rearrange("p (k n) -> p k n", k=JC)
                pe.wait_ge(y_ready.sem, y_ready.at(l, 1))
                for n in range(2):
                    u = U_GLU + n
                    pe.wait_ge(unit_out[u % 2].sem, unit_out[u % 2].at(l, u // 2))
                    tiles(U_GLU + n, lambda m, k: w[:, k, P * (2 * n + m):P * (2 * n + m) + P],
                          lambda k: yT[:, k, :], JC)
                pe.wait_ge(os_ready.sem, os_ready.at(l, 2))
                for q in range(4):
                    i = I_GLU + 1 + q // 2
                    pe.wait_ge(landed[i % RING].sem, chunk_at(l, i))
                    u = U_Y + q
                    pe.wait_ge(unit_out[u % 2].sem, unit_out[u % 2].at(l, u // 2))
                    w = slot_of(i).rearrange("p (k n) -> p k n", k=JC)
                    c = 2 * P * (q % 2)
                    tiles(U_Y + q, lambda m, k: w[:, k, c + P * m:c + P * m + P], lambda k: oS[:, k, :], JC)
                pe.wait_ge(m_ready.sem, m_ready.at(l, 8))
                for q in range(4):
                    pe.wait_ge(landed[(I_OUT + q) % RING].sem, chunk_at(l, I_OUT + q))
                    u = U_OUT + q
                    pe.wait_ge(unit_out[u % 2].sem, unit_out[u % 2].at(l, u // 2))
                    w = slot_of(I_OUT + q).rearrange("p (k n) -> p k n", k=KD)
                    tiles(U_OUT + q, lambda m, k: w[:, k, P * m:P * m + P], lambda k: mT[:, k, :], KD)

                sum_squares(l, 4).then_inc(ss_done.sem, ss_done.up())

                def up(s, n, turn=0, times=1):
                    pe.wait_ge(unit_out[n % 2].sem, unit_out[n % 2].at(l, n // 2) + turn * 2)
                    for m in range(2):
                        piece(l, s + m, pj[n % 2][:, T * m:T * m + T], turn * TURN)\
                            .then_inc(w_used.sem, 1)
                        w_used.made += times

                def dn(s, c, turn=0, times=1):
                    pe.wait_ge(a_split.sem, a_split.at(l, c + 1) + turn * 2)
                    for k in range(2):
                        pe.wait_ge(w_lo.sem, w_lo.at(l, s + k + 1) + turn * TURN)
                        hi, lo = wh[:, (s + k) % SPLIT, :], wl[:, (s + k) % SPLIT, :]
                        xh, xl = ah[:, T * k:T * k + T], al[:, T * k:T * k + T]
                        for m in range(KD):
                            o = down[m // 2][:, T * (m % 2):T * (m % 2) + T]
                            c8 = slice(P * m, P * m + P)
                            mm(o, hi[:, c8], xh, times == 1 and c == 0 and k == 0 and m % 2 == 0, False)
                            mm(o, hi[:, c8], xl, False, False)
                            ins = mm(o, lo[:, c8], xh, False, False)
                        ins.then_inc(w_used.sem, 1)
                        w_used.made += times

                def ffn_step(cc, turn=0, times=1):
                    up(ffn_piece(cc), U_FFN + 2 * cc, turn, times)
                    up(ffn_piece(cc, 1), U_FFN + 2 * cc + 1, turn, times)
                    if cc:
                        dn(ffn_piece(cc, 2), cc - 1, turn, times)

                ffn_step(0)
                ffn_step(1)
                with pe.Fori(0, LOOP) as j:
                    ffn_step(2, j, LOOP)
                    ffn_step(3, j, LOOP)
                ffn_step(STEPS - 1)
                s = len(PIECES) - 2
                pe.wait_ge(a_split.sem, a_split.at(l, STEPS))
                pe.wait_ge(w_lo.sem, w_lo.at(l, s + 2))
                for m in range(KD):
                    o = down[m // 2][:, T * (m % 2):T * (m % 2) + T]
                    for k in range(2):
                        hi, lo = (w[:, (s + k) % SPLIT, P * m:P * m + P] for w in (wh, wl))
                        xh, xl = ah[:, T * k:T * k + T], al[:, T * k:T * k + T]
                        mm(o, hi, xh, False, False)
                        mm(o, hi, xl, False, False)
                        ins = mm(o, lo, xh, False, k == 1)
                    if m % 2:
                        ins.then_inc(down_done.sem, down_done.up())
                pe.wait_ge(down_done.sem, down_done.at(l, 4))
                pe.sem_inc(w_used.sem, w_used.up(2))

            sum_squares(DEPTH, 0).then_inc(ss_done.sem, 1)
            pe.wait_ge(h_new.sem, h_new.at(DEPTH, KD))
            for b, o in enumerate(down):
                for e in range(4):
                    t, k = b // 2, 4 * (b % 2) + e
                    ins = nc.tensor.transpose(o[:, P * e:P * e + P], hT[:, k, P * t:P * t + P], ident)
                ins.then_inc(fin_turned.sem, 1)

        @block.scalar
        def _(a):
            A = nc.scalar.activation

            def squares(l, first, x_first):
                for b in range(4):
                    a.wait_ge(x_ready.sem, x_ready.at(l, x_first + b + 1))
                    A(sq[:, 2 * b:2 * b + 2, :], xT[:, 2 * b:2 * b + 2, :], ACT.Square)\
                        .then_inc(sq_ready.sem, sq_ready.up())

            def root(l, n):
                a.wait_ge(ss_done.sem, ss_done.at(l, n))
                A(rstd[:, :], bO[:, 0:T], ACT.Sqrt, bias=kon[:, K_EPS:K_EPS + 1], scale=-1.0 / D)\
                    .then_inc(rms_ready.sem, rms_ready.up())

            def load_root():
                A(eps2[:, :], kon[:, K_EPS:K_EPS + 1], ACT.Sqrt)

            def copy_out(l, n, dst, func=ACT.Copy, scale=1.0):
                t, k = summed(n)
                a.wait_ge(t.sem, t.at(l, k))
                A(dst, unit(n), func, scale=scale).then_inc(unit_out[n % 2].sem, unit_out[n % 2].up())

            def split_hi(l, s, turn=0, times=1):
                i = PIECES[s][0]
                a.wait_ge(landed[i % RING].sem, chunk_at(l, i) + turn * 32)
                if kind_of(i) == "q":
                    a.wait_ge(q_in[i].sem, q_in[i].at(l, 48))
                if kind_of(i) == "pair":
                    a.wait_ge(pair_in.sem, pair_in.at(l, 48))
                a.wait_ge(w_used.sem, w_used.at(l, s + 1 - SPLIT) + turn * TURN)
                src, dst = piece_from(s, wh)
                A(dst, src, ACT.Copy).then_inc(w_hi.sem, 1)
                w_hi.made += times

            def norm_hi(l, first):
                for k in range(KD):
                    a.wait_ge(h_new.sem, h_new.at(l, first + k + 1))
                    A(hh[:, k, :], hT[:, k, :], ACT.Copy).then_inc(h_hi.sem, h_hi.up())

            a.wait_ge(consts_in.sem, 16)
            a.wait_ge(x_turned.sem, 4)
            with a.Fori(0, DEPTH) as l:
                load_root()
                squares(l, 0, -4)
                a.wait_ge(par_turned.sem, par_turned.at(l, 3))
                for n in range(3):
                    A(par[:, n, :], bX[0][:, P * n:P * n + P], ACT.Copy).then_inc(par_ready.sem, par_ready.up())
                for s in range(SPLIT):
                    split_hi(l, s)
                root(l, 1)
                norm_hi(l, 0)
                a.wait_ge(par_ready.sem, par_ready.at(l, 3))
                A(s5p[:, 0, :], par[:, 0, A_ST:A_ST + ST], ACT.Exp).then_inc(step_exp.sem, step_exp.up())
                a.wait_ge(ang_ready.sem, ang_ready.at(l, 1))
                A(s5p[:, 3, :], s5p[:, 1, :], ACT.Exp).then_inc(mag_ready.sem, mag_ready.up())
                split_hi(l, 3)
                split_hi(l, 4)
                a.wait_ge(ang_ready.sem, ang_ready.at(l, 2))
                A(s5p[:, 4, :], s5p[:, 8, :], ACT.Sin)
                A(s5p[:, 5, :], s5p[:, 8, :], ACT.Sin, scale=0.5).then_inc(sin_ready.sem, sin_ready.up())
                for n, dst in enumerate((qr[:, 0:2, :], qr[:, 2:4, :], kr[:, 0:2, :], kr[:, 2:4, :],
                                         vn[:, :, :, :].rearrange("p t b c -> p t (b c)"))):
                    copy_out(l, n, dst)
                    split_hi(l, 5 + 2 * n)
                    if n < 4:
                        split_hi(l, 6 + 2 * n)
                t, k = summed(5)
                a.wait_ge(t.sem, t.at(l, k))
                A(ng[:, :, :], pj[1][:, 0:NT * 3 * HEADS].rearrange("p (t c) -> p t c", t=NT), ACT.Tanh, scale=0.5)\
                    .then_inc(unit_out[1].sem, unit_out[1].up())
                split_hi(l, 14)
                copy_out(l, 6, uT[:, 0:2, :])
                split_hi(l, 15)
                split_hi(l, 16)
                copy_out(l, 7, uT[:, 2:4, :])
                split_hi(l, 17)
                for q in range(SLOTS):
                    f = q // 2
                    if 1 <= q and S_FILL + 2 + q < S_FFN:
                        split_hi(l, S_FILL + 2 + q)
                    if q in CMP_HID:
                        r = CMP_HID[q]
                        a.wait_ge(hid_done.sem, hid_done.at(l, r + 1))
                        A(hid[:, r, 0:2 * NC], (bA, bB)[r][:, 0:2 * NC], ACT.Gelu_apprx_tanh)\
                            .then_inc(hid_ready.sem, hid_ready.up())
                    if q == CMP_OUT:
                        a.wait_ge(kc_done.sem, kc_done.at(l, 1))
                        A(kc[:, 0:NC], bO[:, 0:NC], ACT.Copy).then_inc(kc_ready.sem, kc_ready.up())
                        a.wait_ge(kc_done.sem, kc_done.at(l, 2))
                        for r in range(0, P, 32):
                            ins = A(vc[r:r + NC, :], bB[r:r + NC, 64:64 + HD], ACT.Copy)
                        ins.then_inc(kc_ready.sem, kc_ready.up())
                    if q == CMP_S:
                        for n in range(4):
                            a.wait_ge(bc_turned.sem, bc_turned.at(l, n + 1))
                            src = (bX[0], bX[1], bY, bX[0])[n]
                            dst = (BL[:, 0], BL[:, 1], CL[:, 0], CL[:, 1])[n]
                            A(dst, src[:, :].rearrange("p (j c) -> p j c", j=JC), ACT.Copy)\
                                .then_inc(bc_ready.sem, bc_ready.up())
                    if q == CMP_S + 1:
                        a.wait_ge(cs_ready.sem, cs_ready.at(l, 1))
                        A(cP, cS, ACT.Exp, scale=SCALE).then_inc(ce_ready.sem, ce_ready.up())
                    if q in NSA_S:
                        n = NSA_S[q]
                        w = nsa_unit(n)[3]
                        a.wait_ge(s_max.sem, s_max.at(l, n + 1))
                        if n >= 2:
                            a.wait_ge(t_done.sem, t_done.at(l, n - 1))
                        for b in range(2):
                            ins = A(pr[:, n % 2, w * b:w * b + w], sc[:, n % 2, w * b:w * b + w], ACT.Exp,
                                    bias=nm[:, n % 2, b:b + 1], scale=SCALE, accum_out=sm[:, n % 2, b:b + 1])
                        ins.then_inc(s_exp.sem, s_exp.up())
                    if q in NSA_T:
                        n = NSA_T[q]
                        w = nsa_unit(n)[3]
                        a.wait_ge(t_done.sem, t_done.at(l, n + 1))
                        if n >= 2:
                            a.wait_ge(v_done.sem, v_done.at(l, n - 1))
                        A(pT[:, n % 2, 0:2 * w], bB[:, 0:2 * w], ACT.Copy).then_inc(t_ready.sem, t_ready.up())
                        if n == 0:
                            a.wait_ge(pc_done.sem, pc_done.at(l, 1))
                            A(pcT[:, :, :], bO[:, :].rearrange("p (i t) -> p i t", i=4), ACT.Copy)\
                                .then_inc(pc_ready.sem, pc_ready.up())
                    if q in SB_R:
                        h = SB_R[q]
                        a.wait_ge(r_done.sem, r_done.at(l, h + 1))
                        A(sbw[:, h % 3, :], (bA, bB)[h % 2][:, 0:384], ACT.Exp).then_inc(w_exp.sem, w_exp.up())
                    if q in SB_Z:
                        h = SB_Z[q]
                        a.wait_ge(z_done.sem, z_done.at(l, h + 1))
                        if h >= 3:
                            a.wait_ge(o_done.sem, o_done.at(l, h - 2))
                        A(sbw[:, h % 3, :], (bA, bB)[h % 2][:, 0:384], ACT.Abs).then_inc(z_abs.sem, z_abs.up())
                        a.wait_ge(z_abs.sem, z_abs.at(l, h + 1))
                        A(sbw[:, h % 3, :], sbw[:, h % 3, :], ACT.Exp, scale=-1.0).then_inc(z_exp.sem, z_exp.up())
                        a.wait_ge(z_exp.sem, z_exp.at(l, h + 1))
                        A(sbw[:, h % 3, :], sbw[:, h % 3, :], ACT.Ln, bias=1.0).then_inc(z_ln.sem, z_ln.up())
                    if q % 2:
                        kind, *at = FILL[f]
                        if kind == "sbq":
                            copy_out(l, U_FILL + f, sbq[:, 2 * at[0]:2 * at[0] + 2, :], scale=SCALE)
                        elif kind == "gate":
                            b, i = at
                            copy_out(l, U_FILL + f, gate[:, KD * b + 2 * i:KD * b + 2 * i + 2, :], ACT.Tanh, 0.5)
                a.wait_ge(y_used.sem, y_used.at(l, JC))
                A(yT[:, :, :], yT[:, :, :], ACT.Gelu_apprx_tanh).then_inc(y_ready.sem, y_ready.up())
                for n in range(2):
                    copy_out(l, U_GLU + n, oS[:, 2 * n:2 * n + 2, :], ACT.Tanh, 0.5)
                load_root()
                squares(l, 4, 0)
                split_hi(l, S_FFN)
                split_hi(l, S_FFN + 1)
                root(l, 2)
                norm_hi(l, KD)
                split_hi(l, S_FFN + 2)

                def conv(n, e, tile, turn=0, times=1):
                    t, k = summed(n)
                    a.wait_ge(t.sem, t.at(l, k) + turn * TURN)
                    for m in range(2):
                        ins = A(cv[:, e, T * m:T * m + T], pj[n % 2][:, T * m:T * m + T], ACT.Identity,
                                bias=par[:, 2, bass.ds(tile + (C_B + m), 1)],
                                scale=par[:, 2, bass.ds(tile + (C_W2 + m), 1)])
                    ins.then_inc(cv_last.sem, 1)
                    cv_last.made += times

                def ffn_step(c, cc, turn=0, times=1):
                    s = ffn_piece(cc)
                    split_hi(l, s + 3, turn, times)
                    if cc:
                        split_hi(l, s + 4, turn, times)
                        a.wait_ge(a_ready.sem, a_ready.at(l, cc) + turn * 2)
                    conv(U_FFN + 2 * cc, 0, c * 2, turn, times)
                    if cc:
                        split_hi(l, s + 5, turn, times)
                    split_hi(l, s + (6 if cc else 4), turn, times)
                    conv(U_FFN + 2 * cc + 1, 1, c * 2 + FT, turn, times)
                    n = U_FFN + 2 * cc
                    a.wait_ge(unit_out[n % 2].sem, unit_out[n % 2].at(l, n // 2 + 1) + turn * 2)
                    A(cv[:, 0, :], cv[:, 0, :], ACT.Silu).then_inc(sg_ready.sem, 1)
                    sg_ready.made += times
                    split_hi(l, s + (7 if cc else 5), turn, times)
                    if s + 8 < len(PIECES):
                        split_hi(l, s + (8 if cc else 6), turn, times)
                    a.wait_ge(a_ready.sem, a_ready.at(l, cc + 1) + turn * 2)
                    if cc:
                        a.wait_ge(w_used.sem, w_used.at(l, s + 6) + turn * TURN)
                    A(ah[:, :], aT[:, cc % 2, :], ACT.Copy).then_inc(a_hi.sem, 1)
                    a_hi.made += times

                ffn_step(0, 0)
                ffn_step(1, 1)
                with a.Fori(0, LOOP) as j:
                    ffn_step(j * 2 + 2, 2, j, LOOP)
                    ffn_step(j * 2 + 3, 3, j, LOOP)
                ffn_step(STEPS - 1, STEPS - 1)
            load_root()
            squares(DEPTH, 0, -4)
            sq_ready.made -= 4
            root(DEPTH, 1)
            rms_ready.made -= 1

        @block.vector
        def _(v):
            TT, TS, STT = nc.vector.tensor_tensor, nc.vector.tensor_scalar, nc.vector.scalar_tensor_tensor

            nc.vector.memset(cE[:, :, :], 0.0)
            for st in (stA, stB, stC):
                nc.vector.memset(st[:, :], 0.0).then_inc(setup.sem, 1)
            v.sem_inc(w_lo.sem, w_lo.start)
            v.sem_inc(w_used.sem, w_used.start)
            v.sem_inc(params_free.sem, 1)
            v.sem_inc(unit_out[0].sem, 1)
            v.sem_inc(unit_out[1].sem, 1)
            v.sem_inc(a_split.sem, a_split.start)
            for b, o in enumerate(down):
                v.wait_ge(x_turned.sem, b + 1)
                nc.vector.tensor_copy(xT[:, 2 * b:2 * b + 2, :], o[:, :].rearrange("p (k t) -> p k t", k=2))\
                    .then_inc(x_ready.sem, 1)

            def split_lo(l, s, turn=0, times=1):
                v.wait_ge(w_hi.sem, w_hi.at(l, s + 1) + turn * TURN)
                src, dst = piece_from(s, wl)
                hi = piece_from(s, wh)[1]
                TT(dst, src, hi.bitcast(F32), ALU.subtract).then_inc(w_lo.sem, 1)
                w_lo.made += times

            def norm(l, n, gain, split=True):
                v.wait_ge(rms_ready.sem, rms_ready.at(l, n))
                nc.vector.reciprocal(rstd[:, :], rstd[:, :]).then_inc(dve_step.sem, dve_step.up())
                v.wait_ge(dve_step.sem, dve_step.last(l))

                def lo(k):
                    v.wait_ge(h_hi.sem, h_hi.at(l, KD * (n - 1) + k + 1))
                    TT(hl[:, k, :], hT[:, k, :], hh[:, k, :].bitcast(F32), ALU.subtract)\
                        .then_inc(h_ready.sem, h_ready.up())

                for k in range(KD):
                    STT(hT[:, k, :], xT[:, k, :], par[:, 0, gain + k:gain + k + 1], rstd[:, :], ALU.mult, ALU.mult)\
                        .then_inc(h_new.sem, h_new.up())
                    if split and k:
                        lo(k - 1)
                if split:
                    lo(KD - 1)

            def gate_unit(b, i):
                return U_FILL + FILL.index(("gate", b, i))

            def merge(l, n, b, q):
                u = gate_unit(b, q)
                v.wait_ge(unit_out[u % 2].sem, unit_out[u % 2].at(l, u // 2 + 1))
                t, k = summed(n)
                v.wait_ge(t.sem, t.at(l, k))
                if b == 1:
                    dst = mT[:, 2 * q:2 * q + 2, :]
                else:
                    k = q if b == 2 else 4 + q
                    if k >= 2:
                        v.wait_ge(m_ready.sem, m_ready.at(l, k - 1))
                    dst = yt[:, k % 2, :].rearrange("p (m t) -> p m t", m=2)
                STT(dst, gate[:, KD * b + 2 * q:KD * b + 2 * q + 2, :], 1.0, unit(n),
                    ALU.add, ALU.mult).then_inc(unit_out[n % 2].sem, unit_out[n % 2].up())

            with v.Fori(0, DEPTH) as l:
                v.wait_ge(rows_in.sem, rows_in.at(l, 16 * 17))
                nc.vector.tensor_copy(
     stA[A_ST:A_ST + ST, :].rearrange("t (w p) -> t w p", w=2),
     lstep[A_ST:A_ST + ST, :].rearrange("t (w o) -> t w o", o=1).broadcast_to([ST, 2, HD]))\
         .then_inc(step_row.sem, step_row.up())
                v.wait_ge(par_ready.sem, par_ready.at(l, 1))
                for s in range(SPLIT):
                    split_lo(l, s)
                norm(l, 1, A_MIX)

                def p(n):
                    return s5p[:, n, :]

                lr, li = par[:, 0, A_LR:A_LR + ST], par[:, 0, A_LI:A_LI + ST]
                step, lrs, th, mag, sn, sh, kk, t1, r, cs, ar, ai, den, rden, nr, fr, fi, t2 = map(p, range(18))
                v.wait_ge(step_exp.sem, step_exp.at(l, 1))
                TT(lrs, lr, step, ALU.mult)
                TT(th, li, step, ALU.mult).then_inc(ang_ready.sem, ang_ready.up())
                v.wait_ge(ang_ready.sem, ang_ready.at(l, 1))
                TS(kk, th, 1.0 / TWO_PI, MAGIC, ALU.mult, ALU.add).then_inc(dve_step.sem, dve_step.up())
                v.wait_ge(dve_step.sem, dve_step.last(l))
                TS(kk, kk, -MAGIC, None, ALU.add).then_inc(dve_step.sem, dve_step.up())
                v.wait_ge(dve_step.sem, dve_step.last(l))
                src = th
                for part in PI_PARTS:
                    STT(r, kk, -part, src, ALU.mult, ALU.add).then_inc(dve_step.sem, dve_step.up())
                    v.wait_ge(dve_step.sem, dve_step.last(l))
                    src = r
                TS(r, r, 3.1415925, -3.1415925, ALU.min, ALU.max).then_inc(ang_ready.sem, ang_ready.up())
                split_lo(l, 3)
                split_lo(l, 4)
                v.wait_ge(sin_ready.sem, sin_ready.at(l, 1))
                v.wait_ge(mag_ready.sem, mag_ready.at(l, 1))
                TT(cs, sh, sh, ALU.mult).then_inc(dve_step.sem, dve_step.up())
                v.wait_ge(dve_step.sem, dve_step.last(l))
                TS(cs, cs, -2.0, 1.0, ALU.mult, ALU.add).then_inc(dve_step.sem, dve_step.up())
                v.wait_ge(dve_step.sem, dve_step.last(l))
                TT(ar, mag, cs, ALU.mult)
                TT(ai, mag, sn, ALU.mult)
                TT(den, lr, lr, ALU.mult)
                TT(t1, li, li, ALU.mult).then_inc(dve_step.sem, dve_step.up())
                v.wait_ge(dve_step.sem, dve_step.last(l))
                TS(nr, ar, -1.0, None, ALU.add)
                TT(den, den, t1, ALU.add).then_inc(dve_step.sem, dve_step.up())
                v.wait_ge(dve_step.sem, dve_step.last(l))
                TT(t1, nr, lr, ALU.mult)
                TT(t2, ai, li, ALU.mult)
                nc.vector.reciprocal(rden, den).then_inc(dve_step.sem, dve_step.up())
                v.wait_ge(dve_step.sem, dve_step.last(l))
                TT(fr, t1, t2, ALU.add).then_inc(dve_step.sem, dve_step.up())
                v.wait_ge(dve_step.sem, dve_step.last(l))
                TT(fr, fr, rden, ALU.mult).then_inc(dve_step.sem, dve_step.up())
                v.wait_ge(dve_step.sem, dve_step.last(l))
                TT(t1, ai, lr, ALU.mult)
                TT(t2, nr, li, ALU.mult).then_inc(dve_step.sem, dve_step.up())
                v.wait_ge(dve_step.sem, dve_step.last(l))
                TT(fi, t1, t2, ALU.subtract).then_inc(dve_step.sem, dve_step.up())
                v.wait_ge(dve_step.sem, dve_step.last(l))
                TT(fi, fi, rden, ALU.mult).then_inc(dve_step.sem, dve_step.up())
                v.wait_ge(dve_step.sem, dve_step.last(l))
                TC, TN = tab[:, 0], tab[:, 1]
                nc.vector.tensor_copy(TC[:, :, 0], cs)
                nc.vector.tensor_copy(TN[:, :, 0], sn).then_inc(tab_d.sem, tab_d.up())
                v.wait_ge(tab_d.sem, tab_d.at(l, 1))

                v.wait_ge(mats_in.sem, mats_in.at(l, 16 * 6))

                def w3(ap):
                    return ap.rearrange("p (t o) -> p t o", o=1).broadcast_to([P, ST, GCH])

                def w3r(ap):
                    return w3(ap)

                TT(bb[:, 0], bnat[:, 0], w3(fr), ALU.mult)
                TT(bbt[:, 0], bnat[:, 1], w3(fi), ALU.mult)
                TT(bb[:, 1], bnat[:, 1], w3(fr), ALU.mult)
                TT(bbt[:, 1], bnat[:, 0], w3(fi), ALU.mult).then_inc(dve_step.sem, dve_step.up())
                v.wait_ge(dve_step.sem, dve_step.last(l))
                split_lo(l, 5)
                TT(bb[:, 0], bb[:, 0], bbt[:, 0], ALU.subtract)
                TT(bb[:, 1], bb[:, 1], bbt[:, 1], ALU.add).then_inc(dve_step.sem, dve_step.up())
                v.wait_ge(dve_step.sem, dve_step.last(l))
                v.wait_ge(bx_clear.sem, bx_clear.at(l, 1))
                for c in range(2):
                    nc.vector.tensor_copy(bx[0:STATES, c, :, 0:GCH], bb[0:STATES, c])
                    nc.vector.tensor_copy(bx[STATES:P, c, :, GCH:2 * GCH], bb[STATES:P, c])\
                        .then_inc(bx_ready.sem, bx_ready.up())
                split_lo(l, 6)
                split_lo(l, 7)
                for e in range(7):
                    n = 1 << e
                    if e:
                        v.wait_ge(tab_p.sem, tab_p.at(l, e))
                    cn = TC[:, :, n - 1:n].broadcast_to([P, ST, n])
                    nn = TN[:, :, n - 1:n].broadcast_to([P, ST, n])
                    TT(TC[:, :, n:2 * n], TC[:, :, 0:n], cn, ALU.mult)
                    TT(tmp_d[:, :, 0:n], TN[:, :, 0:n], nn, ALU.mult).then_inc(dve_step.sem, dve_step.up())
                    v.wait_ge(dve_step.sem, dve_step.last(l))
                    TT(TC[:, :, n:2 * n], TC[:, :, n:2 * n], tmp_d[:, :, 0:n], ALU.subtract)\
                        .then_inc(tab_d.sem, tab_d.up())
                    if e in (1, 3, 4, 5, 6):
                        split_lo(l, {1: 8, 3: 9, 4: 10, 5: 11, 6: 12}[e])
                    v.wait_ge(tab_d.sem, tab_d.at(l, e + 2))

                split_lo(l, 13)
                sin_b = kon[:, K_SIN:K_SIN + T].rearrange("p (o t) -> p o t", o=1)
                for n, (o, dst) in enumerate(((bO, kr[:, 0:2, :]), (bX[1], kr[:, 2:3, :]),
                                              (bA, qr[:, 0:2, :]), (bB, qr[:, 2:4, :]))):
                    v.wait_ge(rot_done.sem, rot_done.at(l, n + 1))
                    if n:
                        v.wait_ge(rot_ready.sem, rot_ready.at(l, n))
                    m = dst.shape[1]
                    r2 = rt[:, 0:T * m].rearrange("p (m t) -> p m t", m=m)
                    TT(r2, o[:, 0:T * m].rearrange("p (m t) -> p m t", m=m), sin_b.broadcast_to([P, m, T]), ALU.mult)\
                        .then_inc(dve_step.sem, dve_step.up())
                    v.wait_ge(dve_step.sem, dve_step.last(l))
                    v.wait_ge(rot_cos.sem, rot_cos.at(l, n + 1))
                    TT(dst, dst, r2, ALU.add).then_inc(rot_ready.sem, rot_ready.up())
                    if n in (1, 3):
                        split_lo(l, 14 + n // 2)
                v.wait_ge(rot_ready.sem, rot_ready.at(l, 4))
                v.wait_ge(unit_out[1].sem, unit_out[1].at(l, 2))

                for c, (src, own, sw) in enumerate(((kr[:, 0, :], par[:, 0, A_PK:A_PK + L2], par[:, 0, A_PKS:A_PKS + L2]),
                                                    (kr[:, 3, :], par[:, 0, A_PV:A_PV + L2], par[:, 1, B_PVS:B_PVS + L2]))):
                    rows = src.rearrange("p (m w) -> p m w", w=CSTR)
                    for g in range(2):
                        for w in range(2):
                            pos = (own if g == w else sw)[HD * g:HD * g + HD, :]
                            for b in range(2):
                                h8 = L2 // 2
                                ins = TT(blk[HD * w:HD * w + HD, c, g, :, h8 * b:h8 * b + h8],
                                         rows[HD * g:HD * g + HD, b:b + NC, w::2],
                                         pos[:, h8 * b:h8 * b + h8].rearrange("p (o a) -> p o a", o=1)
                                         .broadcast_to([HD, NC, h8]), ALU.add)
                    ins.then_inc(blk_ready.sem, blk_ready.up())
                    split_lo(l, 16 + c)
                v.wait_ge(unit_out[1].sem, unit_out[1].at(l, 3))
                TS(ng[:, :, :], ng[:, :, :], 0.5, 0.5, ALU.mult, ALU.add).then_inc(dve_step.sem, dve_step.up())
                v.wait_ge(dve_step.sem, dve_step.last(l))

                def cmp_softmax():
                    v.wait_ge(cs_done.sem, cs_done.at(l, 1))

                    def per_key(n):
                        return cm[:, n, :].rearrange("p (n o) -> p n o", o=1).broadcast_to([P, NSA, NC])

                    cmask = kon[:, K_CMASK:K_CMASK + 16 * NT].rearrange("p (o t c) -> p o t c", o=1, t=NT)
                    for s in range(2):
                        raw = (bA, bO)[s][:, 0:8 * NSA].rearrange("p (i t c) -> p i t c", i=4, c=16)
                        ins = TT(cS.rearrange("p (i s t) c -> p i s t c", i=4, s=2)[:, :, s, :, :], raw[:, :, :, 0:NC],
                                 cmask[:, :, :, 0:NC].broadcast_to([P, 4, NT, NC]), ALU.add)
                    ins.then_inc(dve_step.sem, dve_step.up())
                    v.wait_ge(dve_step.sem, dve_step.last(l))
                    nc.vector.tensor_reduce(cm[:, 0, :], cS, AX, ALU.max).then_inc(dve_step.sem, dve_step.up())
                    v.wait_ge(dve_step.sem, dve_step.last(l))
                    TS(cm[:, 0, :], cm[:, 0, :], 0.1 * NEG, None, ALU.max).then_inc(dve_step.sem, dve_step.up())
                    v.wait_ge(dve_step.sem, dve_step.last(l))
                    TT(cS, cS, per_key(0), ALU.subtract).then_inc(cs_ready.sem, cs_ready.up())
                    v.wait_ge(ce_ready.sem, ce_ready.at(l, 1))
                    nc.vector.tensor_reduce(cm[:, 1, :], cP, AX, ALU.add).then_inc(dve_step.sem, dve_step.up())
                    v.wait_ge(dve_step.sem, dve_step.last(l))
                    TS(cm[:, 1, :], cm[:, 1, :], 1e-30, None, ALU.max).then_inc(dve_step.sem, dve_step.up())
                    v.wait_ge(dve_step.sem, dve_step.last(l))
                    nc.vector.reciprocal(cm[:, 1, :], cm[:, 1, :]).then_inc(dve_step.sem, dve_step.up())
                    v.wait_ge(dve_step.sem, dve_step.last(l))
                    g0 = ng[:, :, :].rearrange("p t (s i b) -> p i s t b", s=2, b=3)
                    TT(cm[:, 2, :].rearrange("p (i s t) -> p i s t", i=4, s=2),
                       cm[:, 1, :].rearrange("p (i s t) -> p i s t", i=4, s=2), g0[:, :, :, :, 0], ALU.mult)\
                           .then_inc(dve_step.sem, dve_step.up())
                    v.wait_ge(dve_step.sem, dve_step.last(l))
                    TT(cP, cP, per_key(2), ALU.mult).then_inc(cp_ready.sem, cp_ready.up())

                def nsa_max(n):
                    t, w = nsa_unit(n)[2:]
                    v.wait_ge(s_done.sem, s_done.at(l, n + 1))
                    if n >= 2:
                        v.wait_ge(s_exp.sem, s_exp.at(l, n - 1))
                    v.sem_inc(passed.sem, 1)
                    for b in range(2):
                        ins = nc.vector.tensor_tensor_reduce(
                            sc[:, n % 2, w * b:w * b + w], bA[:, w * b:w * b + w],
                            kon[:, K_MASK + T - w:K_MASK + T], 1.0, 3.0 * NEG, ALU.add, ALU.max,
                            mx[:, n % 2, b:b + 1])
                    ins.then_inc(dve_step.sem, dve_step.up())
                    v.wait_ge(dve_step.sem, dve_step.last(l))
                    TS(nm[:, n % 2, :], mx[:, n % 2, :], -SCALE, None, ALU.mult).then_inc(s_max.sem, s_max.up())

                def nsa_sum(n):
                    i, s, t, w = nsa_unit(n)
                    v.wait_ge(s_exp.sem, s_exp.at(l, n + 1))
                    if n >= 2:
                        v.wait_ge(s_prob.sem, s_prob.at(l, n - 1))
                    TS(rc[:, n % 2, :], sm[:, n % 2, :], 1e-30, None, ALU.max).then_inc(dve_step.sem, dve_step.up())
                    v.wait_ge(dve_step.sem, dve_step.last(l))
                    nc.vector.reciprocal(rc[:, n % 2, :], rc[:, n % 2, :]).then_inc(dve_step.sem, dve_step.up())
                    v.wait_ge(dve_step.sem, dve_step.last(l))
                    c = 3 * (4 * s + i) + 1
                    TT(rg[:, n % 2, :], rc[:, n % 2, :], ng[:, t, c:c + 2], ALU.mult).then_inc(s_rec.sem, s_rec.up())

                def halves(ap, m=4):
                    return ap.rearrange("p (m t) -> p m t", m=m)

                def s5_turn(s):
                    v.wait_ge(x5_done.sem, x5_done.at(l, s + 1))
                    if s:
                        v.wait_ge(h5_ready.sem, h5_ready.at(l, s))
                    for c in range(2):
                        ins = TT(halves(s5a[:, c, :]), halves(bX[s % 2][:, :]),
                                 tab[:, c, s:s + 1, :].broadcast_to([P, 4, P]), ALU.mult)
                    ins.then_inc(x5_used.sem, x5_used.up())

                def s5_scan(s):
                    v.wait_ge(x5_turned.sem, x5_turned.at(l, s + 1))
                    decay = mag[:, s:s + 1].broadcast_to([P, P])
                    cn, nn = tab[:, 0, s, P - 1:P], tab[:, 1, s, P - 1:P]
                    for b in range(2):
                        for c in range(2):
                            g = s5x[:, c, P * b:P * b + P]
                            ins = nc.vector.tensor_tensor_scan(g, decay, g, s5i[:, 2 + c:3 + c] if b else 0.0,
                                                               ALU.mult, ALU.add)
                        if b:
                            break
                        ins.then_inc(dve_step.sem, dve_step.up())
                        v.wait_ge(dve_step.sem, dve_step.last(l))
                        gr, gi = s5x[:, 0, P - 1:P], s5x[:, 1, P - 1:P]
                        TT(s5i[:, 0:1], gi, nn, ALU.mult)
                        TT(s5i[:, 1:2], gi, cn, ALU.mult).then_inc(dve_step.sem, dve_step.up())
                        v.wait_ge(dve_step.sem, dve_step.last(l))
                        STT(s5i[:, 2:3], gr, cn, s5i[:, 0:1], ALU.mult, ALU.subtract)
                        STT(s5i[:, 3:4], gr, nn, s5i[:, 1:2], ALU.mult, ALU.add).then_inc(dve_step.sem, dve_step.up())
                        v.wait_ge(dve_step.sem, dve_step.last(l))
                    ins.then_inc(g5_ready.sem, g5_ready.up())

                for q in range(SLOTS):
                    f = q // 2
                    if 1 <= q and S_FILL + 2 + q < S_FFN:
                        split_lo(l, S_FILL + 2 + q)
                    if q == CMP_S + 1:
                        cmp_softmax()
                    if q in NSA_S:
                        nsa_max(NSA_S[q])
                    if q - 1 in SB_Z:
                        h = SB_Z[q - 1]
                        v.wait_ge(z_ln.sem, z_ln.at(l, h + 1))
                        if h >= 2:
                            v.wait_ge(r_done.sem, r_done.at(l, h - 1))
                        STT(sbp[:, h % 2, :], (bA, bB)[h % 2][:, 0:384], 0.0, sbw[:, h % 3, :],
                            ALU.max, ALU.add).then_inc(z_sp.sem, z_sp.up())
                    if q in S5_X:
                        s5_turn(S5_X[q])
                    if q - 1 in S5_X:
                        s5_scan(S5_X[q - 1])
                    if q in NSA_S:
                        nsa_sum(NSA_S[q])
                    if q in NSA_V and NSA_V[q] % 4 == 3:
                        n = NSA_V[q]
                        v.wait_ge(v_done.sem, v_done.at(l, n + 1))
                        nc.vector.tensor_copy(oN[:, n // 4, :], bO[:, 0:T]).then_inc(on_ready.sem, on_ready.up())
                    if q in SB_O and SB_O[q] % 2:
                        h = SB_O[q]
                        v.wait_ge(o_done.sem, o_done.at(l, h + 1))
                        nc.vector.tensor_copy(oB[:, h // 2, :], bO[:, 0:T]).then_inc(ob_ready.sem, ob_ready.up())
                    if q in S5_Y and S5_Y[q] % 4 == 3:
                        j = S5_Y[q] // 4
                        v.wait_ge(y_done.sem, y_done.at(l, 4 * j + 4))
                        STT(yT[:, j, :], uT[:, j, :], par[:, 0, A_D + j:A_D + j + 1],
                            bY[:, 0:T], ALU.mult, ALU.add).then_inc(y_used.sem, y_used.up())
                    if q % 2:
                        kind, *at = FILL[f]
                        n = U_FILL + f
                        if kind in ("sbk", "sbv"):
                            t, k = summed(n)
                            v.wait_ge(t.sem, t.at(l, k))
                            dst = (sbk[:, 2 * at[0]:2 * at[0] + 2, :] if kind == "sbk"
                                   else sbv[:, :, T * at[0]:T * at[0] + T])
                            nc.vector.tensor_copy(dst, unit(n)).then_inc(unit_out[n % 2].sem, unit_out[n % 2].up())
                        elif kind == "y":
                            merge(l, n, *at)

                for n in range(2):
                    u = U_GLU + n
                    v.wait_ge(unit_out[u % 2].sem, unit_out[u % 2].at(l, u // 2 + 1))
                    o = oS[:, 2 * n:2 * n + 2, :]
                    TS(o, o, 0.5, 0.5, ALU.mult, ALU.add).then_inc(dve_step.sem, dve_step.up())
                    v.wait_ge(dve_step.sem, dve_step.last(l))
                    TT(o, o, yT[:, 2 * n:2 * n + 2, :], ALU.mult).then_inc(os_ready.sem, os_ready.up())
                for q in range(4):
                    merge(l, U_Y + q, 0, q)
                for q in range(4):
                    n = U_OUT + q
                    t, k = summed(n)
                    v.wait_ge(t.sem, t.at(l, k))
                    xq = xT[:, 2 * q:2 * q + 2, :]
                    STT(xq, unit(n), 0.5, xq, ALU.mult, ALU.add).then_inc(unit_out[n % 2].sem, unit_out[n % 2].up())
                    x_ready.made += 1
                    v.wait_ge(unit_out[n % 2].sem, unit_out[n % 2].at(l, n // 2 + 1))
                    v.sem_inc(x_ready.sem, 1)
                split_lo(l, S_FFN)
                split_lo(l, S_FFN + 1)
                norm(l, 2, A_FFN)
                split_lo(l, S_FFN + 2)

                def taps(n, e, tile, turn=0, times=1):
                    u = unit_out[n % 2]
                    v.wait_ge(cv_last.sem, cv_last.at(l, n - U_FFN + 1) + turn * 4)
                    for back, col in ((1, B_W1), (2, B_W0)):
                        for m in range(2):
                            dst = cv[:, e, T * m + back:T * m + T]
                            ins = STT(dst, pj[n % 2][:, T * m:T * m + T - back],
                                      par[:, 1, bass.ds(tile + (col + m), 1)], dst, ALU.mult, ALU.add)
                        if back == 1:
                            ins.then_inc(cv_mid.sem, 1)
                            v.wait_ge(cv_mid.sem, cv_mid.at(l, n - U_FFN + 1) + turn * 4)
                        else:
                            ins.then_inc(u.sem, 1)
                    cv_mid.made += times
                    u.made += times

                def ffn_step(c, cc, turn=0, times=1):
                    s = ffn_piece(cc)
                    split_lo(l, s + 3, turn, times)
                    if cc:
                        split_lo(l, s + 4, turn, times)
                    taps(U_FFN + 2 * cc, 0, c * 2, turn, times)
                    if cc:
                        split_lo(l, s + 5, turn, times)
                    split_lo(l, s + (6 if cc else 4), turn, times)
                    taps(U_FFN + 2 * cc + 1, 1, c * 2 + FT, turn, times)
                    split_lo(l, s + (7 if cc else 5), turn, times)
                    if s + 8 < len(PIECES):
                        split_lo(l, s + (8 if cc else 6), turn, times)
                    v.wait_ge(a_hi.sem, a_hi.at(l, cc + 1) + turn * 2)
                    TT(al[:, :], aT[:, cc % 2, :], ah[:, :].bitcast(F32), ALU.subtract).then_inc(a_split.sem, 1)
                    a_split.made += times

                ffn_step(0, 0)
                ffn_step(1, 1)
                with v.Fori(0, LOOP) as j:
                    ffn_step(j * 2 + 2, 2, j, LOOP)
                    ffn_step(j * 2 + 3, 3, j, LOOP)
                ffn_step(STEPS - 1, STEPS - 1)
                for b, o in enumerate(down):
                    v.wait_ge(down_done.sem, down_done.at(l, b + 1))
                    xq = xT[:, 2 * b:2 * b + 2, :]
                    TT(xq, xq, o[:, :].rearrange("p (k t) -> p k t", k=2), ALU.add)\
                        .then_inc(x_ready.sem, x_ready.up())

            saved = dve_step.made, h_new.made
            dve_step.made = 0
            norm(DEPTH, 1, A_FIN, split=False)
            dve_step.made, h_new.made = saved
            for b, o in enumerate(down):
                t, k = b // 2, 4 * (b % 2)
                v.wait_ge(fin_turned.sem, b + 1)
                nc.vector.tensor_copy(mT[:, 4 * t + k // 2:4 * t + k // 2 + 2, :],
                                      o[:, :].rearrange("p (k t) -> p k t", k=2)).then_inc(fin_ready.sem, 1)

        @block.gpsimd
        def _(g):
            TT = nc.gpsimd.tensor_tensor
            with g.Fori(0, DEPTH) as l:
                nc.gpsimd.memset(bx, 0.0).then_inc(bx_clear.sem, bx_clear.up())
                g.wait_ge(mats_in.sem, mats_in.at(l, 16 * 6))
                for c, mask in enumerate((K_PAR, K_NPAR)):
                    for w in range(2):
                        m = kon[:, mask + w:mask + w + 1].rearrange("p (a b) -> p a b", a=1)
                        ins = TT(cx[:, c, :, STATES * w:STATES * w + STATES], cnat[:, c],
                                 m.broadcast_to([P, JC, STATES]), ALU.mult)
                    ins.then_inc(cx_ready.sem, cx_ready.up())
                TC, TN = tab[:, 0], tab[:, 1]
                for e in range(7):
                    n = 1 << e
                    g.wait_ge(tab_d.sem, tab_d.at(l, e + 1))
                    if e:
                        g.wait_ge(tab_p.sem, tab_p.at(l, e))
                    cn = TC[:, :, n - 1:n].broadcast_to([P, ST, n])
                    nn = TN[:, :, n - 1:n].broadcast_to([P, ST, n])
                    TT(TN[:, :, n:2 * n], TN[:, :, 0:n], cn, ALU.mult)
                    TT(tmp_p[:, :, 0:n], TC[:, :, 0:n], nn, ALU.mult).then_inc(pool_step.sem, pool_step.up())
                    g.wait_ge(pool_step.sem, pool_step.at(l, pool_step.made))
                    TT(TN[:, :, n:2 * n], TN[:, :, n:2 * n], tmp_p[:, :, 0:n], ALU.add)\
                        .then_inc(tab_p.sem, tab_p.up())
                cos_b = kon[:, K_COS:K_COS + T].rearrange("p (o t) -> p o t", o=1)
                for n, dst in enumerate((kr[:, 0:2, :], kr[:, 2:3, :], qr[:, 0:2, :], qr[:, 2:4, :])):
                    g.wait_ge(rot_done.sem, rot_done.at(l, n + 1))
                    TT(dst, dst, cos_b.broadcast_to([P, dst.shape[1], T]), ALU.mult)\
                        .then_inc(rot_cos.sem, rot_cos.up())

                def add_merged(k, n):
                    g.wait_ge(unit_out[n % 2].sem, unit_out[n % 2].at(l, n // 2 + 1))
                    if k >= 4:
                        g.wait_ge(m_ready.sem, m_ready.at(l, k - 3))
                    m = mT[:, 2 * (k % 4):2 * (k % 4) + 2, :]
                    TT(m, m, yt[:, k % 2, :].rearrange("p (m t) -> p m t", m=2), ALU.add)\
                        .then_inc(m_ready.sem, m_ready.up())

                def s5_turn(s):
                    g.wait_ge(x5_used.sem, x5_used.at(l, s + 1))
                    c, n = s5a[:, 0, :], s5a[:, 1, :]
                    TT(s5x[:, 0, :], c[:, 0:T], n[:, T:2 * T], ALU.add)
                    TT(s5x[:, 1, :], c[:, T:2 * T], n[:, 0:T], ALU.subtract).then_inc(x5_turned.sem, x5_turned.up())

                def s5_back(s):
                    g.wait_ge(g5_ready.sem, g5_ready.at(l, s + 1))
                    gs = s5x[:, :, :].rearrange("p c (b t) -> p (c b) t", b=2)
                    for c in range(2):
                        ins = TT(s5a[:, c, :].rearrange("p (m t) -> p m t", m=4), gs,
                                 tab[:, c, s:s + 1, :].broadcast_to([P, 4, P]), ALU.mult)
                    ins.then_inc(pool_step.sem, pool_step.up())
                    g.wait_ge(pool_step.sem, pool_step.at(l, pool_step.made))
                    if s >= 2:
                        g.wait_ge(y_done.sem, y_done.at(l, s - 1))
                    c, n = s5a[:, 0, :], s5a[:, 1, :]
                    TT(s5h[:, s % 2, 0, :], c[:, 0:T], n[:, T:2 * T], ALU.subtract)
                    TT(s5h[:, s % 2, 1, :], c[:, T:2 * T], n[:, 0:T], ALU.add).then_inc(h5_ready.sem, h5_ready.up())

                def diagonal(ap):
                    d = ap.rearrange("p (b t) -> p b t", b=3)[:, 0:3:2, :]
                    g.sem_inc(passed.sem, 1)
                    return nc.gpsimd.affine_select(out=d, in_=d, pattern=[[0, 2], [1, P]], compare_op=ALU.is_gt,
                                                   fill=0.0, base=0, channel_multiplier=-1)

                for q in range(SLOTS):
                    f = q // 2
                    if q - 1 in SB_Z:
                        h = SB_Z[q - 1]
                        g.wait_ge(z_sp.sem, z_sp.at(l, h + 1))
                        diagonal(sbp[:, h % 2, :]).then_inc(z_spm.sem, z_spm.up())
                    if q in SB_R:
                        h = SB_R[q]
                        g.wait_ge(w_exp.sem, w_exp.at(l, h + 1))
                        diagonal(sbw[:, h % 3, :]).then_inc(w_ready.sem, w_ready.up())
                    if q in S5_X:
                        s5_turn(S5_X[q])
                    if q in NSA_S:
                        n = NSA_S[q]
                        w = nsa_unit(n)[3]
                        g.wait_ge(s_rec.sem, s_rec.at(l, n + 1))
                        pv = cols(pr[:, n % 2, :], w)
                        TT(pv, pv, rg[:, n % 2, :].rearrange("p (b o) -> p b o", o=1)
                           .broadcast_to([P, 2, w]), ALU.mult).then_inc(s_prob.sem, s_prob.up())
                    if q - 1 in S5_X:
                        s5_back(S5_X[q - 1])
                    if q % 2 and FILL[f][0] == "y" and FILL[f][1] == 2:
                        add_merged(FILL[f][2], U_FILL + f)
                for q in range(4):
                    add_merged(4 + q, U_Y + q)

                def product(cc, turn=0, times=1):
                    n = U_FFN + 2 * cc + 1
                    g.wait_ge(sg_ready.sem, sg_ready.at(l, cc + 1) + turn * 2)
                    g.wait_ge(unit_out[n % 2].sem, unit_out[n % 2].at(l, n // 2 + 1) + turn * 2)
                    g.wait_ge(a_split.sem, a_split.at(l, cc - 1) + turn * 2)
                    TT(aT[:, cc % 2, :], cv[:, 0, :], cv[:, 1, :], ALU.mult).then_inc(a_ready.sem, 1)
                    a_ready.made += times

                product(0)
                product(1)
                with g.Fori(0, LOOP) as j:
                    product(2, j, LOOP)
                    product(3, j, LOOP)
                product(STEPS - 1)

        off = [(t.name, t.made, t.per_layer) for t in tallies if t.made != t.per_layer]
        assert not off, off


def kernel(**inputs):
    import numpy as np
    import concourse.bacc as bacc
    from concourse.bass_utils import run_bass_kernel_spmd

    names = ["x", "norm_mix", "w_in", "ssm_lam_re", "ssm_lam_im", "ssm_log_step", "ssm_b_re", "ssm_b_im",
             "ssm_c_re", "ssm_c_im", "ssm_d", "ssm_w_glu", "cmp_w1_k", "cmp_w2_k", "cmp_pos_k",
             "cmp_w1_v", "cmp_w2_v", "cmp_pos_v", "w_branch", "w_out", "norm_ffn", "ffn_w_up",
             "ffn_conv_w", "ffn_conv_b", "ffn_w_down", "norm_final"]
    nc = bacc.Bacc("TRN2", target_bir_lowering=False, num_devices=1)
    arrays, args = {}, []
    for name in names + ["consts"]:
        a = constants() if name == "consts" else np.ascontiguousarray(inputs[name])
        arrays[f"in_{name}"] = a
        args.append(nc.dram_tensor(f"in_{name}", a.shape, mybir.dt.from_np(a.dtype), kind="ExternalInput").ap())
    args.append(nc.dram_tensor("out", (1, T, D), F32, kind="ExternalOutput").ap())
    build(nc, *args)
    r = run_bass_kernel_spmd(nc, [arrays], core_ids=[0])
    return r.results[0]["out"]
```

```python
from contextlib import ExitStack

import concourse.bass as bass
from concourse import mybir

F32 = mybir.dt.float32
F32R = mybir.dt.float32r
ALU = mybir.AluOpType
ACT = mybir.ActivationFunctionType
AX = mybir.AxisListType.X

P = 128
D = 1024
T = 256
DEPTH = 2
KD = D // P
NT = T // P
EPS = 1e-6
HD = 64
SCALE = HD ** -0.5
HEADS = 8
CH = 512
JC = CH // P
GROUPS, STATES, GCH = 32, 64, 16
ST = GROUPS * STATES // P
CMP, CSTR = 32, 16
NC = (T - CMP) // CSTR + 1
L2 = CMP // 2
F = 2816
FT = F // P
STEPS = F // (2 * P)
NEG = -1e30
TWO_PI = 6.283185307179586
PI_HIGH = 6.28125
PI_MID = int((TWO_PI - PI_HIGH) * 2 ** 21) / 2 ** 21
PI_PARTS = (PI_HIGH, PI_MID, TWO_PI - PI_HIGH - PI_MID)
MAGIC = 1.5 * 2 ** 23

C_U, C_Q, C_KV = 0, 512, 1024
C_G = 1792
C_SQ, C_SK, C_SV = 1816, 2328, 2840
C_M = 3352

RING = 3
SLOT = 2048
PLAN = ([("pair", C_Q + P * i, C_Q + CH // 2 + P * i) for i in range(2)]
        + [("pair", C_KV, C_KV + 256), ("pair", C_KV + 512, C_KV + 128),
         ("pair", C_KV + 384, C_KV + 640), ("ngate", C_G), ("in", C_U), ("in", C_U + 256)]
        + [("in", c + 256 * i) for c in (C_SQ, C_SK, C_SV) for i in range(2)]
        + [("in", C_M + D * b + 256 * i) for b in (1, 2, 0) for i in range(4)]
        + [("branch", 1, 0), ("branch", 1, 1), ("branch", 2, 0), ("branch", 2, 1),
           ("branch", 0, 0), ("branch", 0, 1)]
        + [("out", 256 * i) for i in range(4)])
C_FFN = len(PLAN)
CHUNKS = C_FFN + 3 * STEPS
assert CHUNKS % RING == 0
I_KV, I_V, I_GATES, I_U, I_FILL = 2, 4, 5, 6, 8
I_SBV = I_FILL + 4
I_Y = I_FILL + 18
I_OUT = I_Y + 6
LOOP = 4
assert 3 + 2 * LOOP == STEPS

PIECE = SLOT // 2
SPLIT = 3
BY_ROW = {I_V, I_GATES, I_SBV, I_SBV + 1} | {C_FFN + 4 + 3 * c for c in range(STEPS - 1)} | {CHUNKS - 1}
PIECES = [(i, e) for i in range(CHUNKS) for e in range(2)]
PIECE_OF = {at: s for s, at in reversed(list(enumerate(PIECES)))}
S_V, S_GATES, S_U, S_FILL, S_Y, S_OUT, S_FFN = (
    PIECE_OF[(i, 0)] for i in (I_V, I_GATES, I_U, I_FILL, I_Y, I_OUT, C_FFN))
assert len(PIECES) % SPLIT == 0 and S_Y == S_FILL + 36 and S_OUT == S_Y + 12
TURN = 12

FILL = ([("sbq", 0), ("sbq", 1), ("sbk", 0), ("sbk", 1), ("sbv", 0), ("sbv", 1)]
        + [("gate", b, i) for b in (1, 2, 0) for i in range(4)]
        + [("y", 1, i) for i in range(4)] + [("glu", 0), ("glu", 1)] + [("y", 2, i) for i in range(4)])
U_FILL = 8
U_GLU = U_FILL + 22
U_Y = U_FILL + len(FILL)
U_OUT = U_Y + 4
U_FFN = U_OUT + 4
UNITS = U_FFN + 2 * STEPS
assert UNITS % 2 == 0


def ffn_piece(c, n=0):
    return S_FFN + 2 * n + (4 + 6 * (c - 1) if c else 0)


SLOTS = 2 * len(FILL)
NSA = 16
CMP_HID, CMP_OUT, CMP_S = {0: 0, 1: 1}, 2, 3
NSA_S = {5 + n: n for n in range(NSA)}
NSA_T = {7 + n: n for n in range(NSA)}
NSA_V = {8 + n: n for n in range(NSA)}
SB_Z = {24 + 2 * h: h for h in range(HEADS)}
SB_R = {s + 3: h for s, h in SB_Z.items()}
SB_O = {s + 5: h for s, h in SB_Z.items()}
S5_X = {4 + 2 * s: s for s in range(ST)}
S5_Y = {7 + 2 * s: s for s in range(ST)}

OS_SPLIT = {47: 0, 49: 1}
GELU, ON_SPLIT, OB_SPLIT = 42, 35, 44
SPLIT_AT = {q: S_FILL + 2 + q for q in range(1, 37)} | {(32 if j < 7 else 36) + 2 * j: S_Y + j for j in range(3, 10)}

K_ID, K_ROT, K_TRI, K_NEG1 = 0, 128, 256, 384
K_COS, K_SIN = 512, 768
K_MASK = 1024
K_CMASK = 1280
K_PAR = 1312
K_NPAR = 1314
K_EPS = 1316
K_ALL = 1317

A_MIX, A_FFN, A_D, A_FIN, A_LR, A_LI, A_PK, A_PV, A_ST, A_PKS = 0, 8, 16, 20, 32, 48, 64, 80, 96, 112
B_W0, B_W1, B_PVS = 0, 22 * 2, 96
C_W2, C_B = 0, 44


def constants():
    import numpy as np

    k = np.zeros((P, K_ALL), np.float32)
    i = np.arange(P)
    k[:, K_ID:K_ID + P] = np.eye(P)
    for m in range(P):
        d = m % HD
        if d < HD // 2:
            k[m + HD // 2, K_ROT + m] = -1.0
        else:
            k[m - HD // 2, K_ROT + m] = 1.0
    k[:, K_TRI:K_TRI + P] = -(i[:, None] >= i[None, :]).astype(np.float32)
    k[:, K_NEG1:K_NEG1 + P] = -1.0
    freq = (np.float32(1.0) / (np.float32(10000.0) ** (np.arange(0, HD, 2, dtype=np.float32) / np.float32(HD))))
    ang = np.arange(T, dtype=np.float32)[:, None] * freq[None, :].astype(np.float32)
    cs, sn = np.cos(ang).T, np.sin(ang).T
    k[:, K_COS:K_COS + T] = np.tile(cs, (4, 1))
    k[:, K_SIN:K_SIN + T] = np.tile(sn, (4, 1))
    k[:, K_MASK + P:K_MASK + 2 * P] = np.where(i[None, :] <= i[:, None], 0.0, NEG)
    for t in range(NT):
        ends = np.arange(NC) * CSTR + CMP - 1
        k[:, K_CMASK + 16 * t:K_CMASK + 16 * t + NC] = np.where(ends[None, :] <= i[:, None] + P * t, 0.0, NEG)
    for w in range(2):
        k[:, K_PAR + w] = ((i // GCH) % 2 == w)
        k[:, K_NPAR + w] = -k[:, K_PAR + w]
    k[:, K_EPS] = EPS
    return k


def kind_of(i):
    return PLAN[i][0] if i < C_FFN else "ffn"


class Tally:

    def __init__(self, sem, name, per_layer, start=0):
        self.sem, self.name, self.per_layer, self.start, self.made = sem, name, per_layer, start, 0

    def up(self, n=1):
        self.made += n
        return n

    def last(self, l):
        return self.at(l, self.made)

    def at(self, l, k):
        return l * self.per_layer + (self.start + k)


def build(nc, x, norm_mix, w_in, ssm_lam_re, ssm_lam_im, ssm_log_step, ssm_b_re, ssm_b_im,
          ssm_c_re, ssm_c_im, ssm_d, ssm_w_glu, cmp_w1_k, cmp_w2_k, cmp_pos_k,
          cmp_w1_v, cmp_w2_v, cmp_pos_v, w_branch, w_out, norm_ffn, ffn_w_up,
          ffn_conv_w, ffn_conv_b, ffn_w_down, norm_final, consts, out):
    with ExitStack() as ctx:
        def sb(name, shape, dtype=F32):
            return ctx.enter_context(nc.sbuf_tensor(name, shape, dtype))

        def bank(name):
            return ctx.enter_context(nc.psum_tensor(name, [P, 512], F32))

        tallies = []

        def sem(name, per_layer=0, start=0):
            t = Tally(ctx.enter_context(nc.semaphore(name)), name, per_layer, start)
            tallies.append(t)
            return t

        ring = sb("ring", [P, RING, SLOT])
        kon = sb("kon", [P, K_ALL])
        xT = sb("xT", [P, KD, T])
        hh = sb("hh", [P, KD, T], F32R)
        hl = sb("hl", [P, KD, T], F32R)
        wh = sb("wh", [P, SPLIT, PIECE], F32R)
        wl = sb("wl", [P, SPLIT, PIECE], F32R)
        ah = sb("ah", [P, 2 * T], F32R)
        al = sb("al", [P, 2 * T], F32R)
        mT = sb("mT", [P, KD, T])
        rstd = sb("rstd", [P, T])
        eps2 = sb("eps2", [P, 1])
        stA = sb("stA", [P, P])
        stB = sb("stB", [P, P])
        stC = sb("stC", [P, P])
        par = sb("par", [P, 3, P])
        lstep = sb("lstep", [P, 2])
        bnat = sb("bnat", [P, 2, ST, GCH])
        cnat = sb("cnat", [P, 2, JC, STATES])
        w2 = sb("w2", [P, 2, HD])
        uT = sb("uT", [P, JC, T])
        qr = sb("qr", [P, 4, T])
        kr = sb("kr", [P, 4, T])
        vn = sb("vn", [P, NT, 2, P])
        ng = sb("ng", [P, NT, 3 * HEADS])
        hid = sb("hid", [P, 2, 32])
        kc = sb("kc", [P, 16])
        vc = sb("vc", [P, HD])
        cE = sb("cE", [P, NSA, 32])
        cm = sb("cm", [P, 3, NSA])
        pcT = sb("pcT", [P, 4, P])
        mx = sb("mx", [P, 2, 2])
        nm = sb("nm", [P, 2, 2])
        sm = sb("sm", [P, 2, 2])
        rc = sb("rc", [P, 2, 2])
        rg = sb("rg", [P, 2, 2])
        sbq = sb("sbq", [P, JC, T])
        sbk = sb("sbk", [P, 4, T])
        sbv = sb("sbv", [P, NT, CH])
        sbw = sb("sbw", [P, 3, 384])
        sbp = sb("sbp", [P, 2, 384])
        gate = sb("gate", [P, 3 * KD, T])
        oN, oB, oS, yT = qr, sbk, sbq, uT
        tab = sb("tab", [P, 2, ST, P])
        s5p = sb("s5p", [P, 20, ST])
        BL = sb("BL", [P, 2, JC, P])
        CL = sb("CL", [P, 2, JC, P])
        s5a = sb("s5a", [P, 2, 2 * T])
        s5x = sb("s5x", [P, 2, T])
        s5i = sb("s5i", [P, 4])
        s5h = sb("s5h", [P, 2, 2, T])
        work = sb("work", [P, 3, 2, 2 * T])
        sc = work[:, 0]
        pr = work[:, 1]
        pT = work[:, 2]
        cv = work[:, 0]
        aT = work[:, 1]
        yt = work[:, 2]
        cS = work[:, 2, 0, 0:NSA * NC].rearrange("p (n c) -> p n c", c=NC)
        cP = cE[:, :, 0:NC]
        rt = work[:, 0, 0, :]
        blk = s5a[:, :, :].rearrange("p a b -> p (a b)")[:, 0:4 * NC * L2].rearrange(
            "p (r g n a) -> p r g n a", r=2, g=2, n=NC)
        bb = s5h[:, 0, :, :].rearrange("p c (t i) -> p c t i", i=GCH)
        bbt = s5h[:, 1, :, :].rearrange("p c (t i) -> p c t i", i=GCH)
        bx = gate[:, 0:4, :].rearrange("p a b -> p (a b)").rearrange("p (c t i) -> p c t i", c=2, t=ST)
        cx = gate[:, 4:8, :].rearrange("p a b -> p (a b)").rearrange("p (c j q) -> p c j q", c=2, j=JC)
        tmp_d = gate[:, 8:12, :].rearrange("p a b -> p (a b)").rearrange("p (t n) -> p t n", t=ST)
        tmp_p = gate[:, 12:16, :].rearrange("p a b -> p (a b)").rearrange("p (t n) -> p t n", t=ST)

        sq = gate[:, 2 * KD:3 * KD, :]
        hT = sq
        xs = sq.rearrange("p (t a) b -> p t (a b)", t=NT)

        glu_w = tab[:, 0].rearrange("p t c -> p (t c)").rearrange("p (k n) -> p k n", k=JC)

        def cmp_w(r):
            return (mT, hT)[r].rearrange("p a b -> p (a b)").rearrange("p (a e) -> p a e", e=P)

        pj = [bank(f"pj{i}") for i in range(2)]
        bX = [bank(f"bX{i}") for i in range(2)]
        bY = bank("bY")
        bA = bank("bA")
        bB = bank("bB")
        bO = bank("bO")
        down = [bX[0], bX[1], bA, bB]

        consts_in = sem("consts_in")
        x_in = sem("x_in")
        setup = sem("setup")
        passed = sem("passed")
        out_sent = sem("out_sent")
        landed = [sem(f"landed{i}", 16 * CHUNKS // RING) for i in range(RING)]
        pair_in = [sem(f"pair_in{i}", 16) for i in range(5)]
        w_hi = sem("w_hi", len(PIECES))
        w_lo = sem("w_lo", len(PIECES), 6)
        w_used = sem("w_used", len(PIECES), SPLIT)
        cmp_in = [sem(f"cmp_in{i}", 32) for i in range(2)]
        glu_in = sem("glu_in", 16)
        upper_in = sem("upper_in", 32)
        rows_in = sem("rows_in", 16 * 17)
        mats_in = sem("mats_in", 16 * 6)
        params_free = sem("params_free", 1, 1)
        unit_done = sem("unit_done", 2)
        b_hi = sem("b_hi", 11)
        b_split = sem("b_split", 11)
        unit_out = [sem(f"unit_out{i}", UNITS // 2, 1) for i in range(2)]
        x_turned = sem("x_turned")
        x_ready = sem("x_ready", 8, 4)
        sq_ready = sem("sq_ready", 8)
        ss_done = sem("ss_done", 2)
        rms_ready = sem("rms_ready", 2)
        h_new = sem("h_new", 2 * KD)
        h_hi = sem("h_hi", 2 * KD)
        h_ready = [sem(f"h_ready{i}", KD) for i in range(2)]
        step_row = sem("step_row", 1)
        par_turned = sem("par_turned", 3)
        par_ready = sem("par_ready", 1)
        step_exp = sem("step_exp", 1)
        ang_ready = sem("ang_ready", 2)
        mag_ready = sem("mag_ready", 1)
        sin_ready = sem("sin_ready", 1)
        tab_d = sem("tab_d", 8)
        tab_p = sem("tab_p", 7)
        bx_ready = sem("bx_ready", 2)
        cx_ready = sem("cx_ready", 2)
        bx_clear = sem("bx_clear", 1)
        bc_turned = sem("bc_turned", 4)
        bc_ready = sem("bc_ready", 4)
        dve_step = sem("dve_step", 136)
        rot_done = sem("rot_done", 4)
        rot_cos = sem("rot_cos", 4)
        rot_ready = sem("rot_ready", 4)
        blk_ready = sem("blk_ready", 2)
        hid_done = sem("hid_done", 2)
        hid_ready = sem("hid_ready", 2)
        kc_done = sem("kc_done", 2)
        kc_ready = sem("kc_ready", 2)
        cs_done = sem("cs_done", 1)
        cs_ready = sem("cs_ready", 1)
        ce_ready = sem("ce_ready", 1)
        cp_ready = sem("cp_ready", 1)
        pc_done = sem("pc_done", 1)
        pc_ready = sem("pc_ready", 1)
        s_done = sem("s_done", NSA)
        s_max = sem("s_max", NSA)
        s_exp = sem("s_exp", NSA)
        s_rec = sem("s_rec", NSA)
        s_prob = sem("s_prob", NSA)
        t_done = sem("t_done", NSA)
        t_ready = sem("t_ready", NSA)
        v_done = sem("v_done", NSA)
        on_ready = sem("on_ready", 4)
        z_done = sem("z_done", HEADS)
        z_abs = sem("z_abs", HEADS)
        z_exp = sem("z_exp", HEADS)
        z_ln = sem("z_ln", HEADS)
        z_sp = sem("z_sp", HEADS)
        z_spm = sem("z_spm", HEADS)
        r_done = sem("r_done", HEADS)
        w_exp = sem("w_exp", HEADS)
        w_ready = sem("w_ready", HEADS)
        o_done = sem("o_done", HEADS)
        ob_ready = sem("ob_ready", 4)
        x5_done = sem("x5_done", ST)
        x5_used = sem("x5_used", ST)
        x5_turned = sem("x5_turned", ST)
        g5_ready = sem("g5_ready", ST)
        pool_step = sem("pool_step", 7 + ST)
        h5_ready = sem("h5_ready", ST)
        y_done = sem("y_done", ST)
        y_used = sem("y_used", JC)
        y_ready = sem("y_ready", 1)
        os_ready = sem("os_ready", 2)
        m_ready = sem("m_ready", 8)
        cv_last = sem("cv_last", 2 * STEPS)
        cv_mid = sem("cv_mid", 2 * STEPS)
        sg_ready = sem("sg_ready", STEPS)
        a_ready = sem("a_ready", STEPS)
        a_hi = sem("a_hi", STEPS)
        a_split = sem("a_split", STEPS, 2)
        down_done = sem("down_done", 4)
        fin_turned = sem("fin_turned")
        fin_ready = sem("fin_ready")

        ident = kon[:, K_ID:K_ID + P]

        def chunk_at(l, i):
            return landed[i % RING].at(l, 16 * (i // RING + 1))

        def summed(n):
            if n < U_FILL + 18:
                return w_used, 2 * (n + 1)
            if n < U_GLU:
                return w_used, S_Y + n - U_FILL - 17
            if n < U_GLU + 2:
                return unit_done, n - U_GLU + 1
            if n < U_Y:
                return w_used, S_Y + 4 + n - U_GLU - 1
            if n < U_OUT:
                return w_used, S_Y + 9 + n - U_Y
            if n < U_FFN:
                return w_used, S_OUT + 2 * (n - U_OUT + 1)
            return w_used, ffn_piece((n - U_FFN) // 2, (n - U_FFN) % 2) + 2

        def piece_from(s, dst):
            i, e = PIECES[s]
            dst = dst[:, s % SPLIT, :]
            if i == I_GATES:
                n = KD // 2 * 3 * HEADS
                return slot_of(i)[:, n * e:n * e + n], dst[:, 0:n]
            if i in BY_ROW:
                return slot_of(i)[:, PIECE * e:PIECE * e + PIECE], dst
            if i < I_KV:
                src = slot_of(i).rearrange("p (k s i d) -> p k s i d", k=KD, s=2, i=2)
                return src[:, :, :, e, :], dst.rearrange("p (k s d) -> p k s d", k=KD, s=2)
            k = JC if i < C_FFN and PLAN[i][0] == "branch" else KD
            n = PIECE // k
            return (slot_of(i).rearrange("p (k n) -> p k n", k=k)[:, :, n * e:n * e + n],
                    dst.rearrange("p (k n) -> p k n", k=k))

        def unit(n):
            return pj[n % 2][:, :].rearrange("p (m t) -> p m t", m=2)

        def slot_of(i):
            return ring[:, i % RING, :]

        def nsa_unit(n):
            i, s, t = n // 4, n // 2 % 2, n % 2
            return i, s, t, P * (t + 1)

        def cols(ap, w):
            return ap[:, 0:2 * w].rearrange("p (b w) -> p b w", b=2)

        xd = x.rearrange("b (t p) d -> p (b t) d", p=P)
        od = out.rearrange("b (t p) d -> p (b t) d", p=P)

        block = ctx.enter_context(nc.Block())

        @block.sync
        def _(sp):
            sp.dma_start(kon[:, :], consts).then_inc(consts_in.sem, 16)
            sp.dma_start(xs, xd).then_inc(x_in.sem, 16)
            sp.wait_ge(setup.sem, 3)

            def row(w, l):
                return w[bass.ds(l, 1)]

            def par_in(dst, src):
                sp.dma_start(dst, src).then_inc(rows_in.sem, rows_in.up(16))

            def mat_in(dst, src):
                sp.dma_start(dst, src).then_inc(mats_in.sem, mats_in.up(16))

            def chunk_split(i):
                return PIECE_OF[(i, 1)] + 1

            def load(l, i):
                kind, *at = PLAN[i]
                dst = slot_of(i)
                k = chunk_split((i - RING) % CHUNKS)
                sp.wait_ge(w_lo.sem, w_lo.at(l, k if i >= RING else k - len(PIECES)))
                sp.sem_inc(passed.sem, 1)
                if kind in ("in", "ngate", "out"):
                    n = 3 * HEADS if kind == "ngate" else 256
                    w = w_out if kind == "out" else w_in
                    src = row(w, l)[:, :, at[0]:at[0] + n].rearrange("l (k p) n -> p (l k) n", p=P)
                    dst = dst[:, 0:KD * n].rearrange("p (k n) -> p k n", k=KD)
                elif kind == "pair":
                    dst = dst.rearrange("p (k n) -> p k n", k=KD)
                    src = [row(w_in, l)[:, :, c:c + P].rearrange("l (k p) n -> p (l k) n", p=P) for c in at]
                    sp.dma_start(dst[:, :, 0:P], src[0])\
                        .then_inc(pair_in[i].sem, pair_in[i].up(16))
                    dst, src = dst[:, :, P:2 * P], src[1]
                else:
                    b, half = at
                    dst = dst.rearrange("p (k n) -> p k n", k=JC)
                    w = row(w_branch, l)[:, b, :, CH * half:CH * half + CH]
                    if b == 1:
                        src = w.rearrange("l (s k p) n -> s p (l k) n", p=HD, s=2)
                        sp.dma_start(dst[0:HD], src[0]).then_inc(upper_in.sem, upper_in.up(16))
                        dst, src = dst[HD:P], src[1]
                    else:
                        src = w.rearrange("l (k p) n -> p (l k) n", p=P)
                sp.dma_start(dst, src).then_inc(landed[i % RING].sem, landed[i % RING].up(16))

            def load_cmp(l, r):
                src = row((cmp_w1_k, cmp_w1_v)[r], l).rearrange("l (a b) d e -> (b d) (l a) e", b=2)
                dst = cmp_w(r)
                for a in range(0, L2, L2 // 2):
                    sp.dma_start(dst[:, a:a + L2 // 2], src[:, a:a + L2 // 2])\
                        .then_inc(cmp_in[r].sem, cmp_in[r].up(16))

            def load_ffn(l, i, part, c, turn=0, times=1):
                k = chunk_split(i - RING)
                more = turn * TURN if times > 1 else 0
                sp.wait_ge(w_lo.sem, w_lo.at(l, k) + more)
                sp.sem_inc(passed.sem, 1)
                if part == "down":
                    src = row(ffn_w_down, l)[:, bass.ds(c * 256, 256), :].rearrange("l (k p) n -> p (l k) n", p=P)
                    dst = slot_of(i).rearrange("p (k n) -> p k n", k=2)
                else:
                    first = F if part == "value" else 0
                    src = row(ffn_w_up, l)[:, :, bass.ds(c * 256 + first, 256)].rearrange(
                        "l (k p) n -> p (l k) n", p=P)
                    dst = slot_of(i).rearrange("p (k n) -> p k n", k=KD)
                sp.dma_start(dst, src).then_inc(landed[i % RING].sem, 16)
                landed[i % RING].made += 16 * times

            with sp.Fori(0, DEPTH) as l:
                load(l, 0)
                load(l, 1)
                sp.wait_ge(params_free.sem, params_free.at(l, 0))
                sp.sem_inc(passed.sem, 1)
                par_in(stA[A_MIX:A_MIX + 8, :], row(norm_mix, l).rearrange("l (k p) -> (l k) p", p=P))
                par_in(stA[A_FFN:A_FFN + 8, :], row(norm_ffn, l).rearrange("l (k p) -> (l k) p", p=P))
                par_in(stA[A_D:A_D + 4, :], row(ssm_d, l).rearrange("l (k g) i -> (l k) (g i)", k=4))
                par_in(stA[A_FIN:A_FIN + 8, :], norm_final.rearrange("(k p) -> k p", p=P))
                par_in(stA[A_LR:A_LR + ST, :], row(ssm_lam_re, l).rearrange("l (t w) p -> (l t) (w p)", w=2))
                par_in(stA[A_LI:A_LI + ST, :], row(ssm_lam_im, l).rearrange("l (t w) p -> (l t) (w p)", w=2))
                par_in(lstep[A_ST:A_ST + ST, :], row(ssm_log_step, l).rearrange("l (t w) -> (l t) w", w=2))
                for pos, own, st, swap in ((cmp_pos_k, A_PK, stA, A_PKS), (cmp_pos_v, A_PV, stB, B_PVS)):
                    src = row(pos, l).rearrange("l (a b) d -> (l a) b d", b=2)
                    par_in(stA[own:own + L2, :].rearrange("a (b d) -> a b d", b=2), src)
                    dst = st[swap:swap + L2, :].rearrange("a (b d) -> a b d", b=2)
                    for b in range(2):
                        par_in(dst[:, b:b + 1, :], src[:, 1 - b:2 - b, :])
                cw = row(ffn_conv_w, l)
                par_in(stB[B_W0:B_W0 + 2 * FT, :], cw[:, 0, :].rearrange("l (k p) -> (l k) p", p=P))
                par_in(stB[B_W1:B_W1 + 2 * FT, :], cw[:, 1, :].rearrange("l (k p) -> (l k) p", p=P))
                par_in(stC[C_W2:C_W2 + 2 * FT, :], cw[:, 2, :].rearrange("l (k p) -> (l k) p", p=P))
                par_in(stC[C_B:C_B + 2 * FT, :], row(ffn_conv_b, l).rearrange("l (k p) -> (l k) p", p=P))
                for r, w in enumerate((ssm_b_re, ssm_b_im)):
                    mat_in(bnat[:, r], row(w, l).rearrange("l (t w) p i -> (w p) (l t) i", w=2))
                for r, w in enumerate((ssm_c_re, ssm_c_im)):
                    mat_in(cnat[:, r], row(w, l).rearrange("l (j q) i p -> (q i) (l j) p", j=JC))
                for r, w in enumerate((cmp_w2_k, cmp_w2_v)):
                    mat_in(w2[:, r], row(w, l).rearrange("l e d -> (l e) d"))
                for i in range(2, C_FFN):
                    load(l, i)
                    if i == 2:
                        load_cmp(l, 0)
                    if i == 3:
                        for h in h_ready:
                            sp.wait_ge(h.sem, h.at(l, KD // 2))
                        sp.sem_inc(passed.sem, 1)
                        load_cmp(l, 1)
                    if i == I_Y + 2:
                        sp.wait_ge(h5_ready.sem, h5_ready.at(l, ST))
                        sp.sem_inc(passed.sem, 1)
                        sp.dma_start(glu_w, row(ssm_w_glu, l).rearrange("l (k p) n -> p (l k) n", p=P))\
                            .then_inc(glu_in.sem, glu_in.up(16))
                i = C_FFN
                load_ffn(l, i, "gate", 0)
                load_ffn(l, i + 1, "value", 0)
                load_ffn(l, i + 2, "gate", 1)
                load_ffn(l, i + 3, "value", 1)
                load_ffn(l, i + 4, "down", 0)
                i += 5
                with sp.Fori(0, LOOP) as j:
                    for e in range(2):
                        for n, part in enumerate(("gate", "value", "down")):
                            c = j * 2 + (1 + e if part == "down" else 2 + e)
                            load_ffn(l, i + 3 * e + n, part, c, j, LOOP)
                i += 6 * LOOP
                load_ffn(l, i, "gate", STEPS - 1)
                load_ffn(l, i + 1, "value", STEPS - 1)
                load_ffn(l, i + 2, "down", STEPS - 2)
                load_ffn(l, i + 3, "down", STEPS - 1)
            sp.wait_ge(fin_ready.sem, 4)
            sp.dma_start(od, mT[:, :, :].rearrange("p (t a) b -> p t (a b)", t=NT)).then_inc(out_sent.sem, 16)
            sp.wait_ge(out_sent.sem, 16)

        @block.tensor
        def _(pe):
            def mm(o, a, b, start, stop):
                return nc.tensor.matmul(o, a, b, start=start, stop=stop, skip_group_check=True)

            def tiles(n, lhs, rhs, kt, halves=(0, 1)):
                for m in halves:
                    for k in range(kt):
                        ins = mm(pj[n % 2][:, T * m:T * m + T], lhs(m, k), rhs(k), k == 0, k == kt - 1)
                if 1 in halves:
                    ins.then_inc(unit_done.sem, unit_done.up())

            def piece(l, s, o, turn=0):
                pe.wait_ge(w_lo.sem, w_lo.at(l, s + 1) + turn)
                hi, lo = (w[:, s % SPLIT, :].rearrange("p (k n) -> p k n", k=KD) for w in (wh, wl))
                for k in range(KD):
                    if s == S_OUT:
                        pe.wait_ge(b_split.sem, b_split.at(l, 8 + k // 2))
                    if s in (0, S_FFN):
                        h = h_ready[k % 2]
                        pe.wait_ge(h.sem, h.at(l, (KD // 2 if s else 0) + k // 2 + 1))
                    mm(o, hi[:, k, :], hh[:, k, :], k == 0, False)
                    mm(o, hi[:, k, :], hl[:, k, :], False, False)
                    ins = mm(o, lo[:, k, :], hh[:, k, :], False, k == KD - 1)
                return ins

            def turned_piece(l, s, o, n):
                pe.wait_ge(w_lo.sem, w_lo.at(l, s + 1))
                rows = KD // 2
                first = rows * PIECES[s][1]
                hi, lo = (w[:, s % SPLIT, 0:rows * n].rearrange("p (k n) -> p k n", k=rows) for w in (wh, wl))
                for k in range(rows):
                    for t in range(NT):
                        c = slice(P * t, P * t + P)
                        kk = first + k
                        mm(o(t), hh[:, kk, c], hi[:, k, :], kk == 0 and t == 0, False)
                        mm(o(t), hh[:, kk, c], lo[:, k, :], False, False)
                        ins = mm(o(t), hl[:, kk, c], hi[:, k, :], False, kk == KD - 1)
                return ins

            def branch_half(l, s, n, m, first):
                if m == 0:
                    pe.wait_ge(w_lo.sem, w_lo.at(l, s + 1))
                hi, lo = (w[:, s % SPLIT, :].rearrange("p (k n) -> p k n", k=JC) for w in (wh, wl))
                o, c = pj[n % 2][:, T * m:T * m + T], slice(P * m, P * m + P)
                for k in range(JC):
                    if s == S_Y and m == 0:
                        pe.wait_ge(b_split.sem, b_split.at(l, k + 1))
                    x = first + k
                    mm(o, hi[:, k, c], hh[:, x, :], k == 0, False)
                    mm(o, hi[:, k, c], hl[:, x, :], False, False)
                    ins = mm(o, lo[:, k, c], hh[:, x, :], False, k == JC - 1)
                if m:
                    ins.then_inc(w_used.sem, w_used.up())

            def sum_squares(l, first):
                for k in range(KD):
                    if k == KD - 2 and first == 0 and l is not DEPTH:
                        pe.wait_ge(step_row.sem, step_row.at(l, 1))
                        for n, st in enumerate((stA, stB, stC)):
                            nc.tensor.transpose(bX[0][:, P * n:P * n + P], st[:, :], ident)\
                                .then_inc(par_turned.sem, par_turned.up())
                    if k % 2 == 0:
                        pe.wait_ge(sq_ready.sem, sq_ready.at(l, first + k // 2 + 1))
                    ins = mm(bO[:, 0:T], kon[:, K_NEG1:K_NEG1 + P], sq[:, k, :], k == 0, k == KD - 1)
                return ins

            pe.wait_ge(consts_in.sem, 16)
            pe.wait_ge(x_in.sem, 16)
            for b, o in enumerate(down):
                for k in range(2):
                    for t in range(NT):
                        kk = 2 * b + k
                        ins = nc.tensor.transpose(o[:, T * k + P * t:T * k + P * t + P],
                                                  xs[:, t, P * kk:P * kk + P], ident)
                ins.then_inc(x_turned.sem, 1)

            with pe.Fori(0, DEPTH) as l:
                sum_squares(l, 0).then_inc(ss_done.sem, ss_done.up())
                for s in range(8):
                    n = s // 2
                    if s % 2 == 0:
                        pe.wait_ge(unit_out[n % 2].sem, unit_out[n % 2].at(l, n // 2))
                    c = T * (s % 2)
                    piece(l, s, pj[n % 2][:, c:c + T]).then_inc(w_used.sem, w_used.up())
                pe.wait_ge(unit_out[0].sem, unit_out[0].at(l, 2))
                for s in (S_V, S_V + 1):
                    turned_piece(l, s, lambda t: pj[0][:, T * t:T * t + T], T).then_inc(w_used.sem, w_used.up())
                pe.wait_ge(unit_out[1].sem, unit_out[1].at(l, 2))
                for s in (S_GATES, S_GATES + 1):
                    turned_piece(l, s, lambda t: pj[1][:, 3 * HEADS * t:3 * HEADS * (t + 1)], 3 * HEADS)\
                        .then_inc(w_used.sem, w_used.up())
                for n, (o, src, u) in enumerate(((bO, kr[:, 0:2, :], 2), (bX[1], kr[:, 2:3, :], 3),
                                                 (bA, qr[:, 0:2, :], 0), (bB, qr[:, 2:4, :], 1))):
                    pe.wait_ge(unit_out[u % 2].sem, unit_out[u % 2].at(l, u // 2 + 1))
                    src = src.rearrange("p a b -> p (a b)")
                    mm(o[:, 0:src.shape[1]], kon[:, K_ROT:K_ROT + P], src, True, True)\
                        .then_inc(rot_done.sem, rot_done.up())
                for s in range(S_U, S_FILL):
                    n = s // 2
                    if s % 2 == 0:
                        pe.wait_ge(unit_out[n % 2].sem, unit_out[n % 2].at(l, n // 2))
                    c = T * (s % 2)
                    piece(l, s, pj[n % 2][:, c:c + T]).then_inc(w_used.sem, w_used.up())
                def filler(f, half):
                    kind, *at = FILL[f]
                    n = U_FILL + f
                    if half == 0:
                        pe.wait_ge(unit_out[n % 2].sem, unit_out[n % 2].at(l, n // 2))
                    if kind == "sbv":
                        turned_piece(l, S_FILL + 2 * f + half, lambda t: pj[n % 2][:, T * t:T * t + T], T)\
                            .then_inc(w_used.sem, w_used.up())
                    elif kind == "glu":
                        if half == 0 and at[0] == 0:
                            pe.wait_ge(glu_in.sem, glu_in.at(l, 16))
                            pe.wait_ge(y_ready.sem, y_ready.at(l, 1))
                        w = glu_w
                        c = 2 * P * at[0]
                        tiles(n, lambda m, k: w[:, k, c + P * m:c + P * m + P], lambda k: yT[:, k, :], JC, (half,))
                    elif kind == "y":
                        b, q = at
                        if (b, q, half) == (2, 0, 0):
                            pe.wait_ge(b_split.sem, b_split.at(l, 5))
                        branch_half(l, S_Y + 4 * (b - 1) + q, n, half, 4 * (b - 1))
                    else:
                        piece(l, S_FILL + 2 * f + half, pj[n % 2][:, T * half:T * half + T])\
                            .then_inc(w_used.sem, w_used.up())

                def cmp_hidden(r):
                    if r == 0:
                        pe.wait_ge(rot_ready.sem, rot_ready.at(l, 4))
                    pe.wait_ge(cmp_in[r].sem, cmp_in[r].at(l, 32))
                    w = cmp_w(r)
                    pe.wait_ge(blk_ready.sem, blk_ready.at(l, r + 1))
                    for a in range(L2):
                        ins = mm((bA, bB)[r][:, 0:2 * NC], w[:, a, :], blk[:, r, :, :, a], a == 0, a == L2 - 1)
                    ins.then_inc(hid_done.sem, hid_done.up())

                def cmp_out():
                    for r in range(2):
                        pe.wait_ge(hid_ready.sem, hid_ready.at(l, r + 1))
                        for s in range(2):
                            hs = hid[:, r, NC * s:NC * s + NC]
                            if r == 0:
                                ins = mm(bO[HD * s:HD * s + HD, 0:NC], w2[:, 0, :], hs, True, True)
                            else:
                                for t in range(NT):
                                    row = 32 * (2 * s + t)
                                    ins = nc.tensor.matmul(bB[row:row + NC, 64:64 + HD], hs, w2[:, 1, :], start=True,
                                                           stop=True, skip_group_check=True, tile_position=(0, row))
                        ins.then_inc(kc_done.sem, kc_done.up())

                def cmp_scores():
                    pe.wait_ge(kc_ready.sem, kc_ready.at(l, 1))
                    for n in range(NSA):
                        i, s, t, _ = nsa_unit(n)
                        c = 16 * (NT * i + t)
                        ins = mm((bA, bO)[s][:, c:c + NC], qr[HD * s:HD * s + HD, i, P * t:P * t + P],
                                 kc[HD * s:HD * s + HD, 0:NC], True, True)
                    ins.then_inc(cs_done.sem, cs_done.up())

                def s5_operands():
                    for r in range(2):
                        pe.wait_ge(bx_ready.sem, bx_ready.at(l, r + 1))
                        for j in range(JC):
                            ins = nc.tensor.transpose(bX[r][:, P * j:P * j + P],
                                                      bx[:, r, 4 * j:4 * j + 4, :].rearrange("p a b -> p (a b)"), ident)
                        ins.then_inc(bc_turned.sem, bc_turned.up())
                    for r in range(2):
                        pe.wait_ge(cx_ready.sem, cx_ready.at(l, r + 1))
                        if r == 1:
                            pe.wait_ge(bc_ready.sem, bc_ready.at(l, 1))
                        for j in range(JC):
                            ins = nc.tensor.transpose((bY, bX[0])[r][:, P * j:P * j + P], cx[:, r, j, :], ident)
                        ins.then_inc(bc_turned.sem, bc_turned.up())
                    params_free.made += 1
                    pe.sem_inc(params_free.sem, 1)

                def nsa_scores(n):
                    i, s, t, w = nsa_unit(n)
                    if n == 0:
                        pe.wait_ge(cs_ready.sem, cs_ready.at(l, 1))
                    else:
                        pe.wait_ge(s_max.sem, s_max.at(l, n))
                    mm(bA[:, 0:2 * w], qr[HD * s:HD * s + HD, i, P * t:P * t + P],
                       kr[HD * s:HD * s + HD, 1:3, 0:w], True, True).then_inc(s_done.sem, s_done.up())

                def nsa_turn(n):
                    i, s, t, w = nsa_unit(n)
                    pe.wait_ge(s_prob.sem, s_prob.at(l, n + 1))
                    if n == 0:
                        pe.wait_ge(cp_ready.sem, cp_ready.at(l, 1))
                        pe.wait_ge(kc_ready.sem, kc_ready.at(l, 2))
                        for i in range(4):
                            ins = nc.tensor.transpose(bO[:, P * i:P * i + P],
                                                      cE[:, 4 * i:4 * i + 4, :].rearrange("p a b -> p (a b)"), ident)
                        ins.then_inc(pc_done.sem, pc_done.up())
                    else:
                        pe.wait_ge(t_ready.sem, t_ready.at(l, n))
                    for b in range(2):
                        for k in range(t + 1):
                            c = P * (b * (t + 1) + k)
                            ins = nc.tensor.transpose(bB[:, c:c + P], pr[:, n % 2, c:c + P], ident)
                    ins.then_inc(t_done.sem, t_done.up())

                def nsa_values(n):
                    i, s, t, w = nsa_unit(n)
                    pe.wait_ge(t_ready.sem, t_ready.at(l, n + 1))
                    if n % 4 == 0 and n:
                        pe.wait_ge(on_ready.sem, on_ready.at(l, n // 4))
                    if n == 0:
                        pe.wait_ge(pc_ready.sem, pc_ready.at(l, 1))
                    else:
                        pe.wait_ge(v_done.sem, v_done.at(l, n))
                    o = bO[HD * s:HD * s + HD, P * t:P * t + P]
                    row = 32 * (2 * s + t)
                    nc.tensor.matmul(o, vc[row:row + NC, :], pcT[row:row + NC, i, :], start=True, stop=False,
                                     skip_group_check=True, tile_position=(row, HD * s))
                    for b in range(2):
                        for k in range(t + 1):
                            c = P * (b * (t + 1) + k)
                            ins = mm(o, vn[:, k, b, HD * s:HD * s + HD], pT[:, n % 2, c:c + P],
                                     False, b == 1 and k == t)
                    ins.then_inc(v_done.sem, v_done.up())

                def sb_scores(h):
                    i, s = h // 2, HD * (h % 2)
                    if h == 0:
                        for f in (4, 5):
                            n = U_FILL + f
                            pe.wait_ge(unit_out[n % 2].sem, unit_out[n % 2].at(l, n // 2 + 1))
                        pe.wait_ge(s_max.sem, s_max.at(l, NSA))
                        pe.wait_ge(t_ready.sem, t_ready.at(l, NSA))
                    elif h > 1:
                        pe.wait_ge(w_exp.sem, w_exp.at(l, h - 1))
                    z = (bA, bB)[h % 2]
                    mm(z[:, 0:T], sbk[s:s + HD, i, 0:P], sbq[s:s + HD, i, :], True, False)
                    mm(z[:, T:T + P], sbk[s:s + HD, i, P:T], sbq[s:s + HD, i, P:T], False, False)\
                        .then_inc(z_done.sem, z_done.up())

                def sb_rest(h):
                    pe.wait_ge(z_spm.sem, z_spm.at(l, h + 1))
                    z, p = (bA, bB)[h % 2], sbp[:, h % 2, :]
                    tri, neg1 = kon[:, K_TRI:K_TRI + P], kon[:, K_NEG1:K_NEG1 + P]
                    mm(z[:, 0:T], tri, p[:, 0:T], False, False)
                    mm(z[:, P:T], neg1, p[:, T:T + P], False, False)
                    mm(z[:, T:T + P], tri, p[:, T:T + P], False, True).then_inc(r_done.sem, r_done.up())

                def sb_values(h):
                    pe.wait_ge(w_ready.sem, w_ready.at(l, h + 1))
                    if h == 0:
                        pe.wait_ge(on_ready.sem, on_ready.at(l, 4))
                    elif h % 2 == 0:
                        pe.wait_ge(ob_ready.sem, ob_ready.at(l, h // 2))
                    o = bO[HD * (h % 2):HD * (h % 2) + HD, 0:T]
                    w = sbw[:, h % 3, :]
                    mm(o, sbv[:, 0, HD * h:HD * h + HD], w[:, 0:T], True, False)
                    mm(o[:, P:T], sbv[:, 1, HD * h:HD * h + HD], w[:, T:T + P], False, True)\
                        .then_inc(o_done.sem, o_done.up())

                def s5_inputs(s):
                    b, j, r = bX[s % 2], s // 4, 32 * (s % 4)
                    if s == 0:
                        pe.wait_ge(unit_out[0].sem, unit_out[0].at(l, 4))
                        pe.wait_ge(unit_out[1].sem, unit_out[1].at(l, 4))
                        pe.wait_ge(bc_ready.sem, bc_ready.at(l, 4))
                    elif s > 1:
                        pe.wait_ge(x5_used.sem, x5_used.at(l, s - 1))
                    for c in range(2):
                        ins = nc.tensor.matmul(b[:, T * c:T * c + T], BL[r:r + 32, c, j, :], uT[r:r + 32, j, :],
                                               start=True, stop=True, skip_group_check=True, tile_position=(r, 0))
                    ins.then_inc(x5_done.sem, x5_done.up())

                def s5_outputs(s):
                    j, r = s // 4, 32 * (s % 4)
                    pe.wait_ge(h5_ready.sem, h5_ready.at(l, s + 1))
                    if s % 4 == 0 and j:
                        pe.wait_ge(y_used.sem, y_used.at(l, j))
                    for c in range(2):
                        ins = nc.tensor.matmul(bY[r:r + 32, 0:T], CL[:, c, j, r:r + 32],
                                               s5h[:, s % 2, c, :], start=c == 0, stop=c == 1,
                                               skip_group_check=True, tile_position=(0, r))
                    ins.then_inc(y_done.sem, y_done.up())

                for q in range(SLOTS):
                    filler(q // 2, q % 2)
                    if q in CMP_HID:
                        cmp_hidden(CMP_HID[q])
                    if q == CMP_OUT:
                        cmp_out()
                    if q == CMP_S:
                        cmp_scores()
                        s5_operands()
                    if q in S5_X:
                        s5_inputs(S5_X[q])
                    if q in NSA_S:
                        nsa_scores(NSA_S[q])
                    if q in NSA_T:
                        nsa_turn(NSA_T[q])
                    if q in NSA_V:
                        nsa_values(NSA_V[q])
                    if q in SB_Z:
                        sb_scores(SB_Z[q])
                    if q in SB_R:
                        sb_rest(SB_R[q])
                    if q in SB_O:
                        sb_values(SB_O[q])
                    if q in S5_Y:
                        s5_outputs(S5_Y[q])

                pe.wait_ge(b_split.sem, b_split.at(l, 7))
                for q in range(4):
                    u = U_Y + q
                    pe.wait_ge(unit_out[u % 2].sem, unit_out[u % 2].at(l, u // 2))
                    for m in range(2):
                        branch_half(l, S_Y + 8 + q, u, m, 0)
                for q in range(4):
                    u = U_OUT + q
                    pe.wait_ge(unit_out[u % 2].sem, unit_out[u % 2].at(l, u // 2))
                    for m in range(2):
                        piece(l, S_OUT + 2 * q + m, pj[u % 2][:, T * m:T * m + T]).then_inc(w_used.sem, w_used.up())

                sum_squares(l, 4).then_inc(ss_done.sem, ss_done.up())

                def up(s, n, turn=0, times=1):
                    pe.wait_ge(unit_out[n % 2].sem, unit_out[n % 2].at(l, n // 2) + turn * 2)
                    for m in range(2):
                        piece(l, s + m, pj[n % 2][:, T * m:T * m + T], turn * TURN)\
                            .then_inc(w_used.sem, 1)
                        w_used.made += times

                def dn(s, c, turn=0, times=1):
                    pe.wait_ge(a_split.sem, a_split.at(l, c + 1) + turn * 2)
                    for k in range(2):
                        pe.wait_ge(w_lo.sem, w_lo.at(l, s + k + 1) + turn * TURN)
                        hi, lo = wh[:, (s + k) % SPLIT, :], wl[:, (s + k) % SPLIT, :]
                        xh, xl = ah[:, T * k:T * k + T], al[:, T * k:T * k + T]
                        for m in range(KD):
                            o = down[m // 2][:, T * (m % 2):T * (m % 2) + T]
                            c8 = slice(P * m, P * m + P)
                            mm(o, hi[:, c8], xh, times == 1 and c == 0 and k == 0 and m % 2 == 0, False)
                            mm(o, hi[:, c8], xl, False, False)
                            ins = mm(o, lo[:, c8], xh, False, False)
                        ins.then_inc(w_used.sem, 1)
                        w_used.made += times

                def ffn_step(cc, turn=0, times=1):
                    up(ffn_piece(cc), U_FFN + 2 * cc, turn, times)
                    up(ffn_piece(cc, 1), U_FFN + 2 * cc + 1, turn, times)
                    if cc:
                        dn(ffn_piece(cc, 2), cc - 1, turn, times)

                ffn_step(0)
                ffn_step(1)
                with pe.Fori(0, LOOP) as j:
                    ffn_step(2, j, LOOP)
                    ffn_step(3, j, LOOP)
                ffn_step(STEPS - 1)
                s = len(PIECES) - 2
                pe.wait_ge(a_split.sem, a_split.at(l, STEPS))
                pe.wait_ge(w_lo.sem, w_lo.at(l, s + 2))
                for m in range(KD):
                    o = down[m // 2][:, T * (m % 2):T * (m % 2) + T]
                    for k in range(2):
                        hi, lo = (w[:, (s + k) % SPLIT, P * m:P * m + P] for w in (wh, wl))
                        xh, xl = ah[:, T * k:T * k + T], al[:, T * k:T * k + T]
                        mm(o, hi, xh, False, False)
                        mm(o, hi, xl, False, False)
                        ins = mm(o, lo, xh, False, k == 1)
                    if m % 2:
                        ins.then_inc(down_done.sem, down_done.up())
                pe.wait_ge(down_done.sem, down_done.at(l, 4))
                pe.sem_inc(w_used.sem, w_used.up(2))

            sum_squares(DEPTH, 0).then_inc(ss_done.sem, 1)
            for n, b in enumerate((0, 2, 1, 3)):
                o = down[b]
                if n % 2 == 0:
                    pe.wait_ge(h_new.sem, h_new.at(DEPTH, 4 + 2 * n))
                for e in range(4):
                    t, k = b // 2, 4 * (b % 2) + e
                    ins = nc.tensor.transpose(o[:, P * e:P * e + P], hT[:, k, P * t:P * t + P], ident)
                ins.then_inc(fin_turned.sem, 1)

        @block.scalar
        def _(a):
            A = nc.scalar.activation

            def square(l, first, x_first, b):
                a.wait_ge(x_ready.sem, x_ready.at(l, x_first + b + 1))
                A(sq[:, 2 * b:2 * b + 2, :], xT[:, 2 * b:2 * b + 2, :], ACT.Square)\
                    .then_inc(sq_ready.sem, sq_ready.up())

            def squares(l, first, x_first):
                for b in range(4):
                    square(l, first, x_first, b)

            def root(l, n):
                a.wait_ge(ss_done.sem, ss_done.at(l, n))
                A(rstd[:, :], bO[:, 0:T], ACT.Sqrt, bias=kon[:, K_EPS:K_EPS + 1], scale=-1.0 / D)\
                    .then_inc(rms_ready.sem, rms_ready.up())

            def load_root():
                A(eps2[:, :], kon[:, K_EPS:K_EPS + 1], ACT.Sqrt)

            def copy_out(l, n, dst, func=ACT.Copy, scale=1.0):
                t, k = summed(n)
                a.wait_ge(t.sem, t.at(l, k))
                A(dst, unit(n), func, scale=scale).then_inc(unit_out[n % 2].sem, unit_out[n % 2].up())

            def split_hi(l, s, turn=0, times=1):
                i = PIECES[s][0]
                a.wait_ge(landed[i % RING].sem, chunk_at(l, i) + turn * 32)
                if kind_of(i) == "branch" and i < I_Y + 2:
                    a.wait_ge(upper_in.sem, upper_in.at(l, 16 * (i - I_Y + 1)))
                if kind_of(i) == "pair":
                    a.wait_ge(pair_in[i].sem, pair_in[i].at(l, 16))
                a.wait_ge(w_used.sem, w_used.at(l, s + 1 - SPLIT) + turn * TURN)
                src, dst = piece_from(s, wh)
                A(dst, src, ACT.Copy).then_inc(w_hi.sem, 1)
                w_hi.made += times

            def norm_hi(l, first):
                for k in range(KD):
                    a.wait_ge(h_new.sem, h_new.at(l, first + k + 1))
                    A(hh[:, k, :], hT[:, k, :], ACT.Copy).then_inc(h_hi.sem, h_hi.up())

            a.wait_ge(consts_in.sem, 16)
            a.wait_ge(x_turned.sem, 4)
            with a.Fori(0, DEPTH) as l:
                load_root()
                split_hi(l, 0)
                squares(l, 0, -4)
                split_hi(l, 1)
                a.wait_ge(par_turned.sem, par_turned.at(l, 3))
                A(par[:, :, :], bX[0][:, 0:3 * P].rearrange("p (n c) -> p n c", n=3), ACT.Copy)\
                    .then_inc(par_ready.sem, par_ready.up())
                root(l, 1)
                norm_hi(l, 0)
                split_hi(l, 2)
                split_hi(l, 3)
                a.wait_ge(par_ready.sem, par_ready.at(l, 1))
                A(s5p[:, 0, :], par[:, 0, A_ST:A_ST + ST], ACT.Exp).then_inc(step_exp.sem, step_exp.up())
                a.wait_ge(ang_ready.sem, ang_ready.at(l, 1))
                A(s5p[:, 3, :], s5p[:, 1, :], ACT.Exp).then_inc(mag_ready.sem, mag_ready.up())
                split_hi(l, 4)
                a.wait_ge(ang_ready.sem, ang_ready.at(l, 2))
                A(s5p[:, 4, :], s5p[:, 8, :], ACT.Sin)
                A(s5p[:, 5, :], s5p[:, 8, :], ACT.Sin, scale=0.5).then_inc(sin_ready.sem, sin_ready.up())
                for n, dst in enumerate((qr[:, 0:2, :], qr[:, 2:4, :], kr[:, 0:2, :], kr[:, 2:4, :],
                                         vn[:, :, :, :].rearrange("p t b c -> p t (b c)"))):
                    copy_out(l, n, dst)
                    split_hi(l, 5 + 2 * n)
                    split_hi(l, 6 + 2 * n)
                t, k = summed(5)
                a.wait_ge(t.sem, t.at(l, k))
                A(ng[:, :, :], pj[1][:, 0:NT * 3 * HEADS].rearrange("p (t c) -> p t c", t=NT), ACT.Tanh, scale=0.5)\
                    .then_inc(unit_out[1].sem, unit_out[1].up())
                split_hi(l, 15)
                split_hi(l, 16)
                copy_out(l, 6, uT[:, 0:2, :])
                split_hi(l, 17)
                copy_out(l, 7, uT[:, 2:4, :])
                split_hi(l, 18)

                def branch_hi(dst, src):
                    A(hh[:, dst, :], src, ACT.Copy).then_inc(b_hi.sem, b_hi.up())

                for q in range(SLOTS):
                    f = q // 2
                    if q == GELU:
                        a.wait_ge(y_used.sem, y_used.at(l, JC))
                        A(yT[:, :, :], yT[:, :, :], ACT.Gelu_apprx_tanh).then_inc(y_ready.sem, y_ready.up())
                    if q == OB_SPLIT:
                        a.wait_ge(ob_ready.sem, ob_ready.at(l, 4))
                        branch_hi(slice(4, 8), oB[:, :, :])
                    if q in OS_SPLIT:
                        n = OS_SPLIT[q]
                        a.wait_ge(os_ready.sem, os_ready.at(l, n + 1))
                        branch_hi(slice(2 * n, 2 * n + 2), oS[:, 2 * n:2 * n + 2, :])
                    if q in SPLIT_AT:
                        split_hi(l, SPLIT_AT[q])
                    if q in CMP_HID:
                        r = CMP_HID[q]
                        a.wait_ge(hid_done.sem, hid_done.at(l, r + 1))
                        A(hid[:, r, 0:2 * NC], (bA, bB)[r][:, 0:2 * NC], ACT.Gelu_apprx_tanh)\
                            .then_inc(hid_ready.sem, hid_ready.up())
                    if q == CMP_OUT:
                        a.wait_ge(kc_done.sem, kc_done.at(l, 1))
                        A(kc[:, 0:NC], bO[:, 0:NC], ACT.Copy).then_inc(kc_ready.sem, kc_ready.up())
                        a.wait_ge(kc_done.sem, kc_done.at(l, 2))
                        for r in range(0, P, 32):
                            ins = A(vc[r:r + NC, :], bB[r:r + NC, 64:64 + HD], ACT.Copy)
                        ins.then_inc(kc_ready.sem, kc_ready.up())
                    if q == CMP_S:
                        for n in range(4):
                            a.wait_ge(bc_turned.sem, bc_turned.at(l, n + 1))
                            src = (bX[0], bX[1], bY, bX[0])[n]
                            dst = (BL[:, 0], BL[:, 1], CL[:, 0], CL[:, 1])[n]
                            A(dst, src[:, :].rearrange("p (j c) -> p j c", j=JC), ACT.Copy)\
                                .then_inc(bc_ready.sem, bc_ready.up())
                    if q == CMP_S + 1:
                        a.wait_ge(cs_ready.sem, cs_ready.at(l, 1))
                        A(cP, cS, ACT.Exp, scale=SCALE).then_inc(ce_ready.sem, ce_ready.up())
                    if q in NSA_S:
                        n = NSA_S[q]
                        w = nsa_unit(n)[3]
                        a.wait_ge(s_max.sem, s_max.at(l, n + 1))
                        if n >= 2:
                            a.wait_ge(t_done.sem, t_done.at(l, n - 1))
                        for b in range(2):
                            ins = A(pr[:, n % 2, w * b:w * b + w], sc[:, n % 2, w * b:w * b + w], ACT.Exp,
                                    bias=nm[:, n % 2, b:b + 1], scale=SCALE, accum_out=sm[:, n % 2, b:b + 1])
                        ins.then_inc(s_exp.sem, s_exp.up())
                    if q in NSA_T:
                        n = NSA_T[q]
                        w = nsa_unit(n)[3]
                        a.wait_ge(t_done.sem, t_done.at(l, n + 1))
                        if n >= 2:
                            a.wait_ge(v_done.sem, v_done.at(l, n - 1))
                        A(pT[:, n % 2, 0:2 * w], bB[:, 0:2 * w], ACT.Copy).then_inc(t_ready.sem, t_ready.up())
                        if n == 0:
                            a.wait_ge(pc_done.sem, pc_done.at(l, 1))
                            A(pcT[:, :, :], bO[:, :].rearrange("p (i t) -> p i t", i=4), ACT.Copy)\
                                .then_inc(pc_ready.sem, pc_ready.up())
                    if q in SB_R:
                        h = SB_R[q]
                        a.wait_ge(r_done.sem, r_done.at(l, h + 1))
                        A(sbw[:, h % 3, :], (bA, bB)[h % 2][:, 0:384], ACT.Exp).then_inc(w_exp.sem, w_exp.up())
                    if q in SB_Z:
                        h = SB_Z[q]
                        a.wait_ge(z_done.sem, z_done.at(l, h + 1))
                        if h >= 3:
                            a.wait_ge(o_done.sem, o_done.at(l, h - 2))
                        A(sbw[:, h % 3, :], (bA, bB)[h % 2][:, 0:384], ACT.Abs).then_inc(z_abs.sem, z_abs.up())
                        a.wait_ge(z_abs.sem, z_abs.at(l, h + 1))
                        A(sbw[:, h % 3, :], sbw[:, h % 3, :], ACT.Exp, scale=-1.0).then_inc(z_exp.sem, z_exp.up())
                        a.wait_ge(z_exp.sem, z_exp.at(l, h + 1))
                        A(sbw[:, h % 3, :], sbw[:, h % 3, :], ACT.Ln, bias=1.0).then_inc(z_ln.sem, z_ln.up())
                    if q % 2:
                        kind, *at = FILL[f]
                        if kind == "sbq":
                            copy_out(l, U_FILL + f, sbq[:, 2 * at[0]:2 * at[0] + 2, :], scale=SCALE)
                        elif kind == "glu":
                            o = oS[:, 2 * at[0]:2 * at[0] + 2, :]
                            copy_out(l, U_FILL + f, o, ACT.Tanh, 0.5)
                        elif kind == "gate":
                            if q == ON_SPLIT:
                                a.wait_ge(w_used.sem, w_used.at(l, S_Y))
                                for k in range(JC):
                                    branch_hi(slice(k, k + 1), oN[:, k:k + 1, :])
                            b, i = at
                            copy_out(l, U_FILL + f, gate[:, KD * b + 2 * i:KD * b + 2 * i + 2, :], ACT.Tanh, 0.5)
                split_hi(l, S_Y + 10)
                for s in range(S_Y + 11, S_OUT + 3):
                    split_hi(l, s)
                for q in range(4):
                    a.wait_ge(m_ready.sem, m_ready.at(l, 5 + q))
                    branch_hi(slice(2 * q, 2 * q + 2), mT[:, 2 * q:2 * q + 2, :])
                load_root()
                for b in range(4):
                    split_hi(l, S_OUT + 3 + 2 * b)
                    if b < 3:
                        split_hi(l, S_OUT + 4 + 2 * b)
                    square(l, 4, 0, b)
                split_hi(l, S_FFN + 2)
                root(l, 2)
                norm_hi(l, KD)

                def conv(n, e, tile, turn=0, times=1):
                    t, k = summed(n)
                    a.wait_ge(t.sem, t.at(l, k) + turn * TURN)
                    for m in range(2):
                        ins = A(cv[:, e, T * m:T * m + T], pj[n % 2][:, T * m:T * m + T], ACT.Identity,
                                bias=par[:, 2, bass.ds(tile + (C_B + m), 1)],
                                scale=par[:, 2, bass.ds(tile + (C_W2 + m), 1)])
                    ins.then_inc(cv_last.sem, 1)
                    cv_last.made += times

                def ffn_step(c, cc, turn=0, times=1):
                    s = ffn_piece(cc)
                    split_hi(l, s + 3, turn, times)
                    if cc:
                        split_hi(l, s + 4, turn, times)
                        a.wait_ge(a_ready.sem, a_ready.at(l, cc) + turn * 2)
                    conv(U_FFN + 2 * cc, 0, c * 2, turn, times)
                    if cc:
                        split_hi(l, s + 5, turn, times)
                    split_hi(l, s + (6 if cc else 4), turn, times)
                    if not cc:
                        split_hi(l, s + 5)
                    conv(U_FFN + 2 * cc + 1, 1, c * 2 + FT, turn, times)
                    n = U_FFN + 2 * cc
                    a.wait_ge(unit_out[n % 2].sem, unit_out[n % 2].at(l, n // 2 + 1) + turn * 2)
                    A(cv[:, 0, :], cv[:, 0, :], ACT.Silu).then_inc(sg_ready.sem, 1)
                    sg_ready.made += times
                    if cc:
                        split_hi(l, s + 7, turn, times)
                    if s + 8 < len(PIECES):
                        split_hi(l, s + (8 if cc else 6), turn, times)
                    a.wait_ge(a_ready.sem, a_ready.at(l, cc + 1) + turn * 2)
                    if cc:
                        a.wait_ge(w_used.sem, w_used.at(l, s + 6) + turn * TURN)
                    A(ah[:, :], aT[:, cc % 2, :], ACT.Copy).then_inc(a_hi.sem, 1)
                    a_hi.made += times

                ffn_step(0, 0)
                ffn_step(1, 1)
                with a.Fori(0, LOOP) as j:
                    ffn_step(j * 2 + 2, 2, j, LOOP)
                    ffn_step(j * 2 + 3, 3, j, LOOP)
                ffn_step(STEPS - 1, STEPS - 1)
            load_root()
            squares(DEPTH, 0, -4)
            sq_ready.made -= 4
            root(DEPTH, 1)
            rms_ready.made -= 1

        @block.vector
        def _(v):
            TT, TS, STT = nc.vector.tensor_tensor, nc.vector.tensor_scalar, nc.vector.scalar_tensor_tensor

            nc.vector.memset(cE[:, :, :], 0.0)
            for st in (stA, stB, stC):
                nc.vector.memset(st[:, :], 0.0).then_inc(setup.sem, 1)
            v.sem_inc(w_lo.sem, w_lo.start)
            v.sem_inc(w_used.sem, w_used.start)
            v.sem_inc(params_free.sem, 1)
            v.sem_inc(unit_out[0].sem, 1)
            v.sem_inc(unit_out[1].sem, 1)
            v.sem_inc(a_split.sem, a_split.start)
            for b, o in enumerate(down):
                v.wait_ge(x_turned.sem, b + 1)
                nc.vector.tensor_copy(xT[:, 2 * b:2 * b + 2, :], o[:, :].rearrange("p (k t) -> p k t", k=2))\
                    .then_inc(x_ready.sem, 1)

            def split_lo(l, s, turn=0, times=1):
                v.wait_ge(w_hi.sem, w_hi.at(l, s + 1) + turn * TURN)
                src, dst = piece_from(s, wl)
                hi = piece_from(s, wh)[1]
                TT(dst, src, hi.bitcast(F32), ALU.subtract).then_inc(w_lo.sem, 1)
                w_lo.made += times

            def norm(l, n, gain, split=True):
                v.wait_ge(rms_ready.sem, rms_ready.at(l, n))
                nc.vector.reciprocal(rstd[:, :], rstd[:, :]).then_inc(dve_step.sem, dve_step.up())
                v.wait_ge(dve_step.sem, dve_step.last(l))

                def lo(k):
                    v.wait_ge(h_hi.sem, h_hi.at(l, KD * (n - 1) + k + 1))
                    TT(hl[:, k, :], hT[:, k, :], hh[:, k, :].bitcast(F32), ALU.subtract)\
                        .then_inc(h_ready[0].sem, h_ready[0].up())

                for k in range(KD):
                    STT(hT[:, k, :], xT[:, k, :], par[:, 0, gain + k:gain + k + 1], rstd[:, :], ALU.mult, ALU.mult)\
                        .then_inc(h_new.sem, h_new.up())
                    if split and k % 2:
                        lo(k - 1)

            def gate_unit(b, i):
                return U_FILL + FILL.index(("gate", b, i))

            def merge(l, n, b, q):
                u = gate_unit(b, q)
                v.wait_ge(unit_out[u % 2].sem, unit_out[u % 2].at(l, u // 2 + 1))
                t, k = summed(n)
                v.wait_ge(t.sem, t.at(l, k))
                if b == 1:
                    dst = mT[:, 2 * q:2 * q + 2, :]
                else:
                    k = q if b == 2 else 4 + q
                    if k >= 2:
                        v.wait_ge(m_ready.sem, m_ready.at(l, k - 1))
                    dst = yt[:, k % 2, :].rearrange("p (m t) -> p m t", m=2)
                STT(dst, gate[:, KD * b + 2 * q:KD * b + 2 * q + 2, :], 1.0, unit(n),
                    ALU.add, ALU.mult).then_inc(unit_out[n % 2].sem, unit_out[n % 2].up())

            with v.Fori(0, DEPTH) as l:
                v.wait_ge(rows_in.sem, rows_in.at(l, 16 * 17))
                nc.vector.tensor_copy(
     stA[A_ST:A_ST + ST, :].rearrange("t (w p) -> t w p", w=2),
     lstep[A_ST:A_ST + ST, :].rearrange("t (w o) -> t w o", o=1).broadcast_to([ST, 2, HD]))\
         .then_inc(step_row.sem, step_row.up())
                split_lo(l, 0)
                split_lo(l, 1)
                v.wait_ge(par_ready.sem, par_ready.at(l, 1))
                norm(l, 1, A_MIX)
                split_lo(l, 2)

                def p(n):
                    return s5p[:, n, :]

                lr, li = par[:, 0, A_LR:A_LR + ST], par[:, 0, A_LI:A_LI + ST]
                step, lrs, th, mag, sn, sh, kk, t1, r, cs, ar, ai, den, rden, nr, fr, fi, t2 = map(p, range(18))
                v.wait_ge(step_exp.sem, step_exp.at(l, 1))
                TT(lrs, lr, step, ALU.mult)
                TT(th, li, step, ALU.mult).then_inc(ang_ready.sem, ang_ready.up())
                v.wait_ge(ang_ready.sem, ang_ready.at(l, 1))
                TS(kk, th, 1.0 / TWO_PI, MAGIC, ALU.mult, ALU.add).then_inc(dve_step.sem, dve_step.up())
                v.wait_ge(dve_step.sem, dve_step.last(l))
                TS(kk, kk, -MAGIC, None, ALU.add).then_inc(dve_step.sem, dve_step.up())
                v.wait_ge(dve_step.sem, dve_step.last(l))
                src = th
                for part in PI_PARTS:
                    STT(r, kk, -part, src, ALU.mult, ALU.add).then_inc(dve_step.sem, dve_step.up())
                    v.wait_ge(dve_step.sem, dve_step.last(l))
                    src = r
                TS(r, r, 3.1415925, -3.1415925, ALU.min, ALU.max).then_inc(ang_ready.sem, ang_ready.up())
                split_lo(l, 3)
                split_lo(l, 4)
                v.wait_ge(sin_ready.sem, sin_ready.at(l, 1))
                v.wait_ge(mag_ready.sem, mag_ready.at(l, 1))
                TT(cs, sh, sh, ALU.mult).then_inc(dve_step.sem, dve_step.up())
                v.wait_ge(dve_step.sem, dve_step.last(l))
                TS(cs, cs, -2.0, 1.0, ALU.mult, ALU.add).then_inc(dve_step.sem, dve_step.up())
                v.wait_ge(dve_step.sem, dve_step.last(l))
                TT(ar, mag, cs, ALU.mult)
                TT(ai, mag, sn, ALU.mult)
                TT(den, lr, lr, ALU.mult)
                TT(t1, li, li, ALU.mult).then_inc(dve_step.sem, dve_step.up())
                v.wait_ge(dve_step.sem, dve_step.last(l))
                TS(nr, ar, -1.0, None, ALU.add)
                TT(den, den, t1, ALU.add).then_inc(dve_step.sem, dve_step.up())
                v.wait_ge(dve_step.sem, dve_step.last(l))
                TT(t1, nr, lr, ALU.mult)
                TT(t2, ai, li, ALU.mult)
                nc.vector.reciprocal(rden, den).then_inc(dve_step.sem, dve_step.up())
                v.wait_ge(dve_step.sem, dve_step.last(l))
                TT(fr, t1, t2, ALU.add).then_inc(dve_step.sem, dve_step.up())
                v.wait_ge(dve_step.sem, dve_step.last(l))
                TT(fr, fr, rden, ALU.mult).then_inc(dve_step.sem, dve_step.up())
                v.wait_ge(dve_step.sem, dve_step.last(l))
                TT(t1, ai, lr, ALU.mult)
                TT(t2, nr, li, ALU.mult).then_inc(dve_step.sem, dve_step.up())
                v.wait_ge(dve_step.sem, dve_step.last(l))
                TT(fi, t1, t2, ALU.subtract).then_inc(dve_step.sem, dve_step.up())
                v.wait_ge(dve_step.sem, dve_step.last(l))
                TT(fi, fi, rden, ALU.mult).then_inc(dve_step.sem, dve_step.up())
                v.wait_ge(dve_step.sem, dve_step.last(l))
                TC, TN = tab[:, 0], tab[:, 1]
                nc.vector.tensor_copy(TC[:, :, 0], cs)
                nc.vector.tensor_copy(TN[:, :, 0], sn).then_inc(tab_d.sem, tab_d.up())
                v.wait_ge(tab_d.sem, tab_d.at(l, 1))

                split_lo(l, 5)
                v.wait_ge(mats_in.sem, mats_in.at(l, 16 * 6))

                def w3(ap):
                    return ap.rearrange("p (t o) -> p t o", o=1).broadcast_to([P, ST, GCH])

                TT(bb[:, 0], bnat[:, 0], w3(fr), ALU.mult)
                TT(bbt[:, 0], bnat[:, 1], w3(fi), ALU.mult)
                TT(bb[:, 1], bnat[:, 1], w3(fr), ALU.mult)
                TT(bbt[:, 1], bnat[:, 0], w3(fi), ALU.mult).then_inc(dve_step.sem, dve_step.up())
                v.wait_ge(dve_step.sem, dve_step.last(l))
                TT(bb[:, 0], bb[:, 0], bbt[:, 0], ALU.subtract)
                TT(bb[:, 1], bb[:, 1], bbt[:, 1], ALU.add).then_inc(dve_step.sem, dve_step.up())
                v.wait_ge(dve_step.sem, dve_step.last(l))
                v.wait_ge(bx_clear.sem, bx_clear.at(l, 1))
                for c in range(2):
                    nc.vector.tensor_copy(bx[0:STATES, c, :, 0:GCH], bb[0:STATES, c])
                    nc.vector.tensor_copy(bx[STATES:P, c, :, GCH:2 * GCH], bb[STATES:P, c])\
                        .then_inc(bx_ready.sem, bx_ready.up())
                split_lo(l, 6)
                split_lo(l, 7)
                for e in range(7):
                    n = 1 << e
                    if e:
                        v.wait_ge(tab_p.sem, tab_p.at(l, e))
                    cn = TC[:, :, n - 1:n].broadcast_to([P, ST, n])
                    nn = TN[:, :, n - 1:n].broadcast_to([P, ST, n])
                    TT(TC[:, :, n:2 * n], TC[:, :, 0:n], cn, ALU.mult)
                    TT(tmp_d[:, :, 0:n], TN[:, :, 0:n], nn, ALU.mult).then_inc(dve_step.sem, dve_step.up())
                    v.wait_ge(dve_step.sem, dve_step.last(l))
                    TT(TC[:, :, n:2 * n], TC[:, :, n:2 * n], tmp_d[:, :, 0:n], ALU.subtract)\
                        .then_inc(tab_d.sem, tab_d.up())
                    if e in (1, 3, 4, 5, 6):
                        split_lo(l, {1: 8, 3: 9, 4: 10, 5: 11, 6: 12}[e])
                    v.wait_ge(tab_d.sem, tab_d.at(l, e + 2))

                split_lo(l, 13)
                sin_b = kon[:, K_SIN:K_SIN + T].rearrange("p (o t) -> p o t", o=1)
                for n, (o, dst) in enumerate(((bO, kr[:, 0:2, :]), (bX[1], kr[:, 2:3, :]),
                                              (bA, qr[:, 0:2, :]), (bB, qr[:, 2:4, :]))):
                    v.wait_ge(rot_done.sem, rot_done.at(l, n + 1))
                    if n:
                        v.wait_ge(rot_ready.sem, rot_ready.at(l, n))
                    m = dst.shape[1]
                    r2 = rt[:, 0:T * m].rearrange("p (m t) -> p m t", m=m)
                    TT(r2, o[:, 0:T * m].rearrange("p (m t) -> p m t", m=m), sin_b.broadcast_to([P, m, T]), ALU.mult)\
                        .then_inc(dve_step.sem, dve_step.up())
                    v.wait_ge(dve_step.sem, dve_step.last(l))
                    v.wait_ge(rot_cos.sem, rot_cos.at(l, n + 1))
                    TT(dst, dst, r2, ALU.add).then_inc(rot_ready.sem, rot_ready.up())
                    if n in (1, 3):
                        split_lo(l, 14 + n // 2)
                v.wait_ge(rot_ready.sem, rot_ready.at(l, 4))
                v.wait_ge(unit_out[1].sem, unit_out[1].at(l, 2))

                k_pos = par[:, 0, A_PK:A_PK + L2], par[:, 0, A_PKS:A_PKS + L2]
                v_pos = par[:, 0, A_PV:A_PV + L2], par[:, 1, B_PVS:B_PVS + L2]
                for c, (src, own, sw) in enumerate(((kr[:, 0, :], *k_pos), (kr[:, 3, :], *v_pos))):
                    rows = src.rearrange("p (m w) -> p m w", w=CSTR)
                    for g in range(2):
                        for w in range(2):
                            pos = (own if g == w else sw)[HD * g:HD * g + HD, :]
                            for b in range(2):
                                h8 = L2 // 2
                                ins = TT(blk[HD * w:HD * w + HD, c, g, :, h8 * b:h8 * b + h8],
                                         rows[HD * g:HD * g + HD, b:b + NC, w::2],
                                         pos[:, h8 * b:h8 * b + h8].rearrange("p (o a) -> p o a", o=1)
                                         .broadcast_to([HD, NC, h8]), ALU.add)
                    ins.then_inc(blk_ready.sem, blk_ready.up())
                    split_lo(l, 16 + c)
                split_lo(l, 18)

                def branch_lo(dst, src):
                    v.wait_ge(b_hi.sem, b_hi.at(l, b_split.made + 1))
                    TT(hl[:, dst, :], src, hh[:, dst, :].bitcast(F32), ALU.subtract)\
                        .then_inc(b_split.sem, b_split.up())

                v.wait_ge(unit_out[1].sem, unit_out[1].at(l, 3))
                TS(ng[:, :, :], ng[:, :, :], 0.5, 0.5, ALU.mult, ALU.add).then_inc(dve_step.sem, dve_step.up())
                v.wait_ge(dve_step.sem, dve_step.last(l))

                def cmp_softmax():
                    v.wait_ge(cs_done.sem, cs_done.at(l, 1))

                    def per_key(n):
                        return cm[:, n, :].rearrange("p (n o) -> p n o", o=1).broadcast_to([P, NSA, NC])

                    cmask = kon[:, K_CMASK:K_CMASK + 16 * NT].rearrange("p (o t c) -> p o t c", o=1, t=NT)
                    for s in range(2):
                        raw = (bA, bO)[s][:, 0:8 * NSA].rearrange("p (i t c) -> p i t c", i=4, c=16)
                        ins = TT(cS.rearrange("p (i s t) c -> p i s t c", i=4, s=2)[:, :, s, :, :],
                                 raw[:, :, :, 0:NC], cmask[:, :, :, 0:NC].broadcast_to([P, 4, NT, NC]), ALU.add)
                    ins.then_inc(dve_step.sem, dve_step.up())
                    v.wait_ge(dve_step.sem, dve_step.last(l))
                    nc.vector.tensor_reduce(cm[:, 0, :], cS, AX, ALU.max).then_inc(dve_step.sem, dve_step.up())
                    v.wait_ge(dve_step.sem, dve_step.last(l))
                    TS(cm[:, 0, :], cm[:, 0, :], 0.1 * NEG, None, ALU.max).then_inc(dve_step.sem, dve_step.up())
                    v.wait_ge(dve_step.sem, dve_step.last(l))
                    TT(cS, cS, per_key(0), ALU.subtract).then_inc(cs_ready.sem, cs_ready.up())
                    v.wait_ge(ce_ready.sem, ce_ready.at(l, 1))
                    nc.vector.tensor_reduce(cm[:, 1, :], cP, AX, ALU.add).then_inc(dve_step.sem, dve_step.up())
                    v.wait_ge(dve_step.sem, dve_step.last(l))
                    TS(cm[:, 1, :], cm[:, 1, :], 1e-30, None, ALU.max).then_inc(dve_step.sem, dve_step.up())
                    v.wait_ge(dve_step.sem, dve_step.last(l))
                    nc.vector.reciprocal(cm[:, 1, :], cm[:, 1, :]).then_inc(dve_step.sem, dve_step.up())
                    v.wait_ge(dve_step.sem, dve_step.last(l))
                    g0 = ng[:, :, :].rearrange("p t (s i b) -> p i s t b", s=2, b=3)
                    TT(cm[:, 2, :].rearrange("p (i s t) -> p i s t", i=4, s=2),
                       cm[:, 1, :].rearrange("p (i s t) -> p i s t", i=4, s=2), g0[:, :, :, :, 0], ALU.mult)\
                           .then_inc(dve_step.sem, dve_step.up())
                    v.wait_ge(dve_step.sem, dve_step.last(l))
                    TT(cP, cP, per_key(2), ALU.mult).then_inc(cp_ready.sem, cp_ready.up())

                def nsa_max(n):
                    t, w = nsa_unit(n)[2:]
                    v.wait_ge(s_done.sem, s_done.at(l, n + 1))
                    if n >= 2:
                        v.wait_ge(s_exp.sem, s_exp.at(l, n - 1))
                    v.sem_inc(passed.sem, 1)
                    for b in range(2):
                        ins = nc.vector.tensor_tensor_reduce(
                            sc[:, n % 2, w * b:w * b + w], bA[:, w * b:w * b + w],
                            kon[:, K_MASK + T - w:K_MASK + T], 1.0, 3.0 * NEG, ALU.add, ALU.max,
                            mx[:, n % 2, b:b + 1])
                    ins.then_inc(dve_step.sem, dve_step.up())
                    v.wait_ge(dve_step.sem, dve_step.last(l))
                    TS(nm[:, n % 2, :], mx[:, n % 2, :], -SCALE, None, ALU.mult).then_inc(s_max.sem, s_max.up())

                def nsa_sum(n):
                    i, s, t, w = nsa_unit(n)
                    v.wait_ge(s_exp.sem, s_exp.at(l, n + 1))
                    if n >= 2:
                        v.wait_ge(s_prob.sem, s_prob.at(l, n - 1))
                    TS(rc[:, n % 2, :], sm[:, n % 2, :], 1e-30, None, ALU.max).then_inc(dve_step.sem, dve_step.up())
                    v.wait_ge(dve_step.sem, dve_step.last(l))
                    nc.vector.reciprocal(rc[:, n % 2, :], rc[:, n % 2, :]).then_inc(dve_step.sem, dve_step.up())
                    v.wait_ge(dve_step.sem, dve_step.last(l))
                    c = 3 * (4 * s + i) + 1
                    TT(rg[:, n % 2, :], rc[:, n % 2, :], ng[:, t, c:c + 2], ALU.mult).then_inc(s_rec.sem, s_rec.up())

                def halves(ap, m=4):
                    return ap.rearrange("p (m t) -> p m t", m=m)

                def s5_turn(s):
                    v.wait_ge(x5_done.sem, x5_done.at(l, s + 1))
                    if s:
                        v.wait_ge(h5_ready.sem, h5_ready.at(l, s))
                    for c in range(2):
                        ins = TT(halves(s5a[:, c, :]), halves(bX[s % 2][:, :]),
                                 tab[:, c, s:s + 1, :].broadcast_to([P, 4, P]), ALU.mult)
                    ins.then_inc(x5_used.sem, x5_used.up())

                def s5_scan(s):
                    v.wait_ge(x5_turned.sem, x5_turned.at(l, s + 1))
                    decay = mag[:, s:s + 1].broadcast_to([P, P])
                    cn, nn = tab[:, 0, s, P - 1:P], tab[:, 1, s, P - 1:P]
                    for b in range(2):
                        for c in range(2):
                            g = s5x[:, c, P * b:P * b + P]
                            ins = nc.vector.tensor_tensor_scan(g, decay, g, s5i[:, 2 + c:3 + c] if b else 0.0,
                                                               ALU.mult, ALU.add)
                        if b:
                            break
                        ins.then_inc(dve_step.sem, dve_step.up())
                        v.wait_ge(dve_step.sem, dve_step.last(l))
                        gr, gi = s5x[:, 0, P - 1:P], s5x[:, 1, P - 1:P]
                        TT(s5i[:, 0:1], gi, nn, ALU.mult)
                        TT(s5i[:, 1:2], gi, cn, ALU.mult).then_inc(dve_step.sem, dve_step.up())
                        v.wait_ge(dve_step.sem, dve_step.last(l))
                        STT(s5i[:, 2:3], gr, cn, s5i[:, 0:1], ALU.mult, ALU.subtract)
                        STT(s5i[:, 3:4], gr, nn, s5i[:, 1:2], ALU.mult, ALU.add).then_inc(dve_step.sem, dve_step.up())
                        v.wait_ge(dve_step.sem, dve_step.last(l))
                    ins.then_inc(g5_ready.sem, g5_ready.up())

                for q in range(SLOTS):
                    f = q // 2
                    if q == OB_SPLIT:
                        branch_lo(slice(4, 8), oB[:, :, :])
                    if q in OS_SPLIT:
                        n = OS_SPLIT[q]
                        u = U_GLU + n
                        v.wait_ge(unit_out[u % 2].sem, unit_out[u % 2].at(l, u // 2 + 1))
                        o = oS[:, 2 * n:2 * n + 2, :]
                        TS(o, o, 0.5, 0.5, ALU.mult, ALU.add).then_inc(dve_step.sem, dve_step.up())
                        v.wait_ge(dve_step.sem, dve_step.last(l))
                        TT(o, o, yT[:, 2 * n:2 * n + 2, :], ALU.mult).then_inc(os_ready.sem, os_ready.up())
                        branch_lo(slice(2 * n, 2 * n + 2), o)
                    if q in SPLIT_AT:
                        split_lo(l, SPLIT_AT[q])
                    if q == CMP_S + 1:
                        cmp_softmax()
                    if q in NSA_S:
                        nsa_max(NSA_S[q])
                    if q - 1 in SB_Z:
                        h = SB_Z[q - 1]
                        v.wait_ge(z_ln.sem, z_ln.at(l, h + 1))
                        if h >= 2:
                            v.wait_ge(r_done.sem, r_done.at(l, h - 1))
                        STT(sbp[:, h % 2, :], (bA, bB)[h % 2][:, 0:384], 0.0, sbw[:, h % 3, :],
                            ALU.max, ALU.add).then_inc(z_sp.sem, z_sp.up())
                    if q in S5_X:
                        s5_turn(S5_X[q])
                    if q == ON_SPLIT:
                        for k in range(JC):
                            branch_lo(slice(k, k + 1), oN[:, k:k + 1, :])
                    if q - 1 in S5_X:
                        s5_scan(S5_X[q - 1])
                    if q in NSA_S:
                        nsa_sum(NSA_S[q])
                    if q in NSA_V and NSA_V[q] % 4 == 3:
                        n = NSA_V[q]
                        v.wait_ge(v_done.sem, v_done.at(l, n + 1))
                        nc.vector.tensor_copy(oN[:, n // 4, :], bO[:, 0:T]).then_inc(on_ready.sem, on_ready.up())
                    if q in SB_O and SB_O[q] % 2:
                        h = SB_O[q]
                        v.wait_ge(o_done.sem, o_done.at(l, h + 1))
                        nc.vector.tensor_copy(oB[:, h // 2, :], bO[:, 0:T]).then_inc(ob_ready.sem, ob_ready.up())
                    if q in S5_Y and S5_Y[q] % 4 == 3:
                        j = S5_Y[q] // 4
                        v.wait_ge(y_done.sem, y_done.at(l, 4 * j + 4))
                        STT(yT[:, j, :], uT[:, j, :], par[:, 0, A_D + j:A_D + j + 1],
                            bY[:, 0:T], ALU.mult, ALU.add).then_inc(y_used.sem, y_used.up())
                    if q % 2:
                        kind, *at = FILL[f]
                        n = U_FILL + f
                        if kind in ("sbk", "sbv"):
                            t, k = summed(n)
                            v.wait_ge(t.sem, t.at(l, k))
                            dst = (sbk[:, 2 * at[0]:2 * at[0] + 2, :] if kind == "sbk"
                                   else sbv[:, :, T * at[0]:T * at[0] + T])
                            nc.vector.tensor_copy(dst, unit(n)).then_inc(unit_out[n % 2].sem, unit_out[n % 2].up())
                        elif kind == "y":
                            merge(l, n, *at)

                split_lo(l, S_Y + 10)
                for q in range(4):
                    split_lo(l, S_Y + 11 + q)
                    merge(l, U_Y + q, 0, q)
                for q in range(4):
                    branch_lo(slice(2 * q, 2 * q + 2), mT[:, 2 * q:2 * q + 2, :])
                for q in range(4):
                    split_lo(l, S_OUT + 3 + 2 * q)
                    if q < 3:
                        split_lo(l, S_OUT + 4 + 2 * q)
                    n = U_OUT + q
                    t, k = summed(n)
                    v.wait_ge(t.sem, t.at(l, k))
                    xq = xT[:, 2 * q:2 * q + 2, :]
                    STT(xq, unit(n), 0.5, xq, ALU.mult, ALU.add).then_inc(unit_out[n % 2].sem, unit_out[n % 2].up())
                    x_ready.made += 1
                    v.wait_ge(unit_out[n % 2].sem, unit_out[n % 2].at(l, n // 2 + 1))
                    v.sem_inc(x_ready.sem, 1)
                split_lo(l, S_FFN + 2)
                norm(l, 2, A_FFN)

                def taps(n, e, tile, turn=0, times=1):
                    u = unit_out[n % 2]
                    v.wait_ge(cv_last.sem, cv_last.at(l, n - U_FFN + 1) + turn * 4)
                    for back, col in ((1, B_W1), (2, B_W0)):
                        for m in range(2):
                            dst = cv[:, e, T * m + back:T * m + T]
                            ins = STT(dst, pj[n % 2][:, T * m:T * m + T - back],
                                      par[:, 1, bass.ds(tile + (col + m), 1)], dst, ALU.mult, ALU.add)
                        if back == 1:
                            ins.then_inc(cv_mid.sem, 1)
                            v.wait_ge(cv_mid.sem, cv_mid.at(l, n - U_FFN + 1) + turn * 4)
                        else:
                            ins.then_inc(u.sem, 1)
                    cv_mid.made += times
                    u.made += times

                def ffn_step(c, cc, turn=0, times=1):
                    s = ffn_piece(cc)
                    split_lo(l, s + 3, turn, times)
                    if cc:
                        split_lo(l, s + 4, turn, times)
                    taps(U_FFN + 2 * cc, 0, c * 2, turn, times)
                    if cc:
                        split_lo(l, s + 5, turn, times)
                    split_lo(l, s + (6 if cc else 4), turn, times)
                    if not cc:
                        split_lo(l, s + 5)
                    taps(U_FFN + 2 * cc + 1, 1, c * 2 + FT, turn, times)
                    if cc:
                        split_lo(l, s + 7, turn, times)
                    if s + 8 < len(PIECES):
                        split_lo(l, s + (8 if cc else 6), turn, times)
                    v.wait_ge(a_hi.sem, a_hi.at(l, cc + 1) + turn * 2)
                    TT(al[:, :], aT[:, cc % 2, :], ah[:, :].bitcast(F32), ALU.subtract).then_inc(a_split.sem, 1)
                    a_split.made += times

                ffn_step(0, 0)
                ffn_step(1, 1)
                with v.Fori(0, LOOP) as j:
                    ffn_step(j * 2 + 2, 2, j, LOOP)
                    ffn_step(j * 2 + 3, 3, j, LOOP)
                ffn_step(STEPS - 1, STEPS - 1)
                for b, o in enumerate(down):
                    v.wait_ge(down_done.sem, down_done.at(l, b + 1))
                    xq = xT[:, 2 * b:2 * b + 2, :]
                    TT(xq, xq, o[:, :].rearrange("p (k t) -> p k t", k=2), ALU.add)\
                        .then_inc(x_ready.sem, x_ready.up())

            saved = dve_step.made, h_new.made
            dve_step.made = 0
            norm(DEPTH, 1, A_FIN, split=False)
            dve_step.made, h_new.made = saved
            for n, b in enumerate((0, 2, 1, 3)):
                o = down[b]
                t, k = b // 2, 4 * (b % 2)
                v.wait_ge(fin_turned.sem, n + 1)
                nc.vector.tensor_copy(mT[:, 4 * t + k // 2:4 * t + k // 2 + 2, :],
                                      o[:, :].rearrange("p (k t) -> p k t", k=2)).then_inc(fin_ready.sem, 1)

        @block.gpsimd
        def _(g):
            TT = nc.gpsimd.tensor_tensor

            def norm_lo(l, first):
                for k in range(1, KD, 2):
                    g.wait_ge(h_hi.sem, h_hi.at(l, first + k + 1))
                    TT(hl[:, k, :], hT[:, k, :], hh[:, k, :].bitcast(F32), ALU.subtract)\
                        .then_inc(h_ready[1].sem, h_ready[1].up())

            with g.Fori(0, DEPTH) as l:
                nc.gpsimd.memset(bx, 0.0).then_inc(bx_clear.sem, bx_clear.up())
                g.wait_ge(mats_in.sem, mats_in.at(l, 16 * 6))
                for c, mask in enumerate((K_PAR, K_NPAR)):
                    for w in range(2):
                        m = kon[:, mask + w:mask + w + 1].rearrange("p (a b) -> p a b", a=1)
                        ins = TT(cx[:, c, :, STATES * w:STATES * w + STATES], cnat[:, c],
                                 m.broadcast_to([P, JC, STATES]), ALU.mult)
                    ins.then_inc(cx_ready.sem, cx_ready.up())
                norm_lo(l, 0)
                TC, TN = tab[:, 0], tab[:, 1]
                for e in range(7):
                    n = 1 << e
                    g.wait_ge(tab_d.sem, tab_d.at(l, e + 1))
                    if e:
                        g.wait_ge(tab_p.sem, tab_p.at(l, e))
                    cn = TC[:, :, n - 1:n].broadcast_to([P, ST, n])
                    nn = TN[:, :, n - 1:n].broadcast_to([P, ST, n])
                    TT(TN[:, :, n:2 * n], TN[:, :, 0:n], cn, ALU.mult)
                    TT(tmp_p[:, :, 0:n], TC[:, :, 0:n], nn, ALU.mult).then_inc(pool_step.sem, pool_step.up())
                    g.wait_ge(pool_step.sem, pool_step.at(l, pool_step.made))
                    TT(TN[:, :, n:2 * n], TN[:, :, n:2 * n], tmp_p[:, :, 0:n], ALU.add)\
                        .then_inc(tab_p.sem, tab_p.up())
                cos_b = kon[:, K_COS:K_COS + T].rearrange("p (o t) -> p o t", o=1)
                for n, dst in enumerate((kr[:, 0:2, :], kr[:, 2:3, :], qr[:, 0:2, :], qr[:, 2:4, :])):
                    g.wait_ge(rot_done.sem, rot_done.at(l, n + 1))
                    TT(dst, dst, cos_b.broadcast_to([P, dst.shape[1], T]), ALU.mult)\
                        .then_inc(rot_cos.sem, rot_cos.up())

                def add_merged(k, n):
                    g.wait_ge(unit_out[n % 2].sem, unit_out[n % 2].at(l, n // 2 + 1))
                    if k >= 4:
                        g.wait_ge(m_ready.sem, m_ready.at(l, k - 3))
                    m = mT[:, 2 * (k % 4):2 * (k % 4) + 2, :]
                    TT(m, m, yt[:, k % 2, :].rearrange("p (m t) -> p m t", m=2), ALU.add)\
                        .then_inc(m_ready.sem, m_ready.up())

                def s5_turn(s):
                    g.wait_ge(x5_used.sem, x5_used.at(l, s + 1))
                    c, n = s5a[:, 0, :], s5a[:, 1, :]
                    TT(s5x[:, 0, :], c[:, 0:T], n[:, T:2 * T], ALU.add)
                    TT(s5x[:, 1, :], c[:, T:2 * T], n[:, 0:T], ALU.subtract).then_inc(x5_turned.sem, x5_turned.up())

                def s5_back(s):
                    g.wait_ge(g5_ready.sem, g5_ready.at(l, s + 1))
                    gs = s5x[:, :, :].rearrange("p c (b t) -> p (c b) t", b=2)
                    for c in range(2):
                        ins = TT(s5a[:, c, :].rearrange("p (m t) -> p m t", m=4), gs,
                                 tab[:, c, s:s + 1, :].broadcast_to([P, 4, P]), ALU.mult)
                    ins.then_inc(pool_step.sem, pool_step.up())
                    g.wait_ge(pool_step.sem, pool_step.at(l, pool_step.made))
                    if s >= 2:
                        g.wait_ge(y_done.sem, y_done.at(l, s - 1))
                    c, n = s5a[:, 0, :], s5a[:, 1, :]
                    TT(s5h[:, s % 2, 0, :], c[:, 0:T], n[:, T:2 * T], ALU.subtract)
                    TT(s5h[:, s % 2, 1, :], c[:, T:2 * T], n[:, 0:T], ALU.add).then_inc(h5_ready.sem, h5_ready.up())

                def diagonal(ap):
                    d = ap.rearrange("p (b t) -> p b t", b=3)[:, 0:3:2, :]
                    g.sem_inc(passed.sem, 1)
                    return nc.gpsimd.affine_select(out=d, in_=d, pattern=[[0, 2], [1, P]], compare_op=ALU.is_gt,
                                                   fill=0.0, base=0, channel_multiplier=-1)

                for q in range(SLOTS):
                    f = q // 2
                    if q - 1 in SB_Z:
                        h = SB_Z[q - 1]
                        g.wait_ge(z_sp.sem, z_sp.at(l, h + 1))
                        diagonal(sbp[:, h % 2, :]).then_inc(z_spm.sem, z_spm.up())
                    if q in SB_R:
                        h = SB_R[q]
                        g.wait_ge(w_exp.sem, w_exp.at(l, h + 1))
                        diagonal(sbw[:, h % 3, :]).then_inc(w_ready.sem, w_ready.up())
                    if q in S5_X:
                        s5_turn(S5_X[q])
                    if q in NSA_S:
                        n = NSA_S[q]
                        w = nsa_unit(n)[3]
                        g.wait_ge(s_rec.sem, s_rec.at(l, n + 1))
                        pv = cols(pr[:, n % 2, :], w)
                        TT(pv, pv, rg[:, n % 2, :].rearrange("p (b o) -> p b o", o=1)
                           .broadcast_to([P, 2, w]), ALU.mult).then_inc(s_prob.sem, s_prob.up())
                    if q - 1 in S5_X:
                        s5_back(S5_X[q - 1])
                    if q % 2 and FILL[f][0] == "y" and FILL[f][1] == 2:
                        add_merged(FILL[f][2], U_FILL + f)
                for q in range(4):
                    add_merged(4 + q, U_Y + q)

                norm_lo(l, KD)

                def product(cc, turn=0, times=1):
                    n = U_FFN + 2 * cc + 1
                    g.wait_ge(sg_ready.sem, sg_ready.at(l, cc + 1) + turn * 2)
                    g.wait_ge(unit_out[n % 2].sem, unit_out[n % 2].at(l, n // 2 + 1) + turn * 2)
                    g.wait_ge(a_split.sem, a_split.at(l, cc - 1) + turn * 2)
                    TT(aT[:, cc % 2, :], cv[:, 0, :], cv[:, 1, :], ALU.mult).then_inc(a_ready.sem, 1)
                    a_ready.made += times

                product(0)
                product(1)
                with g.Fori(0, LOOP) as j:
                    product(2, j, LOOP)
                    product(3, j, LOOP)
                product(STEPS - 1)

        off = [(t.name, t.made, t.per_layer) for t in tallies if t.made != t.per_layer]
        assert not off, off


def kernel(**inputs):
    import numpy as np
    import concourse.bacc as bacc
    from concourse.bass_utils import run_bass_kernel_spmd

    names = ["x", "norm_mix", "w_in", "ssm_lam_re", "ssm_lam_im", "ssm_log_step", "ssm_b_re", "ssm_b_im",
             "ssm_c_re", "ssm_c_im", "ssm_d", "ssm_w_glu", "cmp_w1_k", "cmp_w2_k", "cmp_pos_k",
             "cmp_w1_v", "cmp_w2_v", "cmp_pos_v", "w_branch", "w_out", "norm_ffn", "ffn_w_up",
             "ffn_conv_w", "ffn_conv_b", "ffn_w_down", "norm_final"]
    nc = bacc.Bacc("TRN2", target_bir_lowering=False, num_devices=1)
    arrays, args = {}, []
    for name in names + ["consts"]:
        a = constants() if name == "consts" else np.ascontiguousarray(inputs[name])
        arrays[f"in_{name}"] = a
        args.append(nc.dram_tensor(f"in_{name}", a.shape, mybir.dt.from_np(a.dtype), kind="ExternalInput").ap())
    args.append(nc.dram_tensor("out", (1, T, D), F32, kind="ExternalOutput").ap())
    build(nc, *args)
    r = run_bass_kernel_spmd(nc, [arrays], core_ids=[0])
    return r.results[0]["out"]
```
